# Optimizing a Trainium2 kernel written in Bass

```python
import jax, jax.numpy as jnp
from jax import lax
import numpy as np

D_MODEL = 1024
BATCH = 1
SEQ = 512
DEPTH = 1

D_CONV = D_MODEL
CONV_A_WIDTH = 31
D_RNN = 1536
N_RNN_HEADS = 16
RNN_HEAD_DIM = D_RNN // N_RNN_HEADS
CONV_B_WIDTH = 4
LRU_C = 8.0
D_FF = 4 * D_MODEL
EPS = 1e-6

SPLITS = (D_CONV, D_CONV, D_RNN, D_RNN, D_MODEL, D_MODEL)
D_IN = sum(SPLITS)


def rms_norm(x, g):
    xf = x.astype(jnp.float32)
    y = xf * lax.rsqrt(jnp.mean(xf * xf, axis=-1, keepdims=True) + EPS)
    return (y * g.astype(jnp.float32)).astype(x.dtype)

def layer_norm(x, g, b):
    xf = x.astype(jnp.float32)
    mu = jnp.mean(xf, axis=-1, keepdims=True)
    xc = xf - mu
    y = xc * lax.rsqrt(jnp.mean(xc * xc, axis=-1, keepdims=True) + EPS)
    return (y * g.astype(jnp.float32) + b.astype(jnp.float32)).astype(x.dtype)

def causal_depthwise_conv(u, w, b):
    k = w.shape[0]
    y = lax.conv_general_dilated(
        u, w[:, None, :].astype(u.dtype), window_strides=(1,), padding=[(k - 1, 0)],
        dimension_numbers=("NWC", "WIO", "NWC"), feature_group_count=u.shape[-1])
    return y + b

def block_diag_linear(x, w, b):
    bsz, s, c = x.shape
    xh = x.reshape(bsz, s, N_RNN_HEADS, RNN_HEAD_DIM)
    y = jnp.einsum("bshi,hij->bshj", xh, w).reshape(bsz, s, c)
    return y + b

def rg_lru(x, w_a, b_a, w_x, b_x, lam):
    s = x.shape[1]
    r = jax.nn.sigmoid(block_diag_linear(x, w_a, b_a).astype(jnp.float32))
    i = jax.nn.sigmoid(block_diag_linear(x, w_x, b_x).astype(jnp.float32))
    log_a = -LRU_C * r * jax.nn.softplus(-lam.astype(jnp.float32))
    a = jnp.exp(log_a)
    mult = jnp.sqrt(-jnp.expm1(2.0 * log_a))
    is_start = (jnp.arange(s) == 0)[None, :, None]
    mult = jnp.where(is_start, 1.0, mult)
    bterm = mult * i * x.astype(jnp.float32)

    def combine(left, right):
        a_l, b_l = left
        a_r, b_r = right
        return a_r * a_l, a_r * b_l + b_r

    _, h = lax.associative_scan(combine, (a, bterm), axis=1)
    return h.astype(x.dtype)

def first_inputs(seed: int = 0) -> dict:
    key = jax.random.key(seed)
    ks = jax.random.split(key, 32)
    f32 = jnp.float32
    L = DEPTH

    def nrm(k, shape, scale):
        return jax.random.normal(k, shape, f32) * scale

    x = jax.random.normal(ks[0], (BATCH, SEQ, D_MODEL), f32)
    g_mix = 1.0 + nrm(ks[1], (L, D_MODEL), 0.02)
    w_in = nrm(ks[2], (L, D_MODEL, D_IN), D_MODEL ** -0.5)
    b_in = nrm(ks[3], (L, D_IN), 0.02)
    conv_a_w = nrm(ks[4], (L, CONV_A_WIDTH, D_CONV), CONV_A_WIDTH ** -0.5)
    conv_a_b = nrm(ks[5], (L, D_CONV), 0.02)
    ln_g = 1.0 + nrm(ks[6], (L, D_CONV), 0.02)
    ln_b = nrm(ks[7], (L, D_CONV), 0.02)
    w_a_out = nrm(ks[8], (L, D_CONV, D_MODEL), D_CONV ** -0.5)
    conv_b_w = nrm(ks[9], (L, CONV_B_WIDTH, D_RNN), CONV_B_WIDTH ** -0.5)
    conv_b_b = nrm(ks[10], (L, D_RNN), 0.02)
    w_rg_a = nrm(ks[11], (L, N_RNN_HEADS, RNN_HEAD_DIM, RNN_HEAD_DIM), RNN_HEAD_DIM ** -0.5)
    b_rg_a = nrm(ks[12], (L, D_RNN), 0.02)
    w_rg_x = nrm(ks[13], (L, N_RNN_HEADS, RNN_HEAD_DIM, RNN_HEAD_DIM), RNN_HEAD_DIM ** -0.5)
    b_rg_x = nrm(ks[14], (L, D_RNN), 0.02)
    a0 = jax.random.uniform(ks[15], (L, D_RNN), f32, 0.9, 0.999)
    s0 = a0 ** (1.0 / LRU_C)
    lam = jnp.log(s0) - jnp.log1p(-s0)
    w_b_out = nrm(ks[16], (L, D_RNN, D_MODEL), D_RNN ** -0.5)
    w_o = nrm(ks[17], (L, D_MODEL, D_MODEL), D_MODEL ** -0.5)
    g_mlp = 1.0 + nrm(ks[18], (L, D_MODEL), 0.02)
    w_1 = nrm(ks[19], (L, D_MODEL, D_FF), D_MODEL ** -0.5)
    w_2 = nrm(ks[20], (L, D_FF, D_MODEL), D_FF ** -0.5)
    g_final = 1.0 + nrm(ks[21], (D_MODEL,), 0.02)
    return {"x": x, "g_mix": g_mix, "w_in": w_in, "b_in": b_in,
            "conv_a_w": conv_a_w, "conv_a_b": conv_a_b, "ln_g": ln_g, "ln_b": ln_b,
            "w_a_out": w_a_out, "conv_b_w": conv_b_w, "conv_b_b": conv_b_b,
            "w_rg_a": w_rg_a, "b_rg_a": b_rg_a, "w_rg_x": w_rg_x, "b_rg_x": b_rg_x,
            "lam": lam, "w_b_out": w_b_out, "w_o": w_o, "g_mlp": g_mlp,
            "w_1": w_1, "w_2": w_2, "g_final": g_final}

def first_block(x, g_mix, w_in, b_in, conv_a_w, conv_a_b, ln_g, ln_b, w_a_out,
              conv_b_w, conv_b_b, w_rg_a, b_rg_a, w_rg_x, b_rg_x, lam, w_b_out,
              w_o, g_mlp, w_1, w_2, g_final):
    cuts = np.cumsum(SPLITS)[:-1].tolist()
    for l in range(DEPTH):
        h = rms_norm(x, g_mix[l])
        z = jnp.einsum("bsd,de->bse", h, w_in[l]) + b_in[l]
        va, ga, xb, gb, sa, sb = jnp.split(z, cuts, axis=-1)

        u = va * jax.nn.sigmoid(ga)
        u = causal_depthwise_conv(u, conv_a_w[l], conv_a_b[l])
        u = jax.nn.silu(layer_norm(u, ln_g[l], ln_b[l]))
        y_a = jnp.einsum("bsc,cd->bsd", u, w_a_out[l])

        v = causal_depthwise_conv(xb, conv_b_w[l], conv_b_b[l])
        v = rg_lru(v, w_rg_a[l], b_rg_a[l], w_rg_x[l], b_rg_x[l], lam[l])
        y_b = jnp.einsum("bsc,cd->bsd", v * jax.nn.gelu(gb), w_b_out[l])

        m = jax.nn.sigmoid(sa) * y_a + jax.nn.sigmoid(sb) * y_b
        x = x + jnp.einsum("bsd,de->bse", m, w_o[l])

        h = rms_norm(x, g_mlp[l])
        f = jnp.square(jax.nn.relu(jnp.einsum("bsd,df->bsf", h, w_1[l])))
        x = x + jnp.einsum("bsf,fd->bsd", f, w_2[l])
    return rms_norm(x, g_final)


DEPTH_2 = 2

N_A_LAYERS = DEPTH_2 // 2
N_B_LAYERS = DEPTH_2 - N_A_LAYERS
HGRN_EXPAND = 128
HGRN_HEADS = D_MODEL // HGRN_EXPAND
HGRN_DK = HGRN_EXPAND
HGRN_DV = D_MODEL // HGRN_HEADS
HGRN_CHUNK = 64
MLA_HEADS = 16
MLA_NOPE = 128
MLA_ROPE = 64
MLA_V = 128
MLA_Q_LORA = 256
MLA_KV_LORA = 256
ROPE_THETA = 10000.0
QBLOCK = 128
D_FF_2 = 4 * D_MODEL


def rmsnorm(x, gain):
    xf = x.astype(jnp.float32)
    y = xf * lax.rsqrt(jnp.mean(xf * xf, axis=-1, keepdims=True) + EPS)
    return (y * gain.astype(jnp.float32)).astype(x.dtype)

def rope_tables(seq):
    half = MLA_ROPE // 2
    inv_freq = ROPE_THETA ** (-jnp.arange(half, dtype=jnp.float32) / half)
    ang = jnp.arange(seq, dtype=jnp.float32)[:, None] * inv_freq[None, :]
    return jnp.cos(ang), jnp.sin(ang)

def apply_rope(x, cos, sin):
    half = MLA_ROPE // 2
    xf = x.astype(jnp.float32)
    x1, x2 = xf[..., :half], xf[..., half:]
    return jnp.concatenate([x1 * cos - x2 * sin, x2 * cos + x1 * sin], axis=-1).astype(x.dtype)

def hgrn_lower_bounds(lb_logits):
    return jnp.cumsum(jax.nn.softmax(lb_logits.astype(jnp.float32), axis=0), axis=0)

def hgrn2_mixer(xn, w_q, w_f, w_i, w_g, g_norm, w_o, lb):
    bsz, seq, _ = xn.shape
    nc = seq // HGRN_CHUNK
    f32 = jnp.float32
    q = jax.nn.silu((xn @ w_q).astype(f32))
    forget = lb + (1.0 - lb) * jax.nn.sigmoid((xn @ w_f).astype(f32))
    log_f = jnp.log(forget)
    k = 1.0 - forget
    v = (xn @ w_i).astype(f32)

    def chunks(t, d):
        return t.reshape(bsz, nc, HGRN_CHUNK, HGRN_HEADS, d).transpose(1, 0, 3, 2, 4)

    causal = jnp.tril(jnp.ones((HGRN_CHUNK, HGRN_CHUNK), dtype=bool))

    def step(state, inp):
        qc, kc, vc, gc = inp
        b = jnp.cumsum(gc, axis=2)
        o_inter = jnp.einsum('bhtd,bhdv->bhtv', qc * jnp.exp(b), state)
        diff = b[:, :, :, None, :] - b[:, :, None, :, :]
        decay = jnp.exp(jnp.where(causal[:, :, None], diff, -jnp.inf))
        scores = jnp.einsum('bhtd,bhsd,bhtsd->bhts', qc, kc, decay)
        o_intra = jnp.einsum('bhts,bhsv->bhtv', scores, vc)
        b_last = b[:, :, -1:, :]
        new_state = jnp.exp(b_last[:, :, 0, :])[..., None] * state + jnp.einsum(
            'bhsd,bhsv->bhdv', kc * jnp.exp(b_last - b), vc)
        return new_state, o_inter + o_intra

    state0 = jnp.zeros((bsz, HGRN_HEADS, HGRN_DK, HGRN_DV), f32)
    _, o = lax.scan(step, state0, (chunks(q, HGRN_DK), chunks(k, HGRN_DK),
                                   chunks(v, HGRN_DV), chunks(log_f, HGRN_DK)))
    o = o.transpose(1, 0, 3, 2, 4).reshape(bsz, seq, HGRN_HEADS, HGRN_DV)
    o = rmsnorm(o, g_norm)
    gate = jax.nn.silu((xn @ w_g).astype(f32)).reshape(bsz, seq, HGRN_HEADS, HGRN_DV)
    o = (o * gate).reshape(bsz, seq, D_MODEL).astype(xn.dtype)
    return o @ w_o

def shared_mla_kv(h, in_norm, w_dkv, kv_norm, w_uk, w_uv, cos, sin):
    bsz, seq, _ = h.shape
    hn = rmsnorm(h, in_norm)
    ckr = hn @ w_dkv
    c_kv = rmsnorm(ckr[..., :MLA_KV_LORA], kv_norm)
    k_rope = apply_rope(ckr[..., MLA_KV_LORA:], cos, sin)
    k_nope = (c_kv @ w_uk).reshape(bsz, seq, MLA_HEADS, MLA_NOPE)
    v = (c_kv @ w_uv).reshape(bsz, seq, MLA_HEADS, MLA_V)
    return k_nope, k_rope, v

def mla_mixer(xn, w_dq, q_norm, w_uq, w_o, k_nope, k_rope, v, cos, sin):
    bsz, seq, _ = xn.shape
    nb = seq // QBLOCK
    c_q = rmsnorm(xn @ w_dq, q_norm)
    q = (c_q @ w_uq).reshape(bsz, seq, MLA_HEADS, MLA_NOPE + MLA_ROPE)
    q_nope = q[..., :MLA_NOPE]
    q_rope = apply_rope(q[..., MLA_NOPE:], cos[:, None, :], sin[:, None, :])
    qn_b = q_nope.reshape(bsz, nb, QBLOCK, MLA_HEADS, MLA_NOPE).transpose(1, 0, 2, 3, 4)
    qr_b = q_rope.reshape(bsz, nb, QBLOCK, MLA_HEADS, MLA_ROPE).transpose(1, 0, 2, 3, 4)
    starts = jnp.arange(nb, dtype=jnp.int32) * QBLOCK
    key_pos = jnp.arange(seq, dtype=jnp.int32)
    scale = (MLA_NOPE + MLA_ROPE) ** -0.5

    def block(args):
        qn, qr, start = args
        s = jnp.einsum('bqhd,bkhd->bhqk', qn, k_nope) + jnp.einsum('bqhr,bkr->bhqk', qr, k_rope)
        s = s.astype(jnp.float32) * scale
        q_pos = start + jnp.arange(QBLOCK, dtype=jnp.int32)
        s = jnp.where(key_pos[None, :] <= q_pos[:, None], s, -jnp.inf)
        p = jax.nn.softmax(s, axis=-1).astype(v.dtype)
        return jnp.einsum('bhqk,bkhv->bqhv', p, v)

    o = lax.map(block, (qn_b, qr_b, starts))
    o = o.transpose(1, 0, 2, 3, 4).reshape(bsz, seq, MLA_HEADS * MLA_V)
    return o @ w_o

def sq_relu_mlp(xn, w_up, w_down):
    return jnp.square(jax.nn.relu(xn @ w_up)) @ w_down

def second_inputs(seed: int = 0) -> dict:
    key = jax.random.key(seed)
    ks = jax.random.split(key, 24)
    f32 = jnp.float32

    def w(k, shape, fan_in):
        return jax.random.normal(k, shape, f32) * (fan_in ** -0.5)

    def gain(k, shape):
        return 1.0 + 0.02 * jax.random.normal(k, shape, f32)

    D = D_MODEL
    return {
        'x': jax.random.normal(ks[0], (BATCH, SEQ, D), f32),
        'hgrn_norm': gain(ks[1], (N_A_LAYERS, D)),
        'hgrn_w_q': w(ks[2], (N_A_LAYERS, D, D), D),
        'hgrn_w_f': w(ks[3], (N_A_LAYERS, D, D), D),
        'hgrn_w_i': w(ks[4], (N_A_LAYERS, D, D), D),
        'hgrn_w_g': w(ks[5], (N_A_LAYERS, D, D), D),
        'hgrn_g_norm': gain(ks[6], (N_A_LAYERS, HGRN_DV)),
        'hgrn_w_o': w(ks[7], (N_A_LAYERS, D, D), D),
        'hgrn_lb_logits': 0.5 * jax.random.normal(ks[8], (N_A_LAYERS + 1, D), f32),
        'mla_norm': gain(ks[9], (N_B_LAYERS, D)),
        'mla_w_dq': w(ks[10], (N_B_LAYERS, D, MLA_Q_LORA), D),
        'mla_q_norm': gain(ks[11], (N_B_LAYERS, MLA_Q_LORA)),
        'mla_w_uq': w(ks[12], (N_B_LAYERS, MLA_Q_LORA, MLA_HEADS * (MLA_NOPE + MLA_ROPE)), MLA_Q_LORA),
        'mla_w_o': w(ks[13], (N_B_LAYERS, MLA_HEADS * MLA_V, D), MLA_HEADS * MLA_V),
        'kv_in_norm': gain(ks[14], (D,)),
        'kv_w_dkv': w(ks[15], (D, MLA_KV_LORA + MLA_ROPE), D),
        'kv_norm': gain(ks[16], (MLA_KV_LORA,)),
        'kv_w_uk': w(ks[17], (MLA_KV_LORA, MLA_HEADS * MLA_NOPE), MLA_KV_LORA),
        'kv_w_uv': w(ks[18], (MLA_KV_LORA, MLA_HEADS * MLA_V), MLA_KV_LORA),
        'mlp_norm': gain(ks[19], (DEPTH_2, D)),
        'mlp_w_up': w(ks[20], (DEPTH_2, D, D_FF_2), D),
        'mlp_w_down': w(ks[21], (DEPTH_2, D_FF_2, D), D_FF_2),
        'final_norm': gain(ks[22], (D,)),
    }

def second_block(x, hgrn_norm, hgrn_w_q, hgrn_w_f, hgrn_w_i, hgrn_w_g, hgrn_g_norm, hgrn_w_o,
              hgrn_lb_logits, mla_norm, mla_w_dq, mla_q_norm, mla_w_uq, mla_w_o,
              kv_in_norm, kv_w_dkv, kv_norm, kv_w_uk, kv_w_uv,
              mlp_norm, mlp_w_up, mlp_w_down, final_norm):
    seq = x.shape[1]
    cos, sin = rope_tables(seq)
    lower_bounds = hgrn_lower_bounds(hgrn_lb_logits)
    h = x
    k_nope = k_rope = v = None
    for l in range(DEPTH_2):
        if l < N_A_LAYERS:
            h = h + hgrn2_mixer(rmsnorm(h, hgrn_norm[l]), hgrn_w_q[l], hgrn_w_f[l], hgrn_w_i[l],
                                hgrn_w_g[l], hgrn_g_norm[l], hgrn_w_o[l], lower_bounds[l])
        else:
            j = l - N_A_LAYERS
            h = h + mla_mixer(rmsnorm(h, mla_norm[j]), mla_w_dq[j], mla_q_norm[j], mla_w_uq[j],
                              mla_w_o[j], k_nope, k_rope, v, cos, sin)
        h = h + sq_relu_mlp(rmsnorm(h, mlp_norm[l]), mlp_w_up[l], mlp_w_down[l])
        if l == N_A_LAYERS - 1:
            k_nope, k_rope, v = shared_mla_kv(h, kv_in_norm, kv_w_dkv, kv_norm, kv_w_uk, kv_w_uv, cos, sin)
    return rmsnorm(h, final_norm)


def setup_inputs(seed=0):
    out = dict(first_inputs(seed))
    for name, value in second_inputs(seed + 1).items():
        if name != "x":
            out[name + "_2"] = value
    return out


def reference(
    x, g_mix, w_in, b_in, conv_a_w, conv_a_b, ln_g, ln_b, w_a_out, conv_b_w, conv_b_b, w_rg_a,
    b_rg_a, w_rg_x, b_rg_x, lam, w_b_out, w_o, g_mlp, w_1, w_2, g_final, hgrn_norm_2,
    hgrn_w_q_2, hgrn_w_f_2, hgrn_w_i_2, hgrn_w_g_2, hgrn_g_norm_2, hgrn_w_o_2, hgrn_lb_logits_2,
    mla_norm_2, mla_w_dq_2, mla_q_norm_2, mla_w_uq_2, mla_w_o_2, kv_in_norm_2, kv_w_dkv_2,
    kv_norm_2, kv_w_uk_2, kv_w_uv_2, mlp_norm_2, mlp_w_up_2, mlp_w_down_2, final_norm_2,
):
    x = first_block(
        x, g_mix, w_in, b_in, conv_a_w, conv_a_b, ln_g, ln_b, w_a_out, conv_b_w, conv_b_b,
        w_rg_a, b_rg_a, w_rg_x, b_rg_x, lam, w_b_out, w_o, g_mlp, w_1, w_2, g_final,
    )
    return second_block(
        x, hgrn_norm_2, hgrn_w_q_2, hgrn_w_f_2, hgrn_w_i_2, hgrn_w_g_2, hgrn_g_norm_2,
        hgrn_w_o_2, hgrn_lb_logits_2, mla_norm_2, mla_w_dq_2, mla_q_norm_2, mla_w_uq_2,
        mla_w_o_2, kv_in_norm_2, kv_w_dkv_2, kv_norm_2, kv_w_uk_2, kv_w_uv_2, mlp_norm_2,
        mlp_w_up_2, mlp_w_down_2, final_norm_2,
    )


_drawn_inputs = setup_inputs


def setup_inputs(seed=0):
    import zlib

    import numpy as np

    out = dict(_drawn_inputs(seed))
    spreads = {}
    factors = {'g_mix': 4.281,
     'conv_a_b': 2.858,
     'ln_g': 5.279,
     'ln_b': 6.024,
     'b_rg_a': 8.0,
     'b_rg_x': 8.0,
     'g_mlp': 2.754,
     'hgrn_norm_2': 3.411,
     'hgrn_g_norm_2': 4.615,
     'mla_norm_2': 8.0,
     'mla_q_norm_2': 8.0,
     'kv_in_norm_2': 8.0,
     'kv_norm_2': 8.0,
     'final_norm_2': 8.806,
     'mlp_norm_2': 3.877}
    for name, (base, spread) in spreads.items():
        noise = np.random.default_rng([zlib.crc32(name.encode()), seed]).standard_normal(out[name].shape)
        drawn = base * np.exp(spread * noise) if base else spread * noise
        out[name] = __import__('jax').numpy.asarray(drawn.astype(out[name].dtype))
    for name, factor in factors.items():
        out[name] = (out[name] * factor).astype(out[name].dtype)
    return out
```

```python
from contextlib import ExitStack

import numpy as np

import concourse.bass as bass
from concourse import mybir

P = 128
T = 512
TB = T // P
D = 1024
KD = D // P
D_RNN = 1536
RT = D_RNN // P
TAPS_A = 31
TAPS_B = 4
HEADS_H = 8
HEADS_M = 16
NOPE, ROPE = 128, 64
LORA = 256
D_FF = 4096
Q_FF = D_FF // 4
SCALE = float(NOPE + ROPE) ** -0.5
LEVELS = (64, 32, 16, 8, 4, 2, 1)
EPS = 1e-6

F32 = mybir.dt.float32
F32R = mybir.dt.float32r
U8 = mybir.dt.uint8
ALU = mybir.AluOpType
ACT = mybir.ActivationFunctionType
AX = mybir.AxisListType.X

VECTOR_WIDTHS = [
    ("g_mix", 8), ("b_in", 56), ("conv_a_b", 8), ("ln_g", 8), ("ln_b", 8), ("conv_b_b", 12),
    ("b_rg_a", 12), ("b_rg_x", 12), ("lam", 12), ("g_mlp", 8), ("g_final", 8), ("hgrn_norm_2", 8),
    ("hgrn_g_norm_2", 1), ("hgrn_lb_logits_2", 16), ("mla_norm_2", 8), ("mla_q_norm_2", 2),
    ("kv_in_norm_2", 8), ("kv_norm_2", 2), ("mlp_norm_2", 16), ("final_norm_2", 8),
    ("conv_b_w", 48), ("conv_a_w", 248), ("eps", 1),
]
COLUMN = {}
_at = 0
for _name, _n in VECTOR_WIDTHS:
    COLUMN[_name] = _at
    _at += _n
N_COLUMNS = _at

CHUNKS = [("ug", 8), ("xb", 6), ("band", 4), ("saya", 8), ("sb", 4), ("gb", 6), ("bo", 8), ("wo", 4),
          ("mlp0", 32), ("hg", 16), ("hwo", 4), ("mlp1", 32), ("kvq", 4), ("att", 8), ("mwo", 8),
          ("mlp2", 32)]
FIRST = {}
_at = 0
for _name, _n in CHUNKS:
    FIRST[_name] = _at
    _at += _n
N_CHUNKS = _at

BAND = [(0, 0), (1, 0), (0, 1), (1, 1), (2, 1), (1, 2), (2, 2)]


def build_program(nc, a, out):
    ctx = ExitStack()
    with ctx:
        top = [nc.sbuf_base + (-nc.sbuf_base) % 32]

        def place(name, shape, dt, at=None):
            size = int(np.prod(shape[1:])) * (1 if dt == U8 else 4)
            where = top[0] if at is None else at
            if at is None:
                top[0] += size + (-size) % 32
            return nc.alloc_sbuf_tensor_at(name, list(shape), dt, offset=where), where

        def sem(name):
            return ctx.enter_context(nc.semaphore(name))

        raw, _ = place("raw", [P, 2, 2048], F32)
        w_hi, _ = place("w_hi", [P, 2, 2048], F32R)
        w_lo, _ = place("w_lo", [P, 2, 2048], F32R)
        vec, _ = place("vec", [P, N_COLUMNS], F32)
        ident, _ = place("ident", [P, P], F32)
        ones, _ = place("ones", [P, P], F32)
        small, _ = place("small", [P, 128], F32)
        tmp, a_tmp = place("tmp", [P, 4, T], F32)
        rst, a_rst = place("rst", [P, 2, T], F32)
        X, _ = place("X", [P, KD, T], F32)
        XH, a_xh = place("XH", [P, KD, T], F32R)
        XL, _ = place("XL", [P, KD, T], F32R)
        S = top[0]
        TILE = T * 4

        x_tm, _ = place("x_tm", [P, TB, D], F32, S)
        CO, _ = place("CO", [P, KD, T], F32, S)
        UH, _ = place("UH", [P, KD, T], F32R, S)
        SBG, _ = place("SBG", [P, KD, T], F32, S)
        at_u = S + KD * TILE
        PAD_A, PAD_B = TAPS_A - 1, 32
        U, _ = place("U", [P, KD, PAD_A + T], F32, at_u)
        UL, _ = place("UL", [P, KD, T], F32R, at_u)
        VA, _ = place("VA", [P, 4, T], F32, at_u + KD * (PAD_A + T) * 4)
        M, _ = place("M", [P, KD, T], F32, at_u + KD * TILE)
        at_g = at_u + 2 * KD * TILE
        XBR, _ = place("XBR", [P, RT, 4 + T], F32, at_g)
        VGH, _ = place("VGH", [P, RT, T], F32R, at_g)
        VH, _ = place("VH", [P, 3, T], F32R, at_g)
        VL, _ = place("VL", [P, 3, T], F32R, at_g + 3 * TILE)
        LR, _ = place("LR", [P, 6, T], F32, at_g + 6 * TILE)
        at_v = at_g + RT * (4 + T) * 4
        V, _ = place("V", [P, RT, T], F32, at_v)
        VGL, _ = place("VGL", [P, RT, T], F32R, at_v)
        at_end = at_v + RT * TILE
        MH, _ = place("MH", [P, KD, T], F32R, S)
        ML, _ = place("ML", [P, KD, T], F32R, at_u)
        FH, _ = place("FH", [P, KD, T], F32R, S)
        FL, _ = place("FL", [P, KD, T], F32R, S + KD * TILE)
        base = S
        OH, _ = place("OH", [P, KD, T], F32R, base)
        OL, _ = place("OL", [P, KD, T], F32R, base + 8 * TILE)
        HQ, _ = place("HQ", [P, 2, T], F32, base + 16 * TILE)
        HK, _ = place("HK", [P, 2, T], F32, base + 18 * TILE)
        HF, _ = place("HF", [P, 2, T], F32, base + 20 * TILE)
        HGATE, _ = place("HGATE", [P, 2, T], F32, base + 22 * TILE)
        HV, _ = place("HV", [P, TB, 256], F32, base + 24 * TILE)
        HE, _ = place("HE", [P, 8, T], F32, base + 26 * TILE)
        HP, _ = place("HP", [P, T], F32, base + 34 * TILE)
        HQD, _ = place("HQD", [P, T], F32, base + 35 * TILE)
        HKD, _ = place("HKD", [P, T], F32, base + 36 * TILE)
        HEB, _ = place("HEB", [P, T], F32, base + 37 * TILE)
        HKT, _ = place("HKT", [P, 3, P], F32, base + 38 * TILE)
        HS, _ = place("HS", [P, 3, P], F32, base + 39 * TILE)
        HSG, _ = place("HSG", [P, 4, T], F32, base + 40 * TILE)
        masks, _ = place("masks", [P, 8, P], U8, base + 44 * TILE)
        reset, _ = place("reset", [P, T], F32, base + 45 * TILE)
        AH, _ = place("AH", [P, HEADS_M, T], F32R, a_xh)
        AL, _ = place("AL", [P, HEADS_M, T], F32R, S)
        base = S + 16 * TILE
        KN, _ = place("KN", [P, 4, T], F32, base)
        QN, _ = place("QN", [P, 4, T], F32, base + 4 * TILE)
        VT, _ = place("VT", [P, TB, 512], F32, base + 8 * TILE)
        PM, _ = place("PM", [P, TB, T], F32, base + 12 * TILE)
        PT, _ = place("PT", [P, TB, T], F32, base + 16 * TILE)
        QR, _ = place("QR", [P, 4, T], F32, base + 20 * TILE)
        KR, _ = place("KR", [P, T], F32, base + 24 * TILE)
        cos_t, _ = place("cos_t", [P, T], F32, base + 25 * TILE)
        sin_t, _ = place("sin_t", [P, T], F32, base + 26 * TILE)
        swap_t, _ = place("swap_t", [P, P], F32, base + 27 * TILE)
        neg_t, _ = place("neg_t", [P, P], F32, base + 27 * TILE + 512)
        CKH, _ = place("CKH", [P, 2, T], F32R, base + 28 * TILE)
        CKL, _ = place("CKL", [P, 2, T], F32R, base + 30 * TILE)
        CQH, _ = place("CQH", [P, 2, T], F32R, a_tmp)
        CQL, _ = place("CQL", [P, 2, T], F32R, a_tmp + 2 * TILE)
        CK, _ = place("CK", [P, 4, T], F32, S + 8 * TILE)
        y_tm, _ = place("y_tm", [P, TB, D], F32, S)
        assert max(at_end, S + 46 * TILE, base + 32 * TILE) <= nc.sbuf_usable_end, (
            max(at_end, S + 46 * TILE, base + 32 * TILE) - nc.sbuf_usable_end)

        ps = ctx.enter_context(nc.psum_tensor("ps", [P, 8, T], F32))

        raw_in = [sem("raw_in_0"), sem("raw_in_1")]
        hi_done = sem("hi_done")
        lo_done = sem("lo_done")
        halves = sem("halves")
        band_in = sem("band_in")
        band_zero = sem("band_zero")
        parts_in = sem("parts_in")
        consts_in = sem("consts_in")
        x_in = sem("x_in")
        hconst_in = sem("hconst_in")
        mconst_in = sem("mconst_in")
        out_done = sem("out_done")

        S_ = {}

        def s_(name):
            if name not in S_:
                S_[name] = sem(name)
            return S_[name]

        kinds = {
            "norm": ["n_mix", "n_mlp0", "n_fin0", "n_hg", "n_mlp1", "n_kv", "n_mla", "n_mlp2", "n_fin1"],
            "small": ["ckv", "cq"],
            "mlp": ["mlp0", "mlp1", "mlp2"],
            "sum": ["wo", "hwo", "mwo"],
        }
        kind_of = {n: kind for kind, stages in kinds.items() for n in stages}

        def signals(n, what):
            if kind_of[n] == "norm":
                if what in ("hi", "lo"):
                    return 0 if n in ("n_fin0", "n_fin1") else KD
                if n == "n_mla" and what != "t":
                    return 0
                return 1 if what in ("std", "inv") else KD
            if kind_of[n] == "small":
                return 1 if what in ("mean", "std", "inv") else 2
            return {"mlp": {"r": 4 + 32, "t": 32, "fh": 32, "fl": 4 + 32, "dn": 4 + 32}, "sum": {"x": 4 + KD}}[kind_of[n]][what]

        def sig(n, what):
            return s_(kind_of[n] + "_" + what)

        def at(n, what, value):
            stages = kinds[kind_of[n]]
            return sig(n, what), value + sum(signals(m, what) for m in stages[:stages.index(n)])

        def half_at(c, j=1):
            return 2 * c + (5 + j)

        def col(name, k=0, n=1):
            return vec[:, COLUMN[name] + k:COLUMN[name] + k + n]

        def dcol(name, k):
            return vec[:, bass.ds(k + COLUMN[name], 1)]

        def w8(t, s, n):
            v = t[:, s].rearrange("p (k n) -> p k n", k=8)
            return [v[:, k, n * P:(n + 1) * P] for k in range(8)]

        def w1(t, s, kt):
            v = t[:, s, 0:kt * P].rearrange("p (k n) -> p k n", k=kt)
            return [v[:, k] for k in range(kt)]

        class Count:

            def __init__(self, eng, name):
                self.eng, self.sem, self.at = eng, s_(name), 0

            def put(self, instruction):
                instruction.then_inc(self.sem, 1)
                self.at = self.at + 1
                return self.at

            def wait(self, value=None):
                self.eng.wait_ge(self.sem, self.at if value is None else value)

        def norm_act(act, n, ready, split=True, squares=True):
            if squares:
                for k in range(KD):
                    act.wait_ge(*ready(k))
                    if k >= 2:
                        act.wait_ge(*at(n, "mean", k - 1))
                    act.activation(tmp[:, k % 2], X[:, k], ACT.Square).then_inc(sig(n, "sq"), 1)
                act.wait_ge(*at(n, "mean", KD))
                act.activation(rst[:, 0], ps[:, 7], ACT.Sqrt, bias=col("eps"), scale=1.0 / D)\
                    .then_inc(sig(n, "std"), 1)
            if split:
                for k in range(KD):
                    act.wait_ge(*at(n, "t", k + 1))
                    act.activation(XH[:, k], tmp[:, 2 + k % 2], ACT.Copy).then_inc(sig(n, "hi"), 1)

        def norm_pe(pe, n):
            for k in range(KD):
                pe.wait_ge(*at(n, "sq", k + 1))
                pe.matmul(ps[:, 7], ones[:], tmp[:, k % 2], start=k == 0, stop=k == KD - 1)\
                    .then_inc(sig(n, "mean"), 1)

        def norm_dve(dve, n, gain, off=0, split=True, invert=True):
            if invert:
                dve.wait_ge(*at(n, "std", 1))
                dve.reciprocal(rst[:, 1], rst[:, 0]).then_inc(sig(n, "inv"), 1)
                dve.wait_ge(*at(n, "inv", 1))
            for k in range(KD + 1):
                if k < KD:
                    if split and k >= 2:
                        dve.wait_ge(*at(n, "lo", k - 1))
                    dve.scalar_tensor_tensor(tmp[:, 2 + k % 2] if split else X[:, k], X[:, k],
                                             col(gain, off + k), rst[:, 1], ALU.mult, ALU.mult)\
                        .then_inc(sig(n, "t"), 1)
                if split and k >= 1:
                    dve.wait_ge(*at(n, "hi", k))
                    dve.tensor_tensor(XL[:, k - 1], tmp[:, 2 + (k - 1) % 2], XH[:, k - 1].bitcast(F32),
                                      ALU.subtract).then_inc(sig(n, "lo"), 1)

        block = ctx.enter_context(nc.Block())

        @block.sync
        def _(sp):
            sp.dma_start(x_tm[:], a["x"].rearrange("b (t p) d -> p (b t) d", p=P)).then_inc(x_in, 16)
            sp.dma_start(vec[:], a["vectors"]).then_inc(consts_in, 16)
            sp.dma_start(ident[:], a["ident"]).then_inc(consts_in, 16)
            sp.dma_start(ones[:], a["ones"]).then_inc(consts_in, 16)

            def slot_free(c):
                sp.wait_ge(lo_done, c + 1)

            def load8(c, s, w, col0, row0=0, waited=False):
                if not waited:
                    slot_free(c)
                v = raw[:, s].rearrange("p (k n) -> p k n", k=8)
                for h in range(2):
                    sp.dma_start(v[:, 4 * h:4 * h + 4],
                                 w[bass.ds(row0 + 512 * h, 512), bass.ds(col0, 256)]
                                 .rearrange("(k p) n -> p k n", p=P)).then_inc(raw_in[s], 16)

            def load1(c, s, w, col0, kt):
                slot_free(c)
                v = raw[:, s, 0:kt * P].rearrange("p (k n) -> p k n", k=kt)
                for h in range(2):
                    sp.dma_start(v[:, h * kt // 2:(h + 1) * kt // 2],
                                 w[h * kt * P // 2:(h + 1) * kt * P // 2, bass.ds(col0, P)]
                                 .rearrange("(k p) n -> p k n", p=P)).then_inc(raw_in[s], 16)

            w_in = a["w_in"]
            c = FIRST["ug"]
            with sp.Fori(0, 4) as i:
                load8(2 * i + c, 0, w_in, i * 256)
                load8(2 * i + c + 1, 1, w_in, i * 256 + D)
            c = FIRST["xb"]
            with sp.Fori(0, 3) as i:
                for s in range(2):
                    load8(2 * i + c + s, s, w_in, i * 512 + 256 * s + 2 * D)
            c = FIRST["band"]
            with sp.Fori(0, 2) as i:
                for s in range(2):
                    slot_free(2 * i + c + s)
                    sp.wait_ge(band_zero, s + 1)
                    n = 0
                    for gate, w in enumerate((a["w_rg_a"], a["w_rg_x"])):
                        for j in range(4):
                            r = 96 * j
                            while r < 96 * j + 96:
                                r1 = min(96 * j + 96, (r // P + 1) * P)
                                q = 96 * j
                                while q < 96 * j + 96:
                                    q1 = min(96 * j + 96, (q // P + 1) * P)
                                    b = 7 * gate + BAND.index((r // P, q // P))
                                    sp.dma_start(
                                        raw[r % P:r % P + r1 - r, s, b * P + q % P:b * P + q % P + q1 - q],
                                        w[bass.ds(i * 8 + 4 * s + j, 1), r - 96 * j:r1 - 96 * j,
                                          q - 96 * j:q1 - 96 * j].rearrange("h r q -> (h r) q"))\
                                        .then_inc(band_in, 16)
                                    n += 16
                                    q = q1
                                r = r1
                    sp.wait_ge(band_in, i * (2 * n) + n * (s + 1))
                    sp.sem_inc(raw_in[s], 32)
            c = FIRST["saya"]
            with sp.Fori(0, 4) as i:
                load8(2 * i + c, 0, w_in, i * 256 + 2 * D + 2 * D_RNN)
                slot_free(2 * i + c + 1)
                sp.sem_inc(s_("w_a_slot"), 1)
                load8(2 * i + c + 1, 1, a["w_a_out"], i * 256, waited=True)
            c = FIRST["sb"]
            with sp.Fori(0, 2) as i:
                for s in range(2):
                    load8(2 * i + c + s, s, w_in, i * 512 + 256 * s + 3 * D + 2 * D_RNN)
            c = FIRST["gb"]
            with sp.Fori(0, 3) as i:
                for s in range(2):
                    load8(2 * i + c + s, s, w_in, i * 512 + 256 * s + 2 * D + D_RNN)
            c = FIRST["bo"]
            with sp.Fori(0, 4) as i:
                for s in range(2):
                    load1(2 * i + c + s, s, a["w_b_out"], i * 256 + P * s, RT)
            c = FIRST["wo"]
            with sp.Fori(0, 2) as i:
                for s in range(2):
                    load8(2 * i + c + s, s, a["w_o"], i * 512 + 256 * s)

            def load_mlp(c, up, down):
                with sp.Fori(0, 4) as q:
                    with sp.Fori(0, 2) as i:
                        for s in range(2):
                            load8(8 * q + 2 * i + c + s, s, up, q * Q_FF + i * 512 + 256 * s)
                    with sp.Fori(0, 2) as i:
                        for s in range(2):
                            load8(8 * q + 2 * i + c + 4 + s, s, down, i * 512 + 256 * s, q * Q_FF)

            load_mlp(FIRST["mlp0"], a["w_1"], a["w_2"])
            sp.wait_ge(*at("mlp0", "dn", 4 + 32))
            sp.dma_start(HE[:, 0:2], a["level_masks"]).then_inc(hconst_in, 16)
            sp.dma_start(reset[:], a["reset"]).then_inc(hconst_in, 16)
            c = FIRST["hg"]
            with sp.Fori(0, 4) as i:
                for n, w in enumerate(("hgrn_w_q_2", "hgrn_w_f_2", "hgrn_w_g_2", "hgrn_w_i_2")):
                    load8(4 * i + c + n, n % 2, a[w], i * 256)
            c = FIRST["hwo"]
            with sp.Fori(0, 2) as i:
                for s in range(2):
                    load8(2 * i + c + s, s, a["hgrn_w_o_2"], i * 512 + 256 * s)
            load_mlp(FIRST["mlp1"], a["mlp_w_up_2"][0], a["mlp_w_down_2"][0])
            sp.wait_ge(*at("mlp1", "dn", 4 + 32))
            sp.dma_start(cos_t[:], a["cos"]).then_inc(mconst_in, 16)
            sp.dma_start(sin_t[:], a["sin"]).then_inc(mconst_in, 16)
            sp.dma_start(swap_t[:], a["swap"]).then_inc(mconst_in, 16)
            sp.dma_start(neg_t[:], a["neg"]).then_inc(mconst_in, 16)
            c = FIRST["kvq"]
            load8(c, 0, a["kv_w_dkv_2"], 0)
            slot_free(c + 1)
            v = raw[:, 1, 0:8 * P].rearrange("p (k n) -> p k n", k=8)
            for h in range(2):
                sp.dma_start(v[:, :, h * ROPE:(h + 1) * ROPE],
                             a["kv_w_dkv_2"][:, LORA:LORA + ROPE].rearrange("(k p) n -> p k n", p=P))\
                    .then_inc(raw_in[1], 16)
            load1(c + 2, 0, a["mla_w_dq_2"], 0, 8)
            load1(c + 3, 1, a["mla_w_dq_2"], P, 8)
            c = FIRST["att"]
            with sp.Fori(0, 4) as i:
                slot_free(2 * i + c)
                for h, w in enumerate(("kv_w_uk_2", "kv_w_uv_2")):
                    sp.dma_start(raw[:, 0, h * 1024:(h + 1) * 1024].rearrange("p (k n) -> p k n", k=2),
                                 a[w][:, bass.ds(i * 512, 512)].rearrange("(k p) n -> p k n", p=P))\
                        .then_inc(raw_in[0], 16)
                slot_free(2 * i + c + 1)
                src = a["mla_w_uq_2"].rearrange("(k p) (h n) -> k p h n", p=P, n=NOPE + ROPE)
                for k in range(2):
                    sp.dma_start(raw[:, 1, k * 512:(k + 1) * 512].rearrange("p (h n) -> p h n", h=4),
                                 src[k][:, bass.ds(i * 4, 4), 0:NOPE]).then_inc(parts_in, 16)
                    sp.dma_start(raw[:, 1, 1024 + k * 256:1280 + k * 256].rearrange("p (h n) -> p h n", h=4),
                                 src[k][:, bass.ds(i * 4, 4), NOPE:NOPE + ROPE]).then_inc(parts_in, 16)
                sp.wait_ge(parts_in, i * 64 + 64)
                sp.sem_inc(raw_in[1], 32)
            c = FIRST["mwo"]
            with sp.Fori(0, 4) as i:
                for s in range(2):
                    load1(2 * i + c + s, s, a["mla_w_o_2"], i * 256 + P * s, 16)
            load_mlp(FIRST["mlp2"], a["mlp_w_up_2"][1], a["mlp_w_down_2"][1])
            for s in range(2):
                load8(N_CHUNKS + s, s, a["mlp_w_down_2"][1], 512 + 256 * s, 3 * Q_FF)
            sp.wait_ge(s_("y_out"), TB * 2)
            sp.dma_start(out.rearrange("b (t p) d -> p (b t) d", p=P), y_tm[:]).then_inc(out_done, 16)
            sp.wait_ge(out_done, 16)

        @block.gpsimd
        def _(pool):
            pool.sem_inc(lo_done, 2)

            def split_lo(c, s):
                pool.wait_ge(hi_done, c + 1)
                pool.tensor_tensor(w_lo[:, s], raw[:, s], w_hi[:, s].bitcast(F32), ALU.subtract)\
                    .then_inc(lo_done, 1)

            with pool.Fori(0, FIRST["band"] // 2) as i:
                for s in range(2):
                    split_lo(2 * i + s, s)
            pool.wait_ge(lo_done, 2 + FIRST["band"])
            for s in range(2):
                pool.memset(raw[:, s], 0.0).then_inc(band_zero, 1)
            with pool.Fori(FIRST["band"] // 2, N_CHUNKS // 2) as i:
                for s in range(2):
                    split_lo(2 * i + s, s)

        @block.scalar
        def _(act):
            def split_hi(c, s):
                act.wait_ge(raw_in[s], 16 * (c - s) + 32)
                act.wait_ge(halves, 2 * c + 2)
                act.activation(w_hi[:, s], raw[:, s], ACT.Copy).then_inc(hi_done, 1)

            split_hi(0, 0)
            split_hi(1, 1)
            act.wait_ge(consts_in, 48)

            for k in range(KD):
                act.wait_ge(s_("x_turned"), k + 1)
                act.activation(X[:, k], ps[:, k % 4], ACT.Copy).then_inc(s_("x_fm"), 1)
            norm_act(act, "n_mix", lambda k: (s_("x_fm"), k + 1))

            ev = s_("ug_evac")
            act.sem_inc(ev, 4)
            c = FIRST["ug"]
            with act.Fori(0, 4) as i:
                for j in range(4):
                    act.wait_ge(halves, half_at(2 * i + c + j // 2, j % 2))
                    act.wait_ge(s_("u_done"), 2 * i + j % 2 + 1)
                    if j < 2:
                        act.activation(VA[:, j], ps[:, j], ACT.Identity, bias=dcol("b_in", 2 * i + j))\
                            .then_inc(ev, 1)
                    else:
                        act.activation(VA[:, j], ps[:, j], ACT.Sigmoid, bias=dcol("b_in", 2 * i + KD + j - 2))\
                            .then_inc(ev, 1)
                    if j % 2:
                        split_hi(2 * i + c + j // 2 + 2, j // 2)

            ev = s_("xb_evac")
            act.wait_ge(s_("ug_evac"), 4 + 16)
            act.sem_inc(ev, 4)
            c = FIRST["xb"]
            with act.Fori(0, 3) as i:
                for j in range(4):
                    act.wait_ge(halves, half_at(2 * i + c + j // 2, j % 2))
                    act.activation(XBR[:, bass.ds(4 * i + j, 1), 4:4 + T], ps[:, j:j + 1], ACT.Identity,
                                   bias=dcol("b_in", 4 * i + 2 * KD + j)).then_inc(ev, 1)
                    if j % 2:
                        split_hi(2 * i + c + j // 2 + 2, j // 2)

            act.wait_ge(s_("lam_abs"), 2)
            act.activation(small[:, 24:36], small[:, 12:24], ACT.Exp, scale=-1.0).then_inc(s_("lam_e"), 1)

            g_r, g_x, g_t, g_s = s_("lru_r"), s_("lru_x"), s_("lru_t"), s_("lru_s")
            c = FIRST["band"]
            act.wait_ge(s_("ch_done"), 1)
            act.wait_ge(s_("v_done"), RT)
            with act.Fori(0, 2) as i:
                for s in range(2):
                    for j in range(3):
                        act.wait_ge(halves, half_at(2 * i + c + s - 1))
                        act.activation(VH[:, j], V[:, bass.ds(6 * i + 3 * s + j, 1)], ACT.Copy)\
                            .then_inc(s_("vh_done"), 1)
                    for j in range(3):
                        t = 6 * i + 3 * s + j
                        act.wait_ge(halves, half_at(2 * i + c + s, 1))
                        act.wait_ge(s_("lru_done"), t + 1)
                        act.activation(LR[:, 0], ps[:, j], ACT.Sigmoid, bias=dcol("b_rg_a", t)).then_inc(g_r, 1)
                        act.activation(LR[:, 1], ps[:, 3 + j], ACT.Sigmoid, bias=dcol("b_rg_x", t)).then_inc(g_x, 1)
                        act.wait_ge(g_r, t + 1)
                        act.activation(LR[:, 2], LR[:, 0], ACT.Tanh, scale=small[:, bass.ds(t + 60, 1)]).then_inc(g_t, 1)
                        act.wait_ge(g_t, t + 1)
                        act.activation(LR[:, 3], LR[:, 2], ACT.Sqrt, scale=-4.0).then_inc(g_s, 1)
                    split_hi(2 * i + c + s + 2, s)

            act.wait_ge(s_("mu_mm"), KD)
            act.activation(rst[:, 0], ps[:, 7], ACT.Copy, scale=1.0 / D).then_inc(s_("mu_done"), 1)
            for k in range(KD):
                act.wait_ge(s_("xc_done"), k + 1)
                if k >= 2:
                    act.wait_ge(s_("var_mm"), k - 1)
                act.activation(tmp[:, k % 2], CO[:, k], ACT.Square).then_inc(s_("xc_sq"), 1)
            act.wait_ge(s_("var_mm"), KD)
            act.activation(rst[:, 0], ps[:, 7], ACT.Sqrt, bias=col("eps"), scale=1.0 / D).then_inc(s_("ln_std"), 1)
            for k in range(KD):
                act.wait_ge(s_("ln_y"), k + 1)
                act.activation(tmp[:, 2 + k % 2], tmp[:, k % 2], ACT.Sigmoid, bias=col("ln_b", k))\
                    .then_inc(s_("ln_sg"), 1)
                act.wait_ge(s_("ln_u"), k + 1)
                act.activation(UH[:, k], tmp[:, 2 + k % 2], ACT.Copy).then_inc(s_("uh_done"), 1)

            c = FIRST["saya"]
            with act.Fori(0, 4) as i:
                for j in range(2):
                    act.wait_ge(halves, half_at(2 * i + c, j))
                    act.wait_ge(s_("ya_done"), 2 * i + j + 1)
                    act.activation(tmp[:, j], ps[:, j], ACT.Sigmoid, bias=dcol("b_in", 2 * i + 40 + j))\
                        .then_inc(s_("sa_done"), 1)
                split_hi(2 * i + c + 2, 0)
                split_hi(2 * i + c + 3, 1)

            ev = s_("sb_evac")
            act.wait_ge(s_("ya_done"), 2 + KD)
            act.sem_inc(ev, 4)
            c = FIRST["sb"]
            with act.Fori(0, 2) as i:
                for j in range(4):
                    act.wait_ge(halves, half_at(2 * i + c + j // 2, j % 2))
                    act.activation(SBG[:, bass.ds(4 * i + j, 1)], ps[:, j:j + 1], ACT.Sigmoid,
                                   bias=dcol("b_in", 4 * i + 48 + j)).then_inc(ev, 1)
                    if j % 2:
                        split_hi(2 * i + c + j // 2 + 2, j // 2)

            ev = s_("gb_evac")
            act.wait_ge(s_("sb_evac"), 4 + KD)
            act.sem_inc(ev, 4)
            c = FIRST["gb"]
            z_, zz, th = s_("gb_z"), s_("gb_zz"), s_("gb_th")
            with act.Fori(0, 3) as i:
                for j in range(4):
                    t = 4 * i + j
                    act.wait_ge(halves, half_at(2 * i + c + j // 2, j % 2))
                    act.wait_ge(s_("vg_lo"), t + 1)
                    act.activation(tmp[:, j % 2], ps[:, j], ACT.Identity, bias=dcol("b_in", 4 * i + 28 + j)).then_inc(z_, 1)
                    act.activation(tmp[:, 2 + j % 2], ps[:, j], ACT.Square, bias=dcol("b_in", 4 * i + 28 + j)).then_inc(ev, 1)
                    act.wait_ge(s_("gb_p"), t + 1)
                    act.activation(tmp[:, 2 + j % 2], tmp[:, 2 + j % 2], ACT.Tanh, scale=0.7978845608028654).then_inc(th, 1)
                    act.wait_ge(s_("vg_t"), t + 1)
                    act.activation(VGH[:, bass.ds(t, 1)], tmp[:, j % 2:j % 2 + 1], ACT.Copy).then_inc(s_("vg_hi"), 1)
                    if j % 2:
                        split_hi(2 * i + c + j // 2 + 2, j // 2)

            c = FIRST["bo"]
            with act.Fori(0, 2) as i:
                for j in range(4):
                    act.wait_ge(s_("m_done"), 4 * i + j + 5)
                    act.activation(MH[:, bass.ds(4 * i + j, 1)], M[:, bass.ds(4 * i + j, 1)], ACT.Copy)\
                        .then_inc(s_("mh_done"), 1)
                    split_hi(4 * i + c + j + 2, j % 2)

            def ahead(c, n):
                with act.Fori(0, n) as i:
                    for s in range(2):
                        split_hi(2 * i + c + s + 2, s)

            ahead(FIRST["wo"], 2)

            def mlp_act(n):
                c = FIRST[n]
                act.sem_inc(sig(n, "r"), 4)
                with act.Fori(0, 4) as q:
                    with act.Fori(0, 2) as i:
                        for j in range(4):
                            act.wait_ge(halves, half_at(8 * q + 2 * i + c + j // 2, j % 2))
                            act.wait_ge(*at(n, "fl", 8 * q + 4 * i + j + 1))
                            act.activation(tmp[:, j], ps[:, j], ACT.Relu).then_inc(sig(n, "r"), 1)
                            act.wait_ge(*at(n, "t", 8 * q + 4 * i + j + 1))
                            act.activation(FH[:, bass.ds(4 * i + j, 1)], tmp[:, j:j + 1], ACT.Copy)\
                                .then_inc(sig(n, "fh"), 1)
                            if j % 2:
                                split_hi(8 * q + 2 * i + c + j // 2 + 2, j // 2)
                    with act.Fori(0, 2) as i:
                        for s in range(2):
                            split_hi(8 * q + 2 * i + c + 6 + s, s)

            norm_act(act, "n_mlp0", lambda k: at("wo", "x", k + 5))
            mlp_act("mlp0")
            norm_act(act, "n_fin0", lambda k: at("mlp0", "dn", 28 + k + 1), split=False)
            norm_act(act, "n_hg", lambda k: at("n_fin0", "t", k + 1))

            act.wait_ge(s_("lb_in"), 1)
            act.activation(small[:, 88:96], small[:, 80:88], ACT.Sigmoid).then_inc(s_("lb_done"), 1)
            c = FIRST["hg"]
            act.sem_inc(s_("hv_done"), 2)
            with act.Fori(0, 4) as i:
                for n in range(2):
                    act.wait_ge(halves, half_at(4 * i + c, n))
                    act.wait_ge(s_("hq_done"), 2 * i + n + 1)
                    act.activation(HSG[:, n], ps[:, n], ACT.Sigmoid).then_inc(s_("hq_sg"), 1)
                split_hi(4 * i + c + 2, 0)
                for n in range(2):
                    act.wait_ge(halves, half_at(4 * i + c + 1, n))
                    act.wait_ge(s_("ho_done"), 2 * i + n + 1)
                    act.activation(HF[:, n], ps[:, 2 + n], ACT.Sigmoid).then_inc(s_("hf_sg"), 1)
                split_hi(4 * i + c + 3, 1)
                for n in range(2):
                    act.wait_ge(halves, half_at(4 * i + c + 2, n))
                    act.wait_ge(s_("hg_done"), 2 * i + n + 1)
                    act.activation(HSG[:, 2 + n], ps[:, n], ACT.Sigmoid).then_inc(s_("hg_sg"), 1)
                split_hi(4 * i + c + 4, 0)
                for n in range(2):
                    act.wait_ge(halves, half_at(4 * i + c + 3, n))
                    act.activation(HV[:, 2 * n:2 * n + 2], ps[:, 2 + n].rearrange("p (b v) -> p b v", b=2),
                                   ACT.Copy).then_inc(s_("hv_done"), 1)
                split_hi(4 * i + c + 5, 1)
                for n in range(2):
                    h = 2 * i + n
                    act.wait_ge(s_("hf_done"), h + 1)
                    act.activation(HF[:, n], HF[:, n], ACT.Ln).then_inc(s_("h_ln"), 1)
                    act.wait_ge(s_("h_scan"), h + 1)
                    act.activation(HEB[:], HF[:, n], ACT.Exp).then_inc(s_("h_eb"), 1)
                    act.wait_ge(s_("h_kd_arg"), h + 1)
                    act.activation(HKD[:], HKD[:], ACT.Exp).then_inc(s_("h_kd_e"), 1)
                    for l in range(len(LEVELS)):
                        act.wait_ge(s_("h_arg"), 14 * h + 2 * l + 2)
                        act.activation(HE[:, l], HE[:, l], ACT.Exp).then_inc(s_("h_e"), 1)
                    act.wait_ge(s_("h_kt"), 3 * h + 3)
                    act.activation(HKT[:], ps[:, 7, 0:384].rearrange("p (b d) -> p b d", b=3), ACT.Copy)\
                        .then_inc(s_("h_kt_c"), 1)
                    act.wait_ge(s_("h_o"), h + 1)
                    act.activation(tmp[:, 0], ps[:, 6], ACT.Square).then_inc(s_("h_sq"), 1)
                    act.wait_ge(s_("h_mean"), h + 1)
                    act.activation(rst[:, 0], ps[:, 7], ACT.Sqrt, bias=col("eps"), scale=1.0 / P).then_inc(s_("h_std"), 1)
                    act.wait_ge(s_("h_t2"), h + 1)
                    act.activation(OH[:, bass.ds(h, 1)], tmp[:, 1:2], ACT.Copy).then_inc(s_("oh_done"), 1)

            ahead(FIRST["hwo"], 2)
            norm_act(act, "n_mlp1", lambda k: at("hwo", "x", k + 5))
            mlp_act("mlp1")
            norm_act(act, "n_kv", lambda k: at("mlp1", "dn", 28 + k + 1))

            c = FIRST["kvq"]

            def small_norm_act(n, ready):
                for k in range(2):
                    act.wait_ge(halves, ready[k])
                    act.activation(CK[:, k], ps[:, k], ACT.Copy).then_inc(sig(n, "c"), 1)
                for k in range(2):
                    act.activation(tmp[:, k], ps[:, k], ACT.Square).then_inc(sig(n, "sq"), 1)
                act.wait_ge(*at(n, "mean", 1))
                act.activation(rst[:, 0], ps[:, 7], ACT.Sqrt, bias=col("eps"), scale=1.0 / LORA)\
                    .then_inc(sig(n, "std"), 1)

            small_norm_act("ckv", [half_at(c, 0), half_at(c, 1)])
            split_hi(c + 2, 0)
            for k in range(2):
                act.wait_ge(*at("ckv", "t", k + 1))
                act.activation(CKH[:, k], CK[:, 2 + k], ACT.Copy).then_inc(sig("ckv", "hi"), 1)
            act.wait_ge(halves, half_at(c + 1))
            act.activation(QR[:, 2], ps[:, 2], ACT.Copy).then_inc(s_("kr_raw"), 1)
            split_hi(c + 3, 1)
            norm_act(act, "n_mla", None, squares=False)
            split_hi(c + 4, 0)
            small_norm_act("cq", [half_at(c + 2), half_at(c + 3)])
            split_hi(c + 5, 1)
            for k in range(2):
                act.wait_ge(*at("cq", "t", k + 1))
                act.activation(CQH[:, k], CK[:, 2 + k], ACT.Copy).then_inc(sig("cq", "hi"), 1)

            c = FIRST["att"]
            act.sem_inc(s_("a_exp"), 4)
            act.sem_inc(s_("a_ptc"), 2)
            with act.Fori(0, 4) as i:
                for h in range(4):
                    act.wait_ge(halves, half_at(2 * i + c, 0))
                    act.activation(KN[:, h], ps[:, h], ACT.Copy).then_inc(s_("kn_done"), 1)
                for b in range(TB):
                    act.wait_ge(halves, half_at(2 * i + c, 1))
                    act.activation(VT[:, b], ps[:, 4 + b], ACT.Copy).then_inc(s_("vt_done"), 1)
                split_hi(2 * i + c + 2, 0)
                for h in range(4):
                    act.wait_ge(halves, half_at(2 * i + c + 1, 0))
                    act.activation(QN[:, h], ps[:, h], ACT.Copy).then_inc(s_("qn_done"), 1)
                for h in range(2):
                    act.wait_ge(halves, half_at(2 * i + c + 1, 1))
                    act.activation(QR[:, 2 + h], ps[:, 4 + h], ACT.Copy).then_inc(s_("qr_raw"), 1)
                split_hi(2 * i + c + 3, 1)

                def exps(h):
                    for b in range(TB):
                        act.wait_ge(s_("a_nmax"), 16 * i + 4 * h + b + 1)
                        act.wait_ge(s_("a_pt"), 16 * i + 4 * h + b + 1)
                        act.activation(PM[:, b, 0:(b + 1) * P], ps[:, b, 0:(b + 1) * P], ACT.Exp,
                                       bias=small[:, 100 + b:101 + b], scale=SCALE,
                                       accum_out=small[:, 104 + b:105 + b]).then_inc(s_("a_exp"), 1)

                def turned(h):
                    for b in range(TB):
                        act.wait_ge(s_("a_pt"), 16 * i + 4 * h + b + 5)
                        act.wait_ge(s_("a_pv"), 4 * i + h + 1)
                        act.activation(PT[:, 0:b + 1, b * P:(b + 1) * P],
                                       ps[:, 4 + b % 2, 0:(b + 1) * P].rearrange("p (j q) -> p j q", q=P),
                                       ACT.Copy).then_inc(s_("a_ptc"), 1)

                def out_hi(h):
                    act.wait_ge(s_("a_pv"), 4 * i + h + 2)
                    act.activation(AH[:, bass.ds(4 * i + h, 1)], ps[:, 6:7], ACT.Copy).then_inc(s_("ah_done"), 1)

                for h in range(4):
                    exps(h)
                    turned(h)
                    out_hi(h)

            ahead(FIRST["mwo"], 4)
            norm_act(act, "n_mlp2", lambda k: at("mwo", "x", k + 5))
            mlp_act("mlp2")
            norm_act(act, "n_fin1", lambda k: at("mlp2", "dn", 28 + k + 1), split=False)
            for g in range(TB * 2):
                act.wait_ge(s_("y_turned"), g + 1)
                act.activation(y_tm[:, g // 2, (g % 2) * 512:(g % 2) * 512 + 512], ps[:, g % 4], ACT.Copy)\
                    .then_inc(s_("y_out"), 1)

        @block.vector
        def _(dve):
            dve.memset(U[:, :, 0:PAD_A], 0.0).then_inc(s_("pads"), 1)
            dve.memset(XBR[:, :, 0:4], 0.0).then_inc(s_("pads"), 1)
            dve.sem_inc(s_("u_done"), 2)
            dve.wait_ge(consts_in, 48)
            lam = Count(dve, "lam_abs")
            nl, ab, e, sm = small[:, 0:12], small[:, 12:24], small[:, 24:36], small[:, 36:48]
            zz, rr, ch = small[:, 48:60], small[:, 72:84], small[:, 60:72]
            lam.put(dve.tensor_scalar(nl, col("lam", 0, 12), -1.0, None, ALU.mult))
            lam.wait()
            lam.put(dve.tensor_tensor(ab, nl, col("lam", 0, 12), ALU.max))
            norm_dve(dve, "n_mix", "g_mix")

            def conv_a(i, base):
                cs = s_("conv")
                for t in range(TAPS_A):
                    acc = CO[:, bass.ds(i, 1)] if t % 2 == 0 else tmp[:, 0:1]
                    src = U[:, bass.ds(i, 1), t:t + T]
                    w = dcol("conv_a_w", i * 31 + t)
                    if t >= 2:
                        dve.wait_ge(cs, base + t - 1)
                    if t == 0:
                        dve.tensor_scalar(acc, src, w, dcol("conv_a_b", i), ALU.mult, ALU.add).then_inc(cs, 1)
                    elif t == 1:
                        dve.tensor_scalar(acc, src, w, None, ALU.mult).then_inc(cs, 1)
                    else:
                        dve.scalar_tensor_tensor(acc, src, w, acc, ALU.mult, ALU.add).then_inc(cs, 1)
                dve.wait_ge(cs, base + TAPS_A)
                dve.tensor_tensor(CO[:, bass.ds(i, 1)], CO[:, bass.ds(i, 1)], tmp[:, 0:1], ALU.add).then_inc(cs, 1)
                dve.wait_ge(cs, base + TAPS_A + 1)

            dve.wait_ge(s_("pads"), 2)
            dve.wait_ge(*at("n_mix", "lo", KD))
            with dve.Fori(0, 4) as i:
                for n in range(2):
                    dve.wait_ge(s_("ug_evac"), 4 * i + 7 + n)
                    dve.tensor_tensor(U[:, bass.ds(2 * i + n, 1), PAD_A:PAD_A + T], VA[:, n:n + 1], VA[:, 2 + n:3 + n],
                                      ALU.mult).then_inc(s_("u_done"), 1)
                dve.wait_ge(s_("u_done"), 2 * i + 4)
                conv_a(i, i * 32)
            with dve.Fori(0, 3) as i:
                for k in range(TAPS_B):
                    for j in range(4):
                        t = 4 * i + j
                        src = XBR[:, bass.ds(t, 1), 1 + k:1 + k + T]
                        w = dcol("conv_b_w", t * 4 + k)
                        acc = V[:, bass.ds(t, 1)]
                        part = s_("v_part")
                        if k == 0:
                            dve.wait_ge(s_("xb_evac"), t + 5)
                            dve.tensor_scalar(acc, src, w, dcol("conv_b_b", t), ALU.mult, ALU.add).then_inc(part, 1)
                        else:
                            dve.wait_ge(part, 12 * i + 4 * (k - 1) + j + 1)
                            dve.scalar_tensor_tensor(acc, src, w, acc, ALU.mult, ALU.add)\
                                .then_inc(part if k < TAPS_B - 1 else s_("v_done"), 1)
                conv_a(i + 4, i * 32 + 4 * 32)

            lc = Count(dve, "lam_chain")
            dve.wait_ge(s_("lam_e"), 1)
            lc.put(dve.tensor_scalar(sm, e, 2.0, None, ALU.add))
            lc.wait()
            lc.put(dve.reciprocal(rr, sm))
            lc.wait()
            lc.put(dve.tensor_tensor(zz, e, rr, ALU.mult))
            lc.wait()
            lc.put(dve.tensor_tensor(sm, zz, zz, ALU.mult))
            lc.wait()
            lc.put(dve.tensor_scalar(rr, sm, 1.0 / 17, None, ALU.mult))
            for n in range(15, 1, -2):
                lc.wait()
                lc.put(dve.scalar_tensor_tensor(rr, rr, 1.0 / n, sm, ALU.add, ALU.mult))
            lc.wait()
            lc.put(dve.scalar_tensor_tensor(rr, rr, 1.0, zz, ALU.add, ALU.mult))
            lc.put(dve.tensor_scalar(nl, nl, 0.0, -4.0, ALU.max, ALU.mult))
            lc.wait()
            dve.scalar_tensor_tensor(ch, rr, -8.0, nl, ALU.mult, ALU.add).then_inc(s_("ch_done"), 1)

            dve.sem_inc(s_("lru_done"), 1)
            conv_a(7, 7 * 32)
            a0 = s_("lru_a")
            with dve.Fori(0, 2) as i:
                for s in range(2):
                    for j in range(3):
                        t = 6 * i + 3 * s + j
                        dve.wait_ge(s_("vh_done"), t + 1)
                        dve.tensor_tensor(VL[:, j:j + 1], V[:, bass.ds(t, 1)], VH[:, j:j + 1].bitcast(F32), ALU.subtract)\
                            .then_inc(s_("vl_done"), 1)
                    for j in range(3):
                        t = 6 * i + 3 * s + j
                        n = 42 * i + 21 * s + 7 * j
                        r, x_, th, sq, inv = LR[:, 0], LR[:, 1], LR[:, 2], LR[:, 3], LR[:, 4]
                        dve.wait_ge(s_("lru_x"), t + 1)
                        dve.wait_ge(s_("vl_done"), 6 * i + 3 * s + 3)
                        dve.tensor_tensor(x_[:, None, :], x_[:, None, :], V[:, bass.ds(t, 1)], ALU.mult).then_inc(a0, 1)
                        dve.wait_ge(s_("lru_t"), t + 1)
                        dve.tensor_scalar(inv, th, -1.0, 1.0, ALU.mult, ALU.add).then_inc(a0, 1)
                        dve.wait_ge(a0, n + 2)
                        dve.reciprocal(inv, inv).then_inc(a0, 1)
                        dve.wait_ge(s_("lru_s"), t + 1)
                        dve.wait_ge(a0, n + 3)
                        dve.scalar_tensor_tensor(r, th, 1.0, inv, ALU.add, ALU.mult).then_inc(a0, 1)
                        dve.tensor_tensor(sq, sq, inv, ALU.mult).then_inc(a0, 1)
                        dve.wait_ge(a0, n + 5)
                        dve.memset(sq[:, 0:1], 1.0).then_inc(a0, 1)
                        dve.wait_ge(a0, n + 6)
                        dve.tensor_tensor(x_, x_, sq, ALU.mult).then_inc(a0, 1)
                        dve.wait_ge(a0, n + 7)
                        dve.tensor_tensor_scan(V[:, bass.ds(t, 1)].rearrange("p a t -> p (a t)"), r, x_, 0.0,
                                               ALU.mult, ALU.add).then_inc(s_("lru_done"), 1)

            dve.wait_ge(s_("lru_done"), 1 + RT)
            for k in range(KD):
                dve.wait_ge(s_("mu_done"), 1)
                dve.tensor_tensor(CO[:, k], CO[:, k], rst[:, 0], ALU.subtract).then_inc(s_("xc_done"), 1)
            dve.wait_ge(s_("ln_std"), 1)
            dve.reciprocal(rst[:, 1], rst[:, 0]).then_inc(s_("ln_inv"), 1)
            dve.wait_ge(s_("ln_inv"), 1)
            dve.wait_ge(s_("xc_done"), KD)
            for k in range(KD + 1):
                if k < KD:
                    if k >= 2:
                        dve.wait_ge(s_("ln_u"), k - 1)
                    dve.scalar_tensor_tensor(tmp[:, k % 2], CO[:, k], col("ln_g", k), rst[:, 1], ALU.mult, ALU.mult)\
                        .then_inc(s_("ln_y"), 1)
                if k >= 1:
                    dve.wait_ge(s_("uh_done"), k)
                    dve.tensor_tensor(UL[:, k - 1], tmp[:, 2 + (k - 1) % 2], UH[:, k - 1].bitcast(F32), ALU.subtract)\
                        .then_inc(s_("ul_done"), 1)
                if k < KD:
                    dve.wait_ge(s_("ln_sg"), k + 1)
                    dve.scalar_tensor_tensor(tmp[:, 2 + k % 2], tmp[:, k % 2], col("ln_b", k), tmp[:, 2 + k % 2],
                                             ALU.add, ALU.mult).then_inc(s_("ln_u"), 1)

            dve.wait_ge(s_("ul_done"), KD)
            dve.sem_inc(s_("ya_done"), 2)
            c = FIRST["saya"]
            with dve.Fori(0, 4) as i:
                for j in range(2):
                    dve.wait_ge(halves, half_at(2 * i + c + 1, j))
                    dve.wait_ge(s_("sa_done"), 2 * i + j + 1)
                    dve.tensor_tensor(M[:, bass.ds(2 * i + j, 1)], ps[:, 2 + j:3 + j], tmp[:, j:j + 1], ALU.mult)\
                        .then_inc(s_("ya_done"), 1)

            dve.wait_ge(s_("ya_done"), 2 + KD)
            dve.sem_inc(s_("vg_lo"), 2)
            with dve.Fori(0, 3) as i:
                for j in range(4):
                    t = 4 * i + j
                    z, w = tmp[:, j % 2], tmp[:, 2 + j % 2]
                    dve.wait_ge(s_("gb_evac"), t + 5)
                    dve.tensor_scalar(w, w, 0.044715, 1.0, ALU.mult, ALU.add).then_inc(s_("gb_q"), 1)
                    dve.wait_ge(s_("gb_q"), t + 1)
                    dve.tensor_tensor(w, w, z, ALU.mult).then_inc(s_("gb_p"), 1)
                    dve.wait_ge(s_("gb_th"), t + 1)
                    dve.scalar_tensor_tensor(w, w, 1.0, z, ALU.add, ALU.mult).then_inc(s_("gb_g"), 1)
                    dve.wait_ge(s_("gb_g"), t + 1)
                    dve.scalar_tensor_tensor(z[:, None, :], w[:, None, :], 0.5, V[:, bass.ds(t, 1)], ALU.mult, ALU.mult)\
                        .then_inc(s_("vg_t"), 1)
                    dve.wait_ge(s_("vg_hi"), t + 1)
                    dve.wait_ge(s_("vg_t"), t + 1)
                    dve.tensor_tensor(VGL[:, bass.ds(t, 1)], z[:, None, :], VGH[:, bass.ds(t, 1)].bitcast(F32), ALU.subtract)\
                        .then_inc(s_("vg_lo"), 1)

            dve.wait_ge(s_("vg_lo"), 2 + RT)
            dve.sem_inc(s_("m_done"), 4)
            dve.sem_inc(s_("yb_evac"), 4)
            c = FIRST["bo"]
            with dve.Fori(0, 2) as i:
                for j in range(4):
                    t = 4 * i + j
                    dve.wait_ge(halves, half_at(4 * i + c + j))
                    dve.wait_ge(s_("m_done"), t + 1)
                    dve.tensor_tensor(tmp[:, j:j + 1], ps[:, j:j + 1], SBG[:, bass.ds(t, 1)], ALU.mult).then_inc(s_("yb_evac"), 1)
                    dve.wait_ge(s_("yb_evac"), t + 5)
                    dve.tensor_tensor(M[:, bass.ds(t, 1)], M[:, bass.ds(t, 1)], tmp[:, j:j + 1], ALU.add).then_inc(s_("m_done"), 1)
                    dve.wait_ge(s_("mh_done"), t + 1)
                    dve.tensor_tensor(ML[:, bass.ds(t, 1)], M[:, bass.ds(t, 1)], MH[:, bass.ds(t, 1)].bitcast(F32), ALU.subtract)\
                        .then_inc(s_("ml_done"), 1)

            def residual(n, c, per, banks_free):
                xs = sig(n, "x")
                dve.wait_ge(*banks_free)
                dve.sem_inc(xs, 4)
                with dve.Fori(0, 2) as i:
                    for j in range(4):
                        dve.wait_ge(halves, half_at(2 * i + c + j // 2, j % 2) if per == 2 else half_at(4 * i + c + j))
                        dve.tensor_tensor(X[:, bass.ds(4 * i + j, 1)], X[:, bass.ds(4 * i + j, 1)], ps[:, j:j + 1], ALU.add)\
                            .then_inc(xs, 1)

            def mlp_dve(n):
                c = FIRST[n]
                dve.sem_inc(sig(n, "fl"), 4)
                dve.sem_inc(sig(n, "dn"), 4)
                with dve.Fori(0, 4) as q:
                    with dve.Fori(0, 2) as i:
                        for j in range(5):
                            f = 8 * q + 4 * i + j
                            if j < 4:
                                dve.wait_ge(*at(n, "r", f + 5))
                                dve.tensor_tensor(tmp[:, j], tmp[:, j], tmp[:, j], ALU.mult).then_inc(sig(n, "t"), 1)
                            if j >= 1:
                                dve.wait_ge(*at(n, "fh", f))
                                dve.tensor_tensor(FL[:, bass.ds(4 * i + j - 1, 1)], tmp[:, j - 1:j],
                                                  FH[:, bass.ds(4 * i + j - 1, 1)].bitcast(F32), ALU.subtract)\
                                    .then_inc(sig(n, "fl"), 1)
                    with dve.Fori(0, 2) as i:
                        for j in range(4):
                            dve.wait_ge(halves, half_at(8 * q + 2 * i + c + 4 + j // 2, j % 2))
                            dve.tensor_tensor(X[:, bass.ds(4 * i + j, 1)], X[:, bass.ds(4 * i + j, 1)], ps[:, j:j + 1],
                                              ALU.add).then_inc(sig(n, "dn"), 1)

            residual("wo", FIRST["wo"], 2, (s_("yb_evac"), 4 + KD))
            norm_dve(dve, "n_mlp0", "g_mlp")
            mlp_dve("mlp0")
            norm_dve(dve, "n_fin0", "g_final", split=False)
            norm_dve(dve, "n_hg", "hgrn_norm_2")

            dve.tensor_tensor(small[:, 80:88], col("hgrn_lb_logits_2", 0, 8), col("hgrn_lb_logits_2", 8, 8), ALU.subtract)\
                .then_inc(s_("lb_in"), 1)
            dve.wait_ge(s_("lb_done"), 1)
            dve.tensor_scalar(small[:, 112:120], small[:, 88:96], -1.0, 1.0, ALU.mult, ALU.add).then_inc(s_("lb_1m"), 1)
            dve.memset(HP[:], 0.0).then_inc(s_("h_p0"), 1)
            dve.wait_ge(s_("lb_1m"), 1)
            dve.wait_ge(s_("h_p0"), 1)
            dve.wait_ge(hconst_in, 32)
            dve.tensor_copy(masks[:].rearrange("p l t -> p (l t)"), HE[:, 0:2].rearrange("p l t -> p (l t)"))\
                .then_inc(s_("masks_done"), 1)
            dve.wait_ge(s_("masks_done"), 1)
            dve.sem_inc(s_("hq_done"), 2)
            dve.sem_inc(s_("hg_done"), 2)
            dve.sem_inc(s_("ho_done"), 2)
            dve.sem_inc(s_("h_g_free"), 2)
            c = FIRST["hg"]
            with dve.Fori(0, 4) as i:
                for n in range(2):
                    dve.wait_ge(s_("hq_sg"), 2 * i + n + 1)
                    dve.tensor_tensor(HQ[:, n], ps[:, n], HSG[:, n], ALU.mult).then_inc(s_("hq_done"), 1)
                hc = s_("h_f")
                for n in range(2):
                    h = 2 * i + n
                    dve.wait_ge(s_("hf_sg"), h + 1)
                    dve.tensor_scalar(HF[:, n], HF[:, n], small[:, bass.ds(h + 112, 1)], small[:, bass.ds(h + 88, 1)],
                                      ALU.mult, ALU.add).then_inc(hc, 1)
                    dve.wait_ge(hc, 2 * h + 1)
                    dve.tensor_scalar(HK[:, n], HF[:, n], -1.0, 1.0, ALU.mult, ALU.add).then_inc(hc, 1)
                    dve.wait_ge(hc, 2 * h + 2)
                    dve.tensor_scalar(HF[:, n], HF[:, n], 2.0 ** -64, None, ALU.max).then_inc(s_("hf_done"), 1)
                for n in range(2):
                    dve.wait_ge(s_("hg_sg"), 2 * i + n + 1)
                    dve.tensor_tensor(HGATE[:, n], ps[:, n], HSG[:, 2 + n], ALU.mult).then_inc(s_("hg_done"), 1)
                for n in range(2):
                    h = 2 * i + n
                    b = HF[:, n]
                    dve.wait_ge(s_("h_ln"), h + 1)
                    dve.tensor_tensor_scan(b, reset[:], b, 0.0, ALU.mult, ALU.add).then_inc(s_("h_scan"), 1)
                    dve.wait_ge(s_("h_scan"), h + 1)
                    b4 = b.rearrange("p (c t) -> p c t", t=P)
                    last = b4[:, :, P - 1:P].to_broadcast([P, TB, P])
                    dve.tensor_tensor(HKD[:].rearrange("p (c t) -> p c t", t=P), last, b4, ALU.subtract)\
                        .then_inc(s_("h_kd_arg"), 1)
                    for l, m in enumerate(LEVELS):
                        bv = b.rearrange("p (g u t) -> p g u t", u=2, t=m)
                        ev = HE[:, l].rearrange("p (g u t) -> p g u t", u=2, t=m)
                        ref = bv[:, :, 0, m - 1:m].to_broadcast([P, T // (2 * m), m])
                        dve.tensor_tensor(ev[:, :, 0], ref, bv[:, :, 0], ALU.subtract).then_inc(s_("h_arg"), 1)
                        dve.tensor_tensor(ev[:, :, 1], bv[:, :, 1], ref, ALU.subtract).then_inc(s_("h_arg"), 1)
                    dve.wait_ge(s_("h_eb"), h + 1)
                    dve.tensor_tensor(HQD[:], HQ[:, n], HEB[:], ALU.mult).then_inc(s_("h_qd"), 1)
                    dve.wait_ge(s_("h_kd_e"), h + 1)
                    dve.tensor_tensor(HKD[:], HKD[:], HK[:, n], ALU.mult).then_inc(s_("h_kd"), 1)
                    for l, m in enumerate(LEVELS):
                        ev = HE[:, l].rearrange("p (g u t) -> p g u t", u=2, t=m)
                        qv = HQ[:, n].rearrange("p (g u t) -> p g u t", u=2, t=m)
                        kv = HK[:, n].rearrange("p (g u t) -> p g u t", u=2, t=m)
                        dve.wait_ge(s_("h_e"), 7 * h + l + 1)
                        dve.tensor_tensor(ev[:, :, 0], ev[:, :, 0], kv[:, :, 0], ALU.mult).then_inc(s_("h_qk"), 1)
                        dve.tensor_tensor(ev[:, :, 1], ev[:, :, 1], qv[:, :, 1], ALU.mult).then_inc(s_("h_qk"), 1)
                    for l in range(len(LEVELS) + 1):
                        dve.wait_ge(s_("h_g"), 8 * h + l + 1)
                        if l:
                            dve.wait_ge(s_("h_g_free"), 8 * h + l + 2)
                        dve.sem_inc(s_("h_g_seen"), 1)
                        dve.copy_predicated(HP[:].rearrange("p (c t) -> p c t", t=P),
                                            masks[:, l:l + 1].to_broadcast([P, TB, P]),
                                            ps[:, 4 + l % 2].rearrange("p (c t) -> p c t", t=P)).then_inc(s_("h_g_free"), 1)
                    for b_ in range(3):
                        dve.wait_ge(s_("h_st"), 3 * h + b_ + 1)
                        dst = HS[:, b_]
                        if b_ == 0:
                            dve.tensor_copy(dst, ps[:, 7, 384:512]).then_inc(s_("h_s"), 1)
                        else:
                            dve.wait_ge(s_("h_s"), 3 * h + b_)
                            dve.scalar_tensor_tensor(dst, HS[:, b_ - 1], HEB[:, b_ * P + P - 1:b_ * P + P], ps[:, 7, 384:512],
                                                     ALU.mult, ALU.add).then_inc(s_("h_s"), 1)
                    dve.wait_ge(s_("h_std"), h + 1)
                    dve.reciprocal(rst[:, 1], rst[:, 0]).then_inc(s_("h_inv"), 1)
                    dve.wait_ge(s_("h_inv"), h + 1)
                    dve.scalar_tensor_tensor(tmp[:, 1], ps[:, 6], col("hgrn_g_norm_2"), rst[:, 1], ALU.mult, ALU.mult)\
                        .then_inc(s_("h_t1"), 1)
                    dve.wait_ge(s_("h_t1"), h + 1)
                    dve.tensor_tensor(tmp[:, 1], tmp[:, 1], HGATE[:, n], ALU.mult).then_inc(s_("h_t2"), 1)
                    dve.wait_ge(s_("oh_done"), h + 1)
                    dve.tensor_tensor(OL[:, bass.ds(h, 1)], tmp[:, 1:2], OH[:, bass.ds(h, 1)].bitcast(F32), ALU.subtract)\
                        .then_inc(s_("ho_done"), 1)

            residual("hwo", FIRST["hwo"], 2, (s_("ho_done"), 2 + HEADS_H))
            norm_dve(dve, "n_mlp1", "mlp_norm_2")
            mlp_dve("mlp1")
            norm_dve(dve, "n_kv", "kv_in_norm_2")

            def small_norm_dve(n, gain, hi, lo, inv):
                dve.wait_ge(*at(n, "std", 1))
                dve.reciprocal(inv, rst[:, 0]).then_inc(sig(n, "inv"), 1)
                dve.wait_ge(*at(n, "inv", 1))
                for k in range(2):
                    dve.scalar_tensor_tensor(CK[:, 2 + k], CK[:, k], col(gain, k), inv, ALU.mult, ALU.mult)\
                        .then_inc(sig(n, "t"), 1)
                for k in range(2):
                    dve.wait_ge(*at(n, "hi", k + 1))
                    dve.tensor_tensor(lo[:, k], CK[:, 2 + k], hi[:, k].bitcast(F32), ALU.subtract).then_inc(sig(n, "lo"), 1)

            small_norm_dve("ckv", "kv_norm_2", CKH, CKL, tmp[:, 0])
            dve.wait_ge(mconst_in, 64)
            dve.wait_ge(s_("kr_raw"), 1)
            dve.wait_ge(*at("ckv", "lo", 2))
            kc = Count(dve, "kr_chain")
            dve.wait_ge(s_("kr_swap"), 1)
            kc.put(dve.tensor_tensor(tmp[:, 2], ps[:, 3], sin_t[:], ALU.mult))
            kc.put(dve.tensor_tensor(KR[:], QR[:, 2], cos_t[:], ALU.mult))
            kc.wait()
            kc.put(dve.tensor_tensor(KR[:], KR[:], tmp[:, 2], ALU.add))
            dve.wait_ge(halves, half_at(FIRST["kvq"] + 1))
            kc.wait()
            norm_dve(dve, "n_mla", "mla_norm_2", invert=False)
            small_norm_dve("cq", "mla_q_norm_2", CQH, CQL, rst[:, 1])

            dve.wait_ge(*at("cq", "lo", 2))
            dve.sem_inc(s_("al_done"), 1)
            with dve.Fori(0, 4) as i:
                for h in range(2):
                    dve.wait_ge(s_("qr_raw"), 2 * i + h + 1)
                    dve.wait_ge(s_("qr_swap"), 2 * i + h + 1)
                    dve.tensor_tensor(rst[:, 0], ps[:, 6 + h], sin_t[:], ALU.mult).then_inc(s_("qr_a"), 1)
                    dve.tensor_tensor(QR[:, h], QR[:, 2 + h], cos_t[:], ALU.mult).then_inc(s_("qr_a"), 1)
                    dve.wait_ge(s_("qr_a"), 4 * i + 2 * h + 2)
                    dve.tensor_tensor(QR[:, h], QR[:, h], rst[:, 0], ALU.add).then_inc(s_("qr_done"), 1)
                    dve.wait_ge(s_("qr_done"), 2 * i + h + 1)

                def row_max(h):
                    for b in range(TB):
                        t = 16 * i + 4 * h + b
                        dg = ps[:, b, b * P:(b + 1) * P]
                        dve.wait_ge(s_("a_qk"), t + 1)
                        dve.tensor_tensor(dg, dg, neg_t[:], ALU.add).then_inc(s_("a_mask"), 1)
                        dve.wait_ge(s_("a_mask"), t + 1)
                        dve.tensor_reduce(small[:, 96 + b:97 + b], ps[:, b, 0:(b + 1) * P], AX, ALU.max)\
                            .then_inc(s_("a_max"), 1)
                        dve.wait_ge(s_("a_max"), t + 1)
                        dve.tensor_scalar(small[:, 100 + b:101 + b], small[:, 96 + b:97 + b], -SCALE, None, ALU.mult)\
                            .then_inc(s_("a_nmax"), 1)

                def scale_rows(h):
                    for b in range(TB):
                        t = 16 * i + 4 * h + b
                        dve.wait_ge(s_("a_exp"), t + 5)
                        dve.reciprocal(small[:, 108 + b:109 + b], small[:, 104 + b:105 + b]).then_inc(s_("a_rs"), 1)
                        dve.wait_ge(s_("a_rs"), t + 1)
                        dve.tensor_scalar(PM[:, b, 0:(b + 1) * P], PM[:, b, 0:(b + 1) * P], small[:, 108 + b:109 + b], None,
                                          ALU.mult).then_inc(s_("a_pm"), 1)

                row_max(0)
                for h in range(4):
                    scale_rows(h)
                    if h < 3:
                        row_max(h + 1)
                    dve.wait_ge(s_("ah_done"), 4 * i + h + 1)
                    dve.tensor_tensor(AL[:, bass.ds(4 * i + h, 1)], ps[:, 6:7], AH[:, bass.ds(4 * i + h, 1)].bitcast(F32),
                                      ALU.subtract).then_inc(s_("al_done"), 1)

            residual("mwo", FIRST["mwo"], 1, (s_("al_done"), 1 + HEADS_M))
            norm_dve(dve, "n_mlp2", "mlp_norm_2", 8)
            mlp_dve("mlp2")
            norm_dve(dve, "n_fin1", "final_norm_2", split=False)

        @block.tensor
        def _(pe):
            pe.sem_inc(halves, 4)
            pe.wait_ge(consts_in, 48)
            pe.wait_ge(x_in, 16)
            for k in range(KD):
                if k >= 4:
                    pe.wait_ge(s_("x_fm"), k - 3)
                for b in range(TB):
                    mm = pe.transpose(ps[:, k % 4, b * P:(b + 1) * P], x_tm[:, b, k * P:(k + 1) * P], ident[:])
                mm.then_inc(s_("x_turned"), 1)

            def product(dst, his, los, xh, xl, start=True, stop=True):
                n = len(his)
                for k in range(n):
                    pe.matmul(dst, his[k], xh[k], start=start and k == 0, stop=False)
                    pe.matmul(dst, his[k], xl[k], start=False, stop=False)
                    mm = pe.matmul(dst, los[k], xh[k], start=False, stop=stop and k == n - 1)
                return mm

            def product_x(dst, his, los, xh, xl, start=True, stop=True):
                n = len(his)
                for k in range(n):
                    pe.matmul(dst, xh[k], his[k], start=start and k == 0, stop=False)
                    pe.matmul(dst, xh[k], los[k], start=False, stop=False)
                    mm = pe.matmul(dst, xl[k], his[k], start=False, stop=stop and k == n - 1)
                return mm

            def tiles(t, n=KD, first=0):
                return [t[:, first + k] for k in range(n)]

            def chunk_in(c):
                pe.wait_ge(lo_done, c + 3)

            def half8(s, n, bank, xh, xl):
                product(ps[:, bank], w8(w_hi, s, n), w8(w_lo, s, n), tiles(xh), tiles(xl)).then_inc(halves, 1)

            norm_pe(pe, "n_mix")
            pe.wait_ge(*at("n_mix", "lo", KD))

            def plain(c, iters, ev, xh, xl):
                with pe.Fori(0, iters) as i:
                    for j in range(4):
                        if j % 2 == 0:
                            chunk_in(2 * i + c + j // 2)
                        pe.wait_ge(*ev(4 * i + j + 1))
                        half8(j // 2, j % 2, j, xh, xl)

            plain(FIRST["ug"], 4, lambda v: (s_("ug_evac"), v), XH, XL)
            plain(FIRST["xb"], 3, lambda v: (s_("xb_evac"), v), XH, XL)

            pe.wait_ge(s_("xb_evac"), 4 + RT)
            c = FIRST["band"]
            with pe.Fori(0, 2) as i:
                for s in range(2):
                    chunk_in(2 * i + c + s)
                    pe.wait_ge(s_("vl_done"), 6 * i + 3 * s + 3)
                    pe.wait_ge(s_("lru_done"), 6 * i + 3 * s + 1)
                    for gate in range(2):
                        for o in range(3):
                            ks = [n for n, (r, q) in enumerate(BAND) if q == o]
                            wt = [[t[:, s, (7 * gate + n) * P:(7 * gate + n + 1) * P] for n in ks] for t in (w_hi, w_lo)]
                            mm = product(ps[:, 3 * gate + o], wt[0], wt[1],
                                         [VH[:, BAND[n][0]] for n in ks], [VL[:, BAND[n][0]] for n in ks])
                        mm.then_inc(halves, 1)

            pe.wait_ge(s_("conv"), 8 * 32)
            pe.wait_ge(s_("lru_done"), 1 + RT)
            for k in range(KD):
                pe.matmul(ps[:, 7], ones[:], CO[:, k], start=k == 0, stop=k == KD - 1).then_inc(s_("mu_mm"), 1)
            for k in range(KD):
                pe.wait_ge(s_("xc_sq"), k + 1)
                pe.matmul(ps[:, 7], ones[:], tmp[:, k % 2], start=k == 0, stop=k == KD - 1).then_inc(s_("var_mm"), 1)

            c = FIRST["saya"]
            pe.wait_ge(s_("ul_done"), KD)
            with pe.Fori(0, 4) as i:
                chunk_in(2 * i + c)
                for j in range(2):
                    pe.wait_ge(s_("ya_done"), 2 * i + j + 1)
                    half8(0, j, j, XH, XL)
                chunk_in(2 * i + c + 1)
                for j in range(2):
                    half8(1, j, 2 + j, UH, UL)

            plain(FIRST["sb"], 2, lambda v: (s_("sb_evac"), v), XH, XL)
            plain(FIRST["gb"], 3, lambda v: (s_("gb_evac"), v), XH, XL)

            def single(c, kt, ev, xh, xl):
                with pe.Fori(0, 2) as i:
                    for j in range(4):
                        chunk_in(4 * i + c + j)
                        pe.wait_ge(*ev(4 * i + j + 1))
                        h, l = w1(w_hi, j % 2, kt), w1(w_lo, j % 2, kt)
                        n = kt // 2
                        product(ps[:, j], h[:n], l[:n], tiles(xh, n), tiles(xl, n), stop=False).then_inc(halves, 1)
                        product(ps[:, j], h[n:], l[n:], tiles(xh, n, n), tiles(xl, n, n), start=False).then_inc(halves, 1)

            pe.wait_ge(s_("vg_lo"), 2 + RT)
            single(FIRST["bo"], RT, lambda v: (s_("yb_evac"), v), VGH, VGL)
            pe.wait_ge(s_("ml_done"), KD)
            plain(FIRST["wo"], 2, lambda v: at("wo", "x", v), MH, ML)

            def mlp_pe(n):
                c = FIRST[n]
                with pe.Fori(0, 4) as q:
                    with pe.Fori(0, 2) as i:
                        for j in range(4):
                            if j % 2 == 0:
                                chunk_in(8 * q + 2 * i + c + j // 2)
                            pe.wait_ge(*at(n, "dn", 8 * q + j + 1))
                            pe.wait_ge(*at(n, "r", 8 * q + 4 * i + j + 1))
                            half8(j // 2, j % 2, j, XH, XL)
                    with pe.Fori(0, 2) as i:
                        for j in range(4):
                            if j % 2 == 0:
                                chunk_in(8 * q + 2 * i + c + 4 + j // 2)
                            pe.wait_ge(*at(n, "fl", 8 * q + 12))
                            pe.wait_ge(*at(n, "dn", 8 * q + 4 * i + j + 1))
                            half8(j // 2, j % 2, j, FH, FL)

            norm_pe(pe, "n_mlp0")
            pe.wait_ge(*at("n_mlp0", "lo", KD))
            mlp_pe("mlp0")
            norm_pe(pe, "n_fin0")
            norm_pe(pe, "n_hg")
            pe.wait_ge(*at("n_hg", "lo", KD))

            c = FIRST["hg"]
            with pe.Fori(0, 4) as i:
                for n in range(4):
                    chunk_in(4 * i + c + n)
                    for j in range(2):
                        if n == 0:
                            pe.wait_ge(s_("hg_done"), 2 * i + j + 1)
                            half8(0, j, j, XH, XL)
                        elif n == 1:
                            pe.wait_ge(s_("hv_done"), 2 * i + j + 1)
                            half8(1, j, 2 + j, XH, XL)
                        elif n == 2:
                            pe.wait_ge(s_("hq_done"), 2 * i + j + 3)
                            half8(0, j, j, XH, XL)
                        else:
                            pe.wait_ge(s_("hf_sg"), 2 * i + j + 1)
                            hi = w_hi[:, 1].rearrange("p (k n) -> p k n", k=8)
                            lo = w_lo[:, 1].rearrange("p (k n) -> p k n", k=8)
                            for b in range(2):
                                t0 = (2 * j + b) * P
                                mm = product_x(ps[:, 2 + j, b * 256:(b + 1) * 256], tiles(hi), tiles(lo),
                                               [XH[:, k, t0:t0 + P] for k in range(KD)],
                                               [XL[:, k, t0:t0 + P] for k in range(KD)])
                            mm.then_inc(halves, 1)
                for n in range(2):
                    h = 2 * i + n
                    for l in range(len(LEVELS) + 1):
                        pe.wait_ge(s_("h_g_free"), 8 * h + l + 1)
                        if l < len(LEVELS):
                            pe.wait_ge(s_("h_qk"), 14 * h + 2 * l + 2)
                        for b in range(TB):
                            t = slice(b * P, (b + 1) * P)
                            st, mv = (HE[:, l, t], HE[:, l, t]) if l < len(LEVELS) else (HK[:, n, t], HQ[:, n, t])
                            mm = pe.matmul(ps[:, 4 + l % 2, t], st, mv, start=True, stop=True)
                        mm.then_inc(s_("h_g"), 1)
                    pe.wait_ge(s_("h_kd"), h + 1)
                    for b in range(3):
                        pe.transpose(ps[:, 7, b * P:(b + 1) * P], HKD[:, b * P:(b + 1) * P], ident[:]).then_inc(s_("h_kt"), 1)
                    pe.wait_ge(s_("h_kt_c"), h + 1)
                    pe.wait_ge(s_("hv_done"), 2 * i + 4)
                    hv = [HV[:, b, n * P:(n + 1) * P] for b in range(TB)]
                    for b in range(3):
                        if b:
                            pe.wait_ge(s_("h_s"), 3 * h + b)
                        pe.matmul(ps[:, 7, 384:512], HKT[:, b], hv[b], start=True, stop=True).then_inc(s_("h_st"), 1)
                    pe.wait_ge(s_("h_g_free"), 8 * h + 10)
                    pe.wait_ge(s_("h_s"), 3 * h + 3)
                    for b in range(TB):
                        t = slice(b * P, (b + 1) * P)
                        mm = pe.matmul(ps[:, 6, t], hv[b], HP[:, t], start=True, stop=b == 0)
                        if b:
                            mm = pe.matmul(ps[:, 6, t], HS[:, b - 1], HQD[:, t], start=False, stop=True)
                    mm.then_inc(s_("h_o"), 1)
                    pe.wait_ge(s_("h_sq"), h + 1)
                    pe.matmul(ps[:, 7], ones[:], tmp[:, 0], start=True, stop=True).then_inc(s_("h_mean"), 1)

            pe.wait_ge(s_("ho_done"), 2 + HEADS_H)
            plain(FIRST["hwo"], 2, lambda v: at("hwo", "x", v), OH, OL)
            norm_pe(pe, "n_mlp1")
            pe.wait_ge(*at("n_mlp1", "lo", KD))
            mlp_pe("mlp1")
            norm_pe(pe, "n_kv")
            pe.wait_ge(*at("n_kv", "lo", KD))

            c = FIRST["kvq"]
            chunk_in(c)
            for j in range(2):
                half8(0, j, j, XH, XL)

            def one_tile(c, s, bank):
                chunk_in(c)
                h, l = w1(w_hi, s, 8), w1(w_lo, s, 8)
                product(ps[:, bank], h[:4], l[:4], tiles(XH, 4), tiles(XL, 4), stop=False).then_inc(halves, 1)
                product(ps[:, bank], h[4:], l[4:], tiles(XH, 4, 4), tiles(XL, 4, 4), start=False).then_inc(halves, 1)

            def small_norm_pe(n):
                for k in range(2):
                    pe.wait_ge(*at(n, "sq", k + 1))
                    mm = pe.matmul(ps[:, 7], ones[:], tmp[:, k], start=k == 0, stop=k == 1)
                mm.then_inc(sig(n, "mean"), 1)

            one_tile(c + 1, 1, 2)
            small_norm_pe("ckv")
            pe.wait_ge(mconst_in, 64)
            pe.wait_ge(s_("kr_raw"), 1)
            pe.matmul(ps[:, 3], swap_t[:], QR[:, 2], start=True, stop=True).then_inc(s_("kr_swap"), 1)
            pe.wait_ge(*at("n_mla", "lo", KD))
            one_tile(c + 2, 0, 0)
            one_tile(c + 3, 1, 1)
            small_norm_pe("cq")

            c = FIRST["att"]
            pe.wait_ge(*at("cq", "lo", 2))
            pe.sem_inc(s_("a_pt"), 4)
            pe.sem_inc(s_("a_pv"), 1)
            with pe.Fori(0, 4) as i:
                def part(t, s, at, k, step, n):
                    return [t[:, s, at + q * step:at + q * step + n] for q in range(k)]

                chunk_in(2 * i + c)
                pe.wait_ge(s_("a_exp"), 16 * i + 4)
                for h in range(4):
                    mm = product(ps[:, h], part(w_hi, 0, h * P, 2, 512, P), part(w_lo, 0, h * P, 2, 512, P),
                                 tiles(CKH, 2), tiles(CKL, 2))
                mm.then_inc(halves, 1)
                pe.wait_ge(s_("al_done"), 4 * i + 1)
                for b in range(TB):
                    mm = product_x(ps[:, 4 + b], part(w_hi, 0, 1024, 2, 512, 512), part(w_lo, 0, 1024, 2, 512, 512),
                                   [CKH[:, k, b * P:(b + 1) * P] for k in range(2)],
                                   [CKL[:, k, b * P:(b + 1) * P] for k in range(2)])
                mm.then_inc(halves, 1)
                chunk_in(2 * i + c + 1)
                for h in range(4):
                    pe.wait_ge(s_("kn_done"), 4 * i + h + 1)
                    mm = product(ps[:, h], part(w_hi, 1, h * P, 2, 512, P), part(w_lo, 1, h * P, 2, 512, P),
                                 tiles(CQH, 2), tiles(CQL, 2))
                mm.then_inc(halves, 1)
                pe.wait_ge(s_("vt_done"), 4 * i + 4)
                for h in range(2):
                    mm = product(ps[:, 4 + h], part(w_hi, 1, 1024 + h * P, 2, 256, P),
                                 part(w_lo, 1, 1024 + h * P, 2, 256, P), tiles(CQH, 2), tiles(CQL, 2))
                mm.then_inc(halves, 1)
                for h in range(2):
                    pe.wait_ge(s_("qr_raw"), 2 * i + h + 1)
                    pe.matmul(ps[:, 6 + h], swap_t[:], QR[:, 2 + h], start=True, stop=True).then_inc(s_("qr_swap"), 1)

                def scores(h):
                    r = slice(ROPE * (h % 2), ROPE * (h % 2) + ROPE)
                    for b in range(TB):
                        n = (b + 1) * P
                        pe.wait_ge(s_("a_exp"), 16 * i + 4 * h + b + 1)
                        pe.matmul(ps[:, b, 0:n], QN[:, h, b * P:n], KN[:, h, 0:n], start=True, stop=False)
                        pe.matmul(ps[:, b, 0:n], QR[r, h // 2, b * P:n], KR[r, 0:n], start=False, stop=True)\
                            .then_inc(s_("a_qk"), 1)

                def turn(h):
                    for b in range(TB):
                        t = 16 * i + 4 * h + b
                        pe.wait_ge(s_("a_pm"), t + 1)
                        pe.wait_ge(s_("a_ptc"), t + 1)
                        for j in range(b + 1):
                            mm = pe.transpose(ps[:, 4 + b % 2, j * P:(j + 1) * P], PM[:, b, j * P:(j + 1) * P], ident[:])
                        mm.then_inc(s_("a_pt"), 1)

                def weigh(h):
                    pe.wait_ge(s_("a_ptc"), 16 * i + 4 * h + 6)
                    pe.wait_ge(s_("al_done"), 4 * i + h + 1)
                    for j in range(TB):
                        mm = pe.matmul(ps[:, 6, j * P:T], VT[:, j, h * P:(h + 1) * P], PT[:, j, j * P:T],
                                       start=j == 0, stop=j == TB - 1)
                    mm.then_inc(s_("a_pv"), 1)

                pe.wait_ge(s_("qn_done"), 4 * i + 4)
                pe.wait_ge(s_("qr_done"), 2 * i + 2)
                scores(0)
                for h in range(4):
                    if h < 3:
                        scores(h + 1)
                    turn(h)
                    weigh(h)

            pe.wait_ge(s_("al_done"), 1 + HEADS_M)
            single(FIRST["mwo"], 16, lambda v: at("mwo", "x", v), AH, AL)
            norm_pe(pe, "n_mlp2")
            pe.wait_ge(*at("n_mlp2", "lo", KD))
            mlp_pe("mlp2")
            norm_pe(pe, "n_fin1")
            pe.wait_ge(*at("n_fin1", "t", KD))
            for g in range(TB * 2):
                b = g // 2
                if g >= 4:
                    pe.wait_ge(s_("y_out"), g - 3)
                for j in range(4):
                    mm = pe.transpose(ps[:, g % 4, j * P:(j + 1) * P], X[:, 4 * (g % 2) + j, b * P:(b + 1) * P], ident[:])
                mm.then_inc(s_("y_turned"), 1)


def level_masks():
    s, t = np.arange(P)[:, None], np.arange(P)[None, :]
    out = [(s // (2 * m) == t // (2 * m)) & (s % (2 * m) < m) & (t % (2 * m) >= m) for m in LEVELS]
    return np.ascontiguousarray(np.stack(out + [s == t], axis=1).astype(np.float32).reshape(P, 2, T))


def rotary():
    half = ROPE // 2
    inv_freq = np.float32(10000.0) ** (-np.arange(half, dtype=np.float32) / np.float32(half))
    ang = (np.arange(T, dtype=np.float32)[:, None] * inv_freq[None, :]).T
    cos, sin = np.cos(ang), np.sin(ang)
    swap = np.zeros((P, P), np.float32)
    swap[np.arange(P), np.arange(P) ^ half] = 1.0
    return np.concatenate([cos] * 4), np.concatenate([-sin, sin] * 2), swap


def constants():
    cos, sin, swap = rotary()
    r = np.ones((P, T), np.float32)
    r[:, ::P] = 0.0
    return {
        "ident": np.eye(P, dtype=np.float32), "ones": np.ones((P, P), np.float32),
        "level_masks": level_masks(), "reset": r, "cos": cos, "sin": sin, "swap": swap,
        "neg": np.triu(np.full((P, P), -1e30, np.float32), 1),
    }


def pack_vectors(inputs):
    cols = []
    for name, n in VECTOR_WIDTHS:
        if name == "eps":
            v = np.full((P, 1), EPS, np.float32)
        elif name in ("conv_a_w", "conv_b_w"):
            w = np.asarray(inputs[name])[0]
            v = w.reshape(w.shape[0], -1, P).transpose(2, 1, 0).reshape(P, n)
        else:
            v = np.asarray(inputs[name]).reshape(n, P).T
        cols.append(v)
    return np.ascontiguousarray(np.concatenate(cols, axis=1))


WEIGHTS = ["w_in", "w_a_out", "w_rg_a", "w_rg_x", "w_b_out", "w_o", "w_1", "w_2", "hgrn_w_q_2", "hgrn_w_f_2",
           "hgrn_w_i_2", "hgrn_w_g_2", "hgrn_w_o_2", "mla_w_dq_2", "mla_w_uq_2", "mla_w_o_2"]
PLAIN = ["x", "kv_w_dkv_2", "kv_w_uk_2", "kv_w_uv_2", "mlp_w_up_2", "mlp_w_down_2"]


def kernel(**inputs):
    import concourse.bacc as _bacc
    from concourse.bass_utils import run_bass_kernel_spmd as _run

    nc = _bacc.Bacc("TRN2", target_bir_lowering=False, num_devices=1)
    arrays = {n: np.ascontiguousarray(inputs[n]) for n in WEIGHTS + PLAIN}
    arrays["vectors"] = pack_vectors(inputs)
    arrays.update(constants())
    aps, sent = {}, {}
    for name, v in arrays.items():
        sent[f"in_{name}"] = v
        ap = nc.dram_tensor(f"in_{name}", v.shape, mybir.dt.from_np(v.dtype), kind="ExternalInput").ap()
        aps[name] = ap[0] if name in WEIGHTS else ap
    out = nc.dram_tensor("out_0", (1, T, D), F32, kind="ExternalOutput").ap()
    build_program(nc, aps, out)
    r = _run(nc, [sent], core_ids=[0])
    return r.results[0]["out_0"]
```

```python
from contextlib import ExitStack

import numpy as np

import concourse.bass as bass
from concourse import mybir

P = 128
T = 512
TB = T // P
D = 1024
KD = D // P
D_RNN = 1536
RT = D_RNN // P
TAPS_A = 31
TAPS_B = 4
HEADS_H = 8
HEADS_M = 16
NOPE, ROPE = 128, 64
LORA = 256
D_FF = 4096
Q_FF = D_FF // 4
SCALE = float(NOPE + ROPE) ** -0.5
LEVELS = (64, 32, 16, 8, 4, 2, 1)
BO_BANKS = (6, 7, 0, 1)
EPS = 1e-6

F32 = mybir.dt.float32
F32R = mybir.dt.float32r
U8 = mybir.dt.uint8
ALU = mybir.AluOpType
ACT = mybir.ActivationFunctionType
AX = mybir.AxisListType.X

VECTOR_WIDTHS = [
    ("g_mix", 8), ("b_in", 56), ("conv_a_b", 8), ("ln_g", 8), ("ln_b", 8), ("conv_b_b", 12),
    ("b_rg_a", 12), ("b_rg_x", 12), ("lam", 12), ("g_mlp", 8), ("g_final", 8), ("hgrn_norm_2", 8),
    ("hgrn_g_norm_2", 1), ("hgrn_lb_logits_2", 16), ("mla_norm_2", 8), ("mla_q_norm_2", 2),
    ("kv_in_norm_2", 8), ("kv_norm_2", 2), ("mlp_norm_2", 16), ("final_norm_2", 8),
    ("conv_b_w", 48), ("conv_a_w", 248), ("eps", 1),
]
COLUMN = {}
_at = 0
for _name, _n in VECTOR_WIDTHS:
    COLUMN[_name] = _at
    _at += _n
N_COLUMNS = _at

CHUNKS = [("xb", 6), ("ug", 8), ("gb", 6), ("sb", 4), ("sa", 4), ("yaband", 8), ("bo", 8), ("wo", 4),
          ("mlp0", 32), ("hg", 16), ("hwo", 4), ("mlp1", 32), ("kvq", 4), ("att", 8), ("mwo", 8),
          ("mlp2", 32)]
FIRST = {}
_at = 0
for _name, _n in CHUNKS:
    FIRST[_name] = _at
    _at += _n
N_CHUNKS = _at

BAND = [(0, 0), (1, 0), (0, 1), (1, 1), (2, 1), (1, 2), (2, 2)]


def build_program(nc, a, out):
    ctx = ExitStack()
    with ctx:
        top = [nc.sbuf_base + (-nc.sbuf_base) % 32]

        def place(name, shape, dt, at=None):
            size = int(np.prod(shape[1:])) * (1 if dt == U8 else 4)
            where = top[0] if at is None else at
            if at is None:
                top[0] += size + (-size) % 32
            return nc.alloc_sbuf_tensor_at(name, list(shape), dt, offset=where), where

        def sem(name):
            return ctx.enter_context(nc.semaphore(name))

        raw, _ = place("raw", [P, 2, 2048], F32)
        w_hi, _ = place("w_hi", [P, 2, 2048], F32R)
        w_lo, _ = place("w_lo", [P, 2, 2048], F32R)
        vec, _ = place("vec", [P, N_COLUMNS], F32)
        ident, _ = place("ident", [P, P], F32)
        ones, _ = place("ones", [P, P], F32)
        small, _ = place("small", [P, 128], F32)
        tmp, a_tmp = place("tmp", [P, 4, T], F32)
        rst, a_rst = place("rst", [P, 2, T], F32)
        X, _ = place("X", [P, KD, T], F32)
        XH, a_xh = place("XH", [P, KD, T], F32R)
        XL, _ = place("XL", [P, KD, T], F32R)
        S = top[0]
        TILE = T * 4

        x_tm, _ = place("x_tm", [P, TB, D], F32, S)
        CO, _ = place("CO", [P, KD, T], F32, S)
        LR, _ = place("LR", [P, 6, T], F32, S)
        MH, _ = place("MH", [P, KD, T], F32R, S)
        V, _ = place("V", [P, RT, T], F32, S + 8 * TILE)
        VGH, _ = place("VGH", [P, RT, T], F32R, S + 8 * TILE)
        G, _ = place("G", [P, RT, T], F32, S + 20 * TILE)
        VGL, _ = place("VGL", [P, RT, T], F32R, S + 20 * TILE)
        XBR, _ = place("XBR", [P, RT, 4 + T], F32, S + 20 * TILE)
        SBG, _ = place("SBG", [P, KD, T], F32, S + 32 * TILE)
        ML, _ = place("ML", [P, KD, T], F32R, S + 32 * TILE)
        GA, _ = place("GA", [P, KD, T], F32, S + 40 * TILE)
        M, _ = place("M", [P, KD, T], F32, S + 40 * TILE)
        PAD = TAPS_A - 1
        UP, _ = place("UP", [P, 2, PAD + T], F32, a_tmp + 2 * TILE)
        VH, _ = place("VH", [P, 3, T], F32R, a_tmp)
        VL, _ = place("VL", [P, 3, T], F32R, a_tmp + 3 * TILE)
        assert a_rst == a_tmp + 4 * TILE
        at_end = S + 48 * TILE
        FH, _ = place("FH", [P, KD, T], F32R, S)
        FL, _ = place("FL", [P, KD, T], F32R, S + KD * TILE)
        base = S
        OH, _ = place("OH", [P, KD, T], F32R, base)
        OL, _ = place("OL", [P, KD, T], F32R, base + 8 * TILE)
        HQ, _ = place("HQ", [P, 2, T], F32, base + 16 * TILE)
        HK, _ = place("HK", [P, 2, T], F32, base + 18 * TILE)
        HF, _ = place("HF", [P, 2, T], F32, base + 20 * TILE)
        HGATE, _ = place("HGATE", [P, 2, T], F32, base + 22 * TILE)
        HV, _ = place("HV", [P, TB, 256], F32, base + 24 * TILE)
        HE, _ = place("HE", [P, 8, T], F32, base + 26 * TILE)
        HP, _ = place("HP", [P, T], F32, base + 34 * TILE)
        HQD, _ = place("HQD", [P, T], F32, base + 35 * TILE)
        HKD, _ = place("HKD", [P, T], F32, base + 36 * TILE)
        HEB, _ = place("HEB", [P, T], F32, base + 37 * TILE)
        HKT, _ = place("HKT", [P, 3, P], F32, base + 38 * TILE)
        HS, _ = place("HS", [P, 3, P], F32, base + 39 * TILE)
        HSG, _ = place("HSG", [P, 4, T], F32, base + 40 * TILE)
        masks, _ = place("masks", [P, 8, P], U8, base + 44 * TILE)
        reset, _ = place("reset", [P, T], F32, base + 45 * TILE)
        AH, _ = place("AH", [P, HEADS_M, T], F32R, a_xh)
        AL, _ = place("AL", [P, HEADS_M, T], F32R, S)
        base = S + 16 * TILE
        KN, _ = place("KN", [P, 4, T], F32, base)
        QN, _ = place("QN", [P, 4, T], F32, base + 4 * TILE)
        VT, _ = place("VT", [P, TB, 512], F32, base + 8 * TILE)
        PM, _ = place("PM", [P, TB, T], F32, base + 12 * TILE)
        PT, _ = place("PT", [P, TB, T], F32, base + 16 * TILE)
        QR, _ = place("QR", [P, 4, T], F32, base + 20 * TILE)
        KR, _ = place("KR", [P, T], F32, base + 24 * TILE)
        cos_t, _ = place("cos_t", [P, T], F32, base + 25 * TILE)
        sin_t, _ = place("sin_t", [P, T], F32, base + 26 * TILE)
        swap_t, _ = place("swap_t", [P, P], F32, base + 27 * TILE)
        neg_t, _ = place("neg_t", [P, P], F32, base + 27 * TILE + 512)
        CKH, _ = place("CKH", [P, 2, T], F32R, base + 28 * TILE)
        CKL, _ = place("CKL", [P, 2, T], F32R, base + 30 * TILE)
        CQH, _ = place("CQH", [P, 2, T], F32R, a_tmp)
        CQL, _ = place("CQL", [P, 2, T], F32R, a_tmp + 2 * TILE)
        CK, _ = place("CK", [P, 4, T], F32, S + 8 * TILE)
        XH2, _ = place("XH2", [P, KD, T], F32R, base)
        XL2, _ = place("XL2", [P, KD, T], F32R, base + 8 * TILE)
        y_tm, _ = place("y_tm", [P, TB, D], F32, S)
        assert max(at_end, S + 46 * TILE, base + 32 * TILE) <= nc.sbuf_usable_end, (
            max(at_end, S + 46 * TILE, base + 32 * TILE) - nc.sbuf_usable_end)

        ps = ctx.enter_context(nc.psum_tensor("ps", [P, 8, T], F32))

        raw_in = [sem("raw_in_0"), sem("raw_in_1")]
        hi_done = sem("hi_done")
        lo_done = sem("lo_done")
        halves = sem("halves")
        band_in = sem("band_in")
        band_zero = sem("band_zero")
        parts_in = sem("parts_in")
        consts_in = sem("consts_in")
        x_in = sem("x_in")
        hconst_in = sem("hconst_in")
        mconst_in = sem("mconst_in")
        out_done = sem("out_done")

        S_ = {}

        def s_(name):
            if name not in S_:
                S_[name] = sem(name)
            return S_[name]

        kinds = {
            "norm": ["n_mix", "n_fin0", "n_hg", "n_fin1"],
            "scaled": ["n_mlp0", "n_mlp1", "n_kv", "n_mla", "n_mlp2"],
            "small": ["ckv", "cq"],
            "mlp": ["mlp0", "mlp1", "mlp2"],
            "sum": ["wo", "hwo", "mwo"],
        }
        kind_of = {n: kind for kind, stages in kinds.items() for n in stages}

        def signals(n, what):
            if kind_of[n] == "norm":
                if what in ("hi", "lo"):
                    return 0 if n in ("n_fin0", "n_fin1") else KD
                return 1 if what in ("std", "inv") else KD
            if kind_of[n] == "scaled":
                if what in ("hi", "lo"):
                    return KD
                return 0 if n == "n_mla" else {"sq": KD, "add": KD - 1, "mean": 1, "std": 1, "inv": 1}[what]
            if kind_of[n] == "small":
                return 1 if what in ("mean", "std", "inv") else 2
            return {"mlp": {"t": 4 + 32, "sq": 32, "fh": 32, "fl": 4 + 32, "dn": 4 + 32}, "sum": {"x": 4 + KD}}[kind_of[n]][what]

        def sig(n, what):
            return s_(kind_of[n] + "_" + what)

        def at(n, what, value):
            stages = kinds[kind_of[n]]
            return sig(n, what), value + sum(signals(m, what) for m in stages[:stages.index(n)])

        def half_at(c, j=1):
            return 2 * c + (5 + j)

        def col(name, k=0, n=1):
            return vec[:, COLUMN[name] + k:COLUMN[name] + k + n]

        def dcol(name, k):
            return vec[:, bass.ds(k + COLUMN[name], 1)]

        def w8(t, s, n):
            v = t[:, s].rearrange("p (k n) -> p k n", k=8)
            return [v[:, k, n * P:(n + 1) * P] for k in range(8)]

        def w1(t, s, kt):
            v = t[:, s, 0:kt * P].rearrange("p (k n) -> p k n", k=kt)
            return [v[:, k] for k in range(kt)]

        class Count:

            def __init__(self, eng, name):
                self.eng, self.sem, self.at = eng, s_(name), 0

            def put(self, instruction):
                instruction.then_inc(self.sem, 1)
                self.at = self.at + 1
                return self.at

            def wait(self, value=None):
                self.eng.wait_ge(self.sem, self.at if value is None else value)

        def norm_act(act, n, ready, split=True, squares=True):
            if squares:
                for k in range(KD):
                    act.wait_ge(*ready(k))
                    if k >= 2:
                        act.wait_ge(*at(n, "mean", k - 1))
                    act.activation(tmp[:, k % 2], X[:, k], ACT.Square).then_inc(sig(n, "sq"), 1)
                act.wait_ge(*at(n, "mean", KD))
                act.activation(rst[:, 0], ps[:, 7], ACT.Sqrt, bias=col("eps"), scale=1.0 / D)\
                    .then_inc(sig(n, "std"), 1)
            if split:
                for k in range(KD):
                    act.wait_ge(*at(n, "t", k + 1))
                    act.activation(XH[:, k], tmp[:, 2 + k % 2], ACT.Copy).then_inc(sig(n, "hi"), 1)

        def norm_pe(pe, n):
            for k in range(KD):
                pe.wait_ge(*at(n, "sq", k + 1))
                pe.matmul(ps[:, 7], ones[:], tmp[:, k % 2], start=k == 0, stop=k == KD - 1)\
                    .then_inc(sig(n, "mean"), 1)

        def norm_dve(dve, n, gain, off=0, split=True, invert=True):
            if invert:
                dve.wait_ge(*at(n, "std", 1))
                dve.reciprocal(rst[:, 1], rst[:, 0]).then_inc(sig(n, "inv"), 1)
                dve.wait_ge(*at(n, "inv", 1))
            for k in range(KD + 1):
                if k < KD:
                    if split and k >= 2:
                        dve.wait_ge(*at(n, "lo", k - 1))
                    dve.scalar_tensor_tensor(tmp[:, 2 + k % 2] if split else X[:, k], X[:, k],
                                             col(gain, off + k), rst[:, 1], ALU.mult, ALU.mult)\
                        .then_inc(sig(n, "t"), 1)
                if split and k >= 1:
                    dve.wait_ge(*at(n, "hi", k))
                    dve.tensor_tensor(XL[:, k - 1], tmp[:, 2 + (k - 1) % 2], XH[:, k - 1].bitcast(F32),
                                      ALU.subtract).then_inc(sig(n, "lo"), 1)

        def scaled_act(act, n, ready, gain, off=0, xh=XH):
            for k in range(KD):
                act.wait_ge(*ready(k))
                act.activation(xh[:, k], X[:, k], ACT.Copy, scale=col(gain, off + k)).then_inc(sig(n, "hi"), 1)

        def squares_act(act, n):
            for k in range(KD):
                if k >= 4:
                    act.wait_ge(*at(n, "add", k - 4 + (k == 4)))
                act.activation(tmp[:, k % 4], X[:, k], ACT.Square).then_inc(sig(n, "sq"), 1)
            act.wait_ge(*at(n, "mean", 1))
            act.activation(rst[:, 0], ps[:, 7], ACT.Sqrt, bias=col("eps"), scale=1.0 / D).then_inc(sig(n, "std"), 1)

        def scaled_dve(dve, n, gain, off=0, xh=XH, xl=XL):
            for k in range(KD):
                dve.wait_ge(*at(n, "hi", k + 1))
                dve.scalar_tensor_tensor(xl[:, k], X[:, k], col(gain, off + k), xh[:, k].bitcast(F32), ALU.mult,
                                         ALU.subtract).then_inc(sig(n, "lo"), 1)

        def squares_dve(dve, n):
            for k in range(1, KD):
                dve.wait_ge(*at(n, "sq", k + 1))
                if k >= 2:
                    dve.wait_ge(*at(n, "add", k - 1))
                dve.tensor_tensor(rst[:, 0], rst[:, 0] if k >= 2 else tmp[:, 0], tmp[:, k % 4], ALU.add)\
                    .then_inc(sig(n, "add"), 1)
            dve.wait_ge(*at(n, "std", 1))
            dve.reciprocal(rst[:, 1], rst[:, 0]).then_inc(sig(n, "inv"), 1)
            dve.wait_ge(*at(n, "inv", 1))

        def squares_pe(pe, n):
            pe.wait_ge(*at(n, "add", KD - 1))
            pe.matmul(ps[:, 7], ones[:], rst[:, 0], start=True, stop=True).then_inc(sig(n, "mean"), 1)

        block = ctx.enter_context(nc.Block())

        @block.sync
        def _(sp):
            sp.dma_start(x_tm[:], a["x"].rearrange("b (t p) d -> p (b t) d", p=P)).then_inc(x_in, 16)
            sp.dma_start(vec[:], a["vectors"]).then_inc(consts_in, 16)
            sp.dma_start(ident[:], a["ident"]).then_inc(consts_in, 16)
            sp.dma_start(ones[:], a["ones"]).then_inc(consts_in, 16)

            def slot_free(c):
                sp.wait_ge(lo_done, c + 1)

            def load8(c, s, w, col0, row0=0, waited=False):
                if not waited:
                    slot_free(c)
                v = raw[:, s].rearrange("p (k n) -> p k n", k=8)
                for h in range(2):
                    sp.dma_start(v[:, 4 * h:4 * h + 4],
                                 w[bass.ds(row0 + 512 * h, 512), bass.ds(col0, 256)]
                                 .rearrange("(k p) n -> p k n", p=P)).then_inc(raw_in[s], 16)

            def load1(c, s, w, col0, kt):
                slot_free(c)
                v = raw[:, s, 0:kt * P].rearrange("p (k n) -> p k n", k=kt)
                for h in range(2):
                    sp.dma_start(v[:, h * kt // 2:(h + 1) * kt // 2],
                                 w[h * kt * P // 2:(h + 1) * kt * P // 2, bass.ds(col0, P)]
                                 .rearrange("(k p) n -> p k n", p=P)).then_inc(raw_in[s], 16)

            w_in = a["w_in"]

            def load_pairs(stage, iters, col0):
                c = FIRST[stage]
                with sp.Fori(0, iters) as i:
                    for s in range(2):
                        load8(2 * i + c + s, s, w_in, i * 512 + 256 * s + col0)

            load_pairs("xb", 3, 2 * D)
            c = FIRST["ug"]
            with sp.Fori(0, 4) as i:
                load8(2 * i + c, 0, w_in, i * 256)
                load8(2 * i + c + 1, 1, w_in, i * 256 + D)
            load_pairs("gb", 3, 2 * D + D_RNN)
            load_pairs("sb", 2, 3 * D + 2 * D_RNN)
            load_pairs("sa", 2, 2 * D + 2 * D_RNN)
            c = FIRST["yaband"]
            with sp.Fori(0, 4) as i:
                slot_free(2 * i + c)
                sp.sem_inc(s_("w_a_slot"), 1)
                load8(2 * i + c, 0, a["w_a_out"], i * 256, waited=True)
                slot_free(2 * i + c + 1)
                sp.wait_ge(band_zero, 1)
                n = 0
                for gate, w in enumerate((a["w_rg_a"], a["w_rg_x"])):
                    for j in range(4):
                        r = 96 * j
                        while r < 96 * j + 96:
                            r1 = min(96 * j + 96, (r // P + 1) * P)
                            q = 96 * j
                            while q < 96 * j + 96:
                                q1 = min(96 * j + 96, (q // P + 1) * P)
                                b = 7 * gate + BAND.index((r // P, q // P))
                                sp.dma_start(
                                    raw[r % P:r % P + r1 - r, 1, b * P + q % P:b * P + q % P + q1 - q],
                                    w[bass.ds(i * 4 + j, 1), r - 96 * j:r1 - 96 * j,
                                      q - 96 * j:q1 - 96 * j].rearrange("h r q -> (h r) q"))\
                                    .then_inc(band_in, 16)
                                n += 16
                                q = q1
                            r = r1
                sp.wait_ge(band_in, i * n + n)
                sp.sem_inc(raw_in[1], 32)
            c = FIRST["bo"]
            with sp.Fori(0, 4) as i:
                for s in range(2):
                    load1(2 * i + c + s, s, a["w_b_out"], i * 256 + P * s, RT)
            c = FIRST["wo"]
            with sp.Fori(0, 2) as i:
                for s in range(2):
                    load8(2 * i + c + s, s, a["w_o"], i * 512 + 256 * s)

            def load_mlp(c, up, down):
                with sp.Fori(0, 4) as q:
                    with sp.Fori(0, 2) as i:
                        for s in range(2):
                            load8(8 * q + 2 * i + c + s, s, up, q * Q_FF + i * 512 + 256 * s)
                    with sp.Fori(0, 2) as i:
                        for s in range(2):
                            load8(8 * q + 2 * i + c + 4 + s, s, down, i * 512 + 256 * s, q * Q_FF)

            load_mlp(FIRST["mlp0"], a["w_1"], a["w_2"])
            sp.wait_ge(*at("mlp0", "dn", 4 + 32))
            sp.dma_start(HE[:, 0:2], a["level_masks"]).then_inc(hconst_in, 16)
            sp.dma_start(reset[:], a["reset"]).then_inc(hconst_in, 16)
            c = FIRST["hg"]
            with sp.Fori(0, 4) as i:
                for n, w in enumerate(("hgrn_w_q_2", "hgrn_w_f_2", "hgrn_w_g_2", "hgrn_w_i_2")):
                    load8(4 * i + c + n, n % 2, a[w], i * 256)
            c = FIRST["hwo"]
            with sp.Fori(0, 2) as i:
                for s in range(2):
                    load8(2 * i + c + s, s, a["hgrn_w_o_2"], i * 512 + 256 * s)
            load_mlp(FIRST["mlp1"], a["mlp_w_up_2"][0], a["mlp_w_down_2"][0])
            sp.wait_ge(*at("mlp1", "dn", 4 + 32))
            sp.dma_start(cos_t[:], a["cos"]).then_inc(mconst_in, 16)
            sp.dma_start(sin_t[:], a["sin"]).then_inc(mconst_in, 16)
            sp.dma_start(swap_t[:], a["swap"]).then_inc(mconst_in, 16)
            sp.dma_start(neg_t[:], a["neg"]).then_inc(mconst_in, 16)
            c = FIRST["kvq"]
            load8(c, 0, a["kv_w_dkv_2"], 0)
            slot_free(c + 1)
            v = raw[:, 1, 0:8 * P].rearrange("p (k n) -> p k n", k=8)
            for h in range(2):
                sp.dma_start(v[:, :, h * ROPE:(h + 1) * ROPE],
                             a["kv_w_dkv_2"][:, LORA:LORA + ROPE].rearrange("(k p) n -> p k n", p=P))\
                    .then_inc(raw_in[1], 16)
            load1(c + 2, 0, a["mla_w_dq_2"], 0, 8)
            load1(c + 3, 1, a["mla_w_dq_2"], P, 8)
            c = FIRST["att"]
            with sp.Fori(0, 4) as i:
                slot_free(2 * i + c)
                for h, w in enumerate(("kv_w_uk_2", "kv_w_uv_2")):
                    sp.dma_start(raw[:, 0, h * 1024:(h + 1) * 1024].rearrange("p (k n) -> p k n", k=2),
                                 a[w][:, bass.ds(i * 512, 512)].rearrange("(k p) n -> p k n", p=P))\
                        .then_inc(raw_in[0], 16)
                slot_free(2 * i + c + 1)
                src = a["mla_w_uq_2"].rearrange("(k p) (h n) -> k p h n", p=P, n=NOPE + ROPE)
                for k in range(2):
                    sp.dma_start(raw[:, 1, k * 512:(k + 1) * 512].rearrange("p (h n) -> p h n", h=4),
                                 src[k][:, bass.ds(i * 4, 4), 0:NOPE]).then_inc(parts_in, 16)
                    sp.dma_start(raw[:, 1, 1024 + k * 256:1280 + k * 256].rearrange("p (h n) -> p h n", h=4),
                                 src[k][:, bass.ds(i * 4, 4), NOPE:NOPE + ROPE]).then_inc(parts_in, 16)
                sp.wait_ge(parts_in, i * 64 + 64)
                sp.sem_inc(raw_in[1], 32)
            c = FIRST["mwo"]
            with sp.Fori(0, 4) as i:
                for s in range(2):
                    load1(2 * i + c + s, s, a["mla_w_o_2"], i * 256 + P * s, 16)
            load_mlp(FIRST["mlp2"], a["mlp_w_up_2"][1], a["mlp_w_down_2"][1])
            for s in range(2):
                load8(N_CHUNKS + s, s, a["mlp_w_down_2"][1], 512 + 256 * s, 3 * Q_FF)
            sp.wait_ge(s_("y_out"), TB * 2)
            sp.dma_start(out.rearrange("b (t p) d -> p (b t) d", p=P), y_tm[:]).then_inc(out_done, 16)
            sp.wait_ge(out_done, 16)

        @block.gpsimd
        def _(pool):
            pool.sem_inc(lo_done, 2)

            def split_lo(c, s):
                pool.wait_ge(hi_done, c + 1)
                pool.tensor_tensor(w_lo[:, s], raw[:, s], w_hi[:, s].bitcast(F32), ALU.subtract)\
                    .then_inc(lo_done, 1)

            with pool.Fori(0, FIRST["yaband"] // 2) as i:
                for s in range(2):
                    split_lo(2 * i + s, s)
            pool.wait_ge(lo_done, 2 + FIRST["yaband"])
            pool.memset(raw[:, 1], 0.0).then_inc(band_zero, 1)
            with pool.Fori(FIRST["yaband"] // 2, N_CHUNKS // 2) as i:
                for s in range(2):
                    split_lo(2 * i + s, s)

        @block.scalar
        def _(act):
            def split_hi(c, s):
                act.wait_ge(raw_in[s], 16 * (c - s) + 32)
                act.wait_ge(halves, 2 * c + 2)
                act.activation(w_hi[:, s], raw[:, s], ACT.Copy).then_inc(hi_done, 1)

            split_hi(0, 0)
            split_hi(1, 1)
            act.wait_ge(consts_in, 48)

            for k in range(KD):
                act.wait_ge(s_("x_turned"), k + 1)
                act.activation(X[:, k], ps[:, k % 4], ACT.Copy).then_inc(s_("x_fm"), 1)
            norm_act(act, "n_mix", lambda k: (s_("x_fm"), k + 1))

            act.wait_ge(s_("lam_abs"), 2)
            act.activation(small[:, 24:36], small[:, 12:24], ACT.Exp, scale=-1.0).then_inc(s_("lam_e"), 1)

            ev = s_("z_evac")
            act.sem_inc(ev, 4)

            def columns(stage, iters, dst, func, bias, off=0):
                c = FIRST[stage]
                with act.Fori(0, iters) as i:
                    for j in range(4):
                        act.wait_ge(halves, half_at(2 * i + c + j // 2, j % 2))
                        act.activation(dst[:, bass.ds(4 * i + j, 1), off:off + T], ps[:, j:j + 1], func,
                                       bias=dcol("b_in", 4 * i + bias + j)).then_inc(ev, 1)
                        if j % 2:
                            split_hi(2 * i + c + j // 2 + 2, j // 2)

            columns("xb", 3, XBR, ACT.Identity, 2 * KD, 4)
            c = FIRST["ug"]
            with act.Fori(0, 4) as i:
                for j in range(4):
                    act.wait_ge(halves, half_at(2 * i + c + j // 2, j % 2))
                    act.activation((CO, GA)[j // 2][:, bass.ds(2 * i + j % 2, 1)], ps[:, j:j + 1],
                                   (ACT.Identity, ACT.Sigmoid)[j // 2],
                                   bias=dcol("b_in", 2 * i + KD * (j // 2) + j % 2)).then_inc(ev, 1)
                    if j % 2:
                        split_hi(2 * i + c + j // 2 + 2, j // 2)
            act.wait_ge(s_("v_done"), RT)
            columns("gb", 3, G, ACT.Identity, 28)
            columns("sb", 2, SBG, ACT.Sigmoid, 48)

            act.wait_ge(s_("mu_mm"), 1)
            act.activation(rst[:, 1], ps[:, 7], ACT.Copy, scale=1.0 / D).then_inc(s_("mu_done"), 1)
            for k in range(KD):
                act.wait_ge(s_("xc_done"), k + 1)
                if k >= 4:
                    act.wait_ge(s_("xc_add"), max(k - 4, 1))
                act.activation(tmp[:, k % 4], CO[:, k], ACT.Square).then_inc(s_("xc_sq"), 1)

            def gelu_act(g):
                for j in range(3):
                    if g:
                        act.wait_ge(s_("gb_g"), 3 * g - 2 + j)
                    act.wait_ge(ev, 4 + 28 + 3 * g + j + 1)
                    act.activation(ps[:, 4 + j], G[:, 3 * g + j], ACT.Square).then_inc(s_("gb_zz"), 1)
                for j in range(3):
                    act.wait_ge(s_("gb_p"), 3 * g + j + 1)
                    act.activation(ps[:, 4 + j], ps[:, 4 + j], ACT.Tanh, scale=0.7978845608028654)\
                        .then_inc(s_("gb_th"), 1)

            c = FIRST["sa"]
            act.wait_ge(s_("u_done"), KD)
            for i in range(2):
                for j in range(4):
                    act.wait_ge(halves, half_at(2 * i + c + j // 2, j % 2))
                    act.activation(M[:, 4 * i + j], ps[:, j], ACT.Sigmoid, bias=col("b_in", 40 + 4 * i + j))\
                        .then_inc(ev, 1)
                    if j % 2:
                        split_hi(2 * i + c + j // 2 + 2, j // 2)
                        gelu_act(2 * i + j // 2)
                if i == 0:
                    act.wait_ge(s_("var_mm"), 1)
                    act.activation(rst[:, 0], ps[:, 7], ACT.Sqrt, bias=col("eps"), scale=1.0 / D)\
                        .then_inc(s_("ln_std"), 1)

            act.wait_ge(halves, half_at(c + 3))
            for k in range(KD):
                act.wait_ge(s_("ln_y"), k + 1)
                act.activation(tmp[:, 2 + k % 2], tmp[:, k % 2], ACT.Sigmoid, bias=col("ln_b", k))\
                    .then_inc(s_("ln_sg"), 1)
                act.wait_ge(s_("ln_u"), k + 1)
                act.activation(XH[:, k], tmp[:, 2 + k % 2], ACT.Copy).then_inc(s_("uh_done"), 1)

            c = FIRST["yaband"]
            act.wait_ge(s_("ch_done"), 2)
            act.wait_ge(s_("ul_done"), KD)
            with act.Fori(0, 4) as i:
                for j in range(3):
                    act.wait_ge(halves, half_at(2 * i + c - 1))
                    act.activation(VH[:, j], V[:, bass.ds(3 * i + j, 1)], ACT.Copy).then_inc(s_("vh_done"), 1)
                split_hi(2 * i + c + 2, 0)
                for j in range(3):
                    act.wait_ge(halves, half_at(2 * i + c + 1))
                    act.wait_ge(s_("lru_done"), 3 * i + 3)
                    act.activation(LR[:, j], ps[:, j], ACT.Sigmoid, bias=dcol("b_rg_a", 3 * i + j))\
                        .then_inc(s_("lru_r"), 1)
                for j in range(3):
                    act.activation(LR[:, 3 + j], ps[:, 3 + j], ACT.Sigmoid, bias=dcol("b_rg_x", 3 * i + j))\
                        .then_inc(s_("lru_x"), 1)
                for j in range(3):
                    act.wait_ge(s_("lru_r"), 3 * i + j + 1)
                    act.activation(ps[:, j], LR[:, j], ACT.Tanh, scale=small[:, bass.ds(3 * i + 60 + j, 1)])\
                        .then_inc(s_("lru_t"), 1)
                    act.wait_ge(s_("lru_t"), 3 * i + j + 1)
                    act.activation(LR[:, j], LR[:, j], ACT.Exp, scale=small[:, bass.ds(3 * i + 24 + j, 1)])\
                        .then_inc(s_("lru_e"), 1)
                for j in range(3):
                    act.activation(ps[:, j], ps[:, j], ACT.Sqrt, scale=-1.0).then_inc(s_("lru_s"), 1)
                split_hi(2 * i + c + 3, 1)
                for j in range(3):
                    act.wait_ge(s_("vg_t"), 3 * i + j + 1)
                    act.activation(VGH[:, bass.ds(3 * i + j, 1)], G[:, bass.ds(3 * i + j, 1)], ACT.Copy)\
                        .then_inc(s_("vg_hi"), 1)

            c = FIRST["bo"]
            with act.Fori(0, 2) as i:
                for j in range(4):
                    act.wait_ge(s_("m_done"), 4 * i + j + 5)
                    act.activation(MH[:, bass.ds(4 * i + j, 1)], M[:, bass.ds(4 * i + j, 1)], ACT.Copy)\
                        .then_inc(s_("mh_done"), 1)
                    split_hi(4 * i + c + j + 2, j % 2)

            def ahead(c, n):
                with act.Fori(0, n) as i:
                    for s in range(2):
                        split_hi(2 * i + c + s + 2, s)

            ahead(FIRST["wo"], 2)

            def mlp_act(n):
                c = FIRST[n]
                with act.Fori(0, 4) as q:
                    with act.Fori(0, 2) as i:
                        for j in range(4):
                            act.wait_ge(*at(n, "t", 8 * q + 4 * i + j + 5))
                            act.activation(FH[:, bass.ds(4 * i + j, 1)], tmp[:, j % 2:j % 2 + 1], ACT.Square)\
                                .then_inc(sig(n, "fh"), 1)
                            if j % 2:
                                split_hi(8 * q + 2 * i + c + j // 2 + 2, j // 2)
                    with act.Fori(0, 2) as i:
                        for s in range(2):
                            split_hi(8 * q + 2 * i + c + 6 + s, s)

            scaled_act(act, "n_mlp0", lambda k: at("wo", "x", k + 5), "g_mlp")
            squares_act(act, "n_mlp0")
            mlp_act("mlp0")
            norm_act(act, "n_fin0", lambda k: at("mlp0", "dn", 28 + k + 1), split=False)
            norm_act(act, "n_hg", lambda k: at("n_fin0", "t", k + 1))

            act.wait_ge(s_("lb_in"), 1)
            act.activation(small[:, 88:96], small[:, 80:88], ACT.Sigmoid).then_inc(s_("lb_done"), 1)
            c = FIRST["hg"]
            act.sem_inc(s_("hv_done"), 2)
            with act.Fori(0, 4) as i:
                for n in range(2):
                    act.wait_ge(halves, half_at(4 * i + c, n))
                    act.wait_ge(s_("hq_done"), 2 * i + n + 1)
                    act.activation(HSG[:, n], ps[:, n], ACT.Sigmoid).then_inc(s_("hq_sg"), 1)
                split_hi(4 * i + c + 2, 0)
                for n in range(2):
                    act.wait_ge(halves, half_at(4 * i + c + 1, n))
                    act.wait_ge(s_("ho_done"), 2 * i + n + 1)
                    act.activation(HF[:, n], ps[:, 2 + n], ACT.Sigmoid).then_inc(s_("hf_sg"), 1)
                split_hi(4 * i + c + 3, 1)
                for n in range(2):
                    act.wait_ge(halves, half_at(4 * i + c + 2, n))
                    act.wait_ge(s_("hg_done"), 2 * i + n + 1)
                    act.activation(HSG[:, 2 + n], ps[:, n], ACT.Sigmoid).then_inc(s_("hg_sg"), 1)
                split_hi(4 * i + c + 4, 0)
                for n in range(2):
                    act.wait_ge(halves, half_at(4 * i + c + 3, n))
                    act.activation(HV[:, 2 * n:2 * n + 2], ps[:, 2 + n].rearrange("p (b v) -> p b v", b=2),
                                   ACT.Copy).then_inc(s_("hv_done"), 1)
                split_hi(4 * i + c + 5, 1)
                for n in range(2):
                    h = 2 * i + n
                    act.wait_ge(s_("hf_done"), h + 1)
                    act.activation(HF[:, n], HF[:, n], ACT.Ln).then_inc(s_("h_ln"), 1)
                    act.wait_ge(s_("h_scan"), h + 1)
                    act.activation(HEB[:], HF[:, n], ACT.Exp).then_inc(s_("h_eb"), 1)
                    act.wait_ge(s_("h_kd_arg"), h + 1)
                    act.activation(HKD[:], HKD[:], ACT.Exp).then_inc(s_("h_kd_e"), 1)
                    for l in range(len(LEVELS)):
                        act.wait_ge(s_("h_arg"), 14 * h + 2 * l + 2)
                        act.activation(HE[:, l], HE[:, l], ACT.Exp).then_inc(s_("h_e"), 1)
                    act.wait_ge(s_("h_kt"), 3 * h + 3)
                    act.activation(HKT[:], ps[:, 7, 0:384].rearrange("p (b d) -> p b d", b=3), ACT.Copy)\
                        .then_inc(s_("h_kt_c"), 1)
                    act.wait_ge(s_("h_o"), h + 1)
                    act.activation(tmp[:, 0], ps[:, 6], ACT.Square).then_inc(s_("h_sq"), 1)
                    act.wait_ge(s_("h_mean"), h + 1)
                    act.activation(rst[:, 0], ps[:, 7], ACT.Sqrt, bias=col("eps"), scale=1.0 / P).then_inc(s_("h_std"), 1)
                    act.wait_ge(s_("h_t2"), h + 1)
                    act.activation(OH[:, bass.ds(h, 1)], tmp[:, 1:2], ACT.Copy).then_inc(s_("oh_done"), 1)

            ahead(FIRST["hwo"], 2)
            scaled_act(act, "n_mlp1", lambda k: at("hwo", "x", k + 5), "mlp_norm_2")
            squares_act(act, "n_mlp1")
            mlp_act("mlp1")
            scaled_act(act, "n_kv", lambda k: at("mlp1", "dn", 28 + k + 1), "kv_in_norm_2")
            squares_act(act, "n_kv")
            scaled_act(act, "n_mla", lambda k: at("mlp1", "dn", 28 + k + 1), "mla_norm_2", 0, XH2)

            c = FIRST["kvq"]

            def small_norm_act(n):
                for k in range(2):
                    act.wait_ge(*at(n, "c", k + 1))
                    act.activation(tmp[:, k], CK[:, k], ACT.Square).then_inc(sig(n, "sq"), 1)
                act.wait_ge(*at(n, "mean", 1))
                act.activation(rst[:, 0], ps[:, 7], ACT.Sqrt, bias=col("eps"), scale=1.0 / LORA)\
                    .then_inc(sig(n, "std"), 1)

            split_hi(c + 2, 0)
            small_norm_act("ckv")
            for k in range(2):
                act.wait_ge(*at("ckv", "t", k + 1))
                act.activation(CKH[:, k], CK[:, 2 + k], ACT.Copy).then_inc(sig("ckv", "hi"), 1)
            split_hi(c + 3, 1)
            split_hi(c + 4, 0)
            split_hi(c + 5, 1)
            small_norm_act("cq")
            for k in range(2):
                act.wait_ge(*at("cq", "t", k + 1))
                act.activation(CQH[:, k], CK[:, 2 + k], ACT.Copy).then_inc(sig("cq", "hi"), 1)

            c = FIRST["att"]
            act.sem_inc(s_("a_exp"), 4)
            act.sem_inc(s_("a_ptc"), 2)
            with act.Fori(0, 4) as i:
                for h in range(4):
                    act.wait_ge(halves, half_at(2 * i + c, 0))
                    act.activation(KN[:, h], ps[:, h], ACT.Copy).then_inc(s_("kn_done"), 1)
                for b in range(TB):
                    act.wait_ge(halves, half_at(2 * i + c, 1))
                    act.activation(VT[:, b], ps[:, 4 + b], ACT.Copy).then_inc(s_("vt_done"), 1)
                split_hi(2 * i + c + 2, 0)
                for h in range(4):
                    act.wait_ge(halves, half_at(2 * i + c + 1, 0))
                    act.activation(QN[:, h], ps[:, h], ACT.Copy).then_inc(s_("qn_done"), 1)
                for h in range(2):
                    act.wait_ge(halves, half_at(2 * i + c + 1, 1))
                    act.activation(QR[:, 2 + h], ps[:, 4 + h], ACT.Copy).then_inc(s_("qr_raw"), 1)
                split_hi(2 * i + c + 3, 1)

                def exps(h):
                    for b in range(TB):
                        act.wait_ge(s_("a_nmax"), 16 * i + 4 * h + b + 1)
                        act.wait_ge(s_("a_pt"), 16 * i + 4 * h + b + 1)
                        act.activation(PM[:, b, 0:(b + 1) * P], ps[:, b, 0:(b + 1) * P], ACT.Exp,
                                       bias=small[:, 100 + b:101 + b], scale=SCALE,
                                       accum_out=small[:, 104 + b:105 + b]).then_inc(s_("a_exp"), 1)

                def turned(h):
                    for b in range(TB):
                        act.wait_ge(s_("a_pt"), 16 * i + 4 * h + b + 5)
                        act.wait_ge(s_("a_pv"), 4 * i + h + 1)
                        act.activation(PT[:, 0:b + 1, b * P:(b + 1) * P],
                                       ps[:, 4 + b % 2, 0:(b + 1) * P].rearrange("p (j q) -> p j q", q=P),
                                       ACT.Copy).then_inc(s_("a_ptc"), 1)

                def out_hi(h):
                    act.wait_ge(s_("a_pv"), 4 * i + h + 2)
                    act.activation(AH[:, bass.ds(4 * i + h, 1)], ps[:, 6:7], ACT.Copy).then_inc(s_("ah_done"), 1)

                for h in range(4):
                    exps(h)
                    turned(h)
                    out_hi(h)

            ahead(FIRST["mwo"], 4)
            scaled_act(act, "n_mlp2", lambda k: at("mwo", "x", k + 5), "mlp_norm_2", 8, XH2)
            squares_act(act, "n_mlp2")
            mlp_act("mlp2")
            norm_act(act, "n_fin1", lambda k: at("mlp2", "dn", 28 + k + 1), split=False)
            for g in range(TB * 2):
                act.wait_ge(s_("y_turned"), g + 1)
                act.activation(y_tm[:, g // 2, (g % 2) * 512:(g % 2) * 512 + 512], ps[:, g % 4], ACT.Copy)\
                    .then_inc(s_("y_out"), 1)

        @block.vector
        def _(dve):
            dve.memset(XBR[:, :, 0:4], 0.0).then_inc(s_("pads"), 1)
            dve.wait_ge(consts_in, 48)
            lam = Count(dve, "lam_abs")
            nl, ab, e, sm = small[:, 0:12], small[:, 12:24], small[:, 24:36], small[:, 36:48]
            zz, rr, ch = small[:, 48:60], small[:, 72:84], small[:, 60:72]
            lam.put(dve.tensor_scalar(nl, col("lam", 0, 12), -1.0, None, ALU.mult))
            lam.wait()
            lam.put(dve.tensor_tensor(ab, nl, col("lam", 0, 12), ALU.max))
            norm_dve(dve, "n_mix", "g_mix")

            lc = Count(dve, "lam_chain")
            dve.wait_ge(s_("lam_e"), 1)
            lc.put(dve.tensor_scalar(sm, e, 2.0, None, ALU.add))
            lc.wait()
            lc.put(dve.reciprocal(rr, sm))
            lc.wait()
            lc.put(dve.tensor_tensor(zz, e, rr, ALU.mult))
            lc.wait()
            lc.put(dve.tensor_tensor(sm, zz, zz, ALU.mult))
            lc.wait()
            lc.put(dve.tensor_scalar(rr, sm, 1.0 / 17, None, ALU.mult))
            for n in range(15, 1, -2):
                lc.wait()
                lc.put(dve.scalar_tensor_tensor(rr, rr, 1.0 / n, sm, ALU.add, ALU.mult))
            lc.wait()
            lc.put(dve.scalar_tensor_tensor(rr, rr, 1.0, zz, ALU.add, ALU.mult))
            lc.put(dve.tensor_scalar(nl, nl, 0.0, -4.0, ALU.max, ALU.mult))
            lc.wait()
            dve.scalar_tensor_tensor(ch, rr, -8.0, nl, ALU.mult, ALU.add).then_inc(s_("ch_done"), 1)
            dve.wait_ge(s_("ch_done"), 1)
            dve.tensor_scalar(e, ch, 2.0, None, ALU.mult).then_inc(s_("ch_done"), 1)

            dve.wait_ge(s_("pads"), 1)
            ev = s_("z_evac")
            with dve.Fori(0, 3) as i:
                for k in range(TAPS_B):
                    for j in range(4):
                        t = 4 * i + j
                        src = XBR[:, bass.ds(t, 1), 1 + k:1 + k + T]
                        w = dcol("conv_b_w", t * 4 + k)
                        acc = V[:, bass.ds(t, 1)]
                        part = s_("v_part")
                        if k == 0:
                            dve.wait_ge(ev, t + 5)
                            dve.tensor_scalar(acc, src, w, dcol("conv_b_b", t), ALU.mult, ALU.add).then_inc(part, 1)
                        else:
                            dve.wait_ge(part, 12 * i + 4 * (k - 1) + j + 1)
                            dve.scalar_tensor_tensor(acc, src, w, acc, ALU.mult, ALU.add)\
                                .then_inc(part if k < TAPS_B - 1 else s_("v_done"), 1)

            dve.wait_ge(*at("n_mix", "lo", KD))
            dve.memset(UP[:, :, 0:PAD], 0.0).then_inc(s_("pads"), 1)
            dve.wait_ge(s_("pads"), 2)
            cs = s_("conv")
            with dve.Fori(0, 4) as i:
                for n in range(2):
                    t = bass.ds(2 * i + n, 1)
                    dve.wait_ge(ev, 4 * i + RT + 7 + n)
                    dve.tensor_tensor(UP[:, n:n + 1, PAD:PAD + T], CO[:, t], GA[:, t], ALU.mult).then_inc(s_("u_done"), 1)
                base = i * (2 * TAPS_A + 2)
                for tap in range(TAPS_A):
                    for n in range(2):
                        acc = CO[:, bass.ds(2 * i + n, 1)] if tap % 2 == 0 else tmp[:, n:n + 1]
                        src = UP[:, n:n + 1, tap:tap + T]
                        w = dcol("conv_a_w", (2 * i + n) * TAPS_A + tap)
                        if tap == 0:
                            dve.wait_ge(s_("u_done"), 2 * i + n + 1)
                            dve.tensor_scalar(acc, src, w, dcol("conv_a_b", 2 * i + n), ALU.mult, ALU.add).then_inc(cs, 1)
                        elif tap == 1:
                            dve.tensor_scalar(acc, src, w, None, ALU.mult).then_inc(cs, 1)
                        else:
                            dve.wait_ge(cs, base + 2 * (tap - 2) + n + 1)
                            dve.scalar_tensor_tensor(acc, src, w, acc, ALU.mult, ALU.add).then_inc(cs, 1)
                for n in range(2):
                    t = bass.ds(2 * i + n, 1)
                    dve.wait_ge(cs, base + 2 * (TAPS_A - 1) + n + 1)
                    dve.tensor_tensor(CO[:, t], CO[:, t], tmp[:, n:n + 1], ALU.add).then_inc(cs, 1)
                dve.wait_ge(cs, base + 2 * TAPS_A + 2)

            dve.wait_ge(s_("mu_done"), 1)
            for k in range(KD):
                dve.tensor_tensor(CO[:, k], CO[:, k], rst[:, 1], ALU.subtract).then_inc(s_("xc_done"), 1)
            for k in range(1, KD):
                dve.wait_ge(s_("xc_sq"), k + 1)
                if k >= 2:
                    dve.wait_ge(s_("xc_add"), k - 1)
                dve.tensor_tensor(rst[:, 0], rst[:, 0] if k >= 2 else tmp[:, 0], tmp[:, k % 4], ALU.add)\
                    .then_inc(s_("xc_add"), 1)

            for g in range(RT // 3):
                for j in range(3):
                    w = ps[:, 4 + j]
                    dve.wait_ge(s_("gb_zz"), 3 * g + j + 1)
                    dve.tensor_scalar(w, w, 0.044715, 1.0, ALU.mult, ALU.add).then_inc(s_("gb_q"), 1)
                for j in range(3):
                    w = ps[:, 4 + j]
                    dve.wait_ge(s_("gb_q"), 3 * g + j + 1)
                    dve.tensor_tensor(w, w, G[:, 3 * g + j], ALU.mult).then_inc(s_("gb_p"), 1)
                for j in range(3):
                    dve.wait_ge(s_("gb_th"), 3 * g + j + 1)
                    dve.scalar_tensor_tensor(G[:, 3 * g + j], ps[:, 4 + j], 1.0, G[:, 3 * g + j], ALU.add, ALU.mult)\
                        .then_inc(s_("gb_g"), 1)
                if g == 1:
                    dve.wait_ge(s_("ln_std"), 1)
                    dve.reciprocal(rst[:, 1], rst[:, 0]).then_inc(s_("ln_inv"), 1)
            dve.wait_ge(s_("ln_inv"), 1)

            for k in range(KD + 1):
                if k < KD:
                    if k >= 2:
                        dve.wait_ge(s_("ln_u"), k - 1)
                    dve.scalar_tensor_tensor(tmp[:, k % 2], CO[:, k], col("ln_g", k), rst[:, 1], ALU.mult, ALU.mult)\
                        .then_inc(s_("ln_y"), 1)
                if k >= 1:
                    dve.wait_ge(s_("uh_done"), k)
                    dve.tensor_tensor(XL[:, k - 1], tmp[:, 2 + (k - 1) % 2], XH[:, k - 1].bitcast(F32), ALU.subtract)\
                        .then_inc(s_("ul_done"), 1)
                if k < KD:
                    dve.wait_ge(s_("ln_sg"), k + 1)
                    if k >= 2:
                        dve.wait_ge(s_("ul_done"), k - 1)
                    dve.scalar_tensor_tensor(tmp[:, 2 + k % 2], tmp[:, k % 2], col("ln_b", k), tmp[:, 2 + k % 2],
                                             ALU.add, ALU.mult).then_inc(s_("ln_u"), 1)

            c = FIRST["yaband"]
            dve.wait_ge(s_("ul_done"), KD)
            dve.sem_inc(s_("lru_done"), 3)
            dve.sem_inc(s_("ma_done"), 2)
            with dve.Fori(0, 4) as i:
                tiles = [(j, bass.ds(3 * i + j, 1), 3 * i + j + 1) for j in range(3)]
                for j, t, n in tiles:
                    dve.wait_ge(s_("vh_done"), n)
                    dve.tensor_tensor(VL[:, j:j + 1], V[:, t], VH[:, j:j + 1].bitcast(F32), ALU.subtract)\
                        .then_inc(s_("vl_done"), 1)
                for j in range(2):
                    dve.wait_ge(halves, half_at(2 * i + c, j))
                    m = M[:, bass.ds(2 * i + j, 1)]
                    dve.tensor_tensor(m, m, ps[:, 6 + j:7 + j], ALU.mult).then_inc(s_("ma_done"), 1)
                for j, t, n in tiles:
                    dve.wait_ge(s_("lru_x"), n)
                    dve.tensor_tensor(LR[:, 3 + j:4 + j], LR[:, 3 + j:4 + j], V[:, t], ALU.mult).then_inc(s_("lru_iv"), 1)
                for j, t, n in tiles:
                    dve.wait_ge(s_("lru_e"), n)
                    dve.wait_ge(s_("lru_s"), n)
                    dve.scalar_tensor_tensor(ps[:, j], LR[:, j], 1.0, ps[:, j], ALU.add, ALU.mult).then_inc(s_("lru_m"), 1)
                for j, t, n in tiles:
                    dve.wait_ge(s_("lru_m"), n)
                    dve.memset(ps[:, j, 0:1], 1.0).then_inc(s_("lru_m1"), 1)
                for j, t, n in tiles:
                    dve.wait_ge(s_("lru_m1"), n)
                    dve.wait_ge(s_("lru_iv"), n)
                    dve.tensor_tensor(LR[:, 3 + j], LR[:, 3 + j], ps[:, j], ALU.mult).then_inc(s_("lru_b"), 1)
                for j, t, n in tiles:
                    dve.wait_ge(s_("lru_b"), n)
                    dve.wait_ge(s_("vl_done"), n)
                    dve.tensor_tensor_scan(V[:, t].rearrange("p a t -> p (a t)"), LR[:, j], LR[:, 3 + j], 0.0,
                                           ALU.mult, ALU.add).then_inc(s_("lru_done"), 1)
                for j, t, n in tiles:
                    dve.wait_ge(s_("lru_done"), 3 * i + j + 4)
                    dve.scalar_tensor_tensor(G[:, t], G[:, t], 0.5, V[:, t], ALU.mult, ALU.mult).then_inc(s_("vg_t"), 1)
                for j, t, n in tiles:
                    dve.wait_ge(s_("vg_hi"), n)
                    dve.tensor_tensor(VGL[:, t], G[:, t], VGH[:, t].bitcast(F32), ALU.subtract).then_inc(s_("vg_lo"), 1)

            dve.wait_ge(s_("vg_lo"), RT)
            dve.sem_inc(s_("m_done"), 4)
            dve.sem_inc(s_("yb_evac"), 4)
            c = FIRST["bo"]
            with dve.Fori(0, 2) as i:
                for j in range(4):
                    t = bass.ds(4 * i + j, 1)
                    dve.wait_ge(halves, half_at(4 * i + c + j))
                    dve.tensor_tensor(SBG[:, t], ps[:, BO_BANKS[j]:BO_BANKS[j] + 1], SBG[:, t], ALU.mult)\
                        .then_inc(s_("yb_evac"), 1)
                    dve.wait_ge(s_("yb_evac"), 4 * i + j + 5)
                    dve.tensor_tensor(M[:, t], M[:, t], SBG[:, t], ALU.add).then_inc(s_("m_done"), 1)
                    dve.wait_ge(s_("mh_done"), 4 * i + j + 1)
                    dve.tensor_tensor(ML[:, t], M[:, t], MH[:, t].bitcast(F32), ALU.subtract).then_inc(s_("ml_done"), 1)

            def residual(n, c, per, banks_free):
                xs = sig(n, "x")
                dve.wait_ge(*banks_free)
                dve.sem_inc(xs, 4)
                with dve.Fori(0, 2) as i:
                    for j in range(4):
                        dve.wait_ge(halves, half_at(2 * i + c + j // 2, j % 2) if per == 2 else half_at(4 * i + c + j))
                        dve.tensor_tensor(X[:, bass.ds(4 * i + j, 1)], X[:, bass.ds(4 * i + j, 1)], ps[:, j:j + 1], ALU.add)\
                            .then_inc(xs, 1)

            def mlp_dve(n):
                c = FIRST[n]
                with dve.Fori(0, 4) as q:
                    with dve.Fori(0, 2) as i:
                        for j in range(4):
                            f = 8 * q + 4 * i + j
                            t, t2 = tmp[:, j % 2:j % 2 + 1], tmp[:, 2 + j % 2:3 + j % 2]
                            dve.wait_ge(halves, half_at(8 * q + 2 * i + c + j // 2, j % 2))
                            dve.wait_ge(*at(n, "fl", f + 3))
                            dve.scalar_tensor_tensor(t, ps[:, j:j + 1], 0.0, rst[:, 1:2], ALU.max, ALU.mult)\
                                .then_inc(sig(n, "t"), 1)
                            dve.wait_ge(*at(n, "t", f + 5))
                            dve.tensor_tensor(t2, t, t, ALU.mult).then_inc(sig(n, "sq"), 1)
                            dve.wait_ge(*at(n, "sq", f + 1))
                            dve.wait_ge(*at(n, "fh", f + 1))
                            dve.tensor_tensor(FL[:, bass.ds(4 * i + j, 1)], t2, FH[:, bass.ds(4 * i + j, 1)].bitcast(F32),
                                              ALU.subtract).then_inc(sig(n, "fl"), 1)
                    with dve.Fori(0, 2) as i:
                        for j in range(4):
                            dve.wait_ge(halves, half_at(8 * q + 2 * i + c + 4 + j // 2, j % 2))
                            dve.tensor_tensor(X[:, bass.ds(4 * i + j, 1)], X[:, bass.ds(4 * i + j, 1)], ps[:, j:j + 1],
                                              ALU.add).then_inc(sig(n, "dn"), 1)

            def scaled(n, gain, off=0, xh=XH, xl=XL):
                m = n[2:]
                dve.sem_inc(sig(m, "fl"), 4)
                dve.sem_inc(sig(m, "dn"), 4)
                dve.sem_inc(sig(m, "t"), 4)
                scaled_dve(dve, n, gain, off, xh, xl)
                squares_dve(dve, n)

            residual("wo", FIRST["wo"], 2, (s_("yb_evac"), 4 + KD))
            scaled("n_mlp0", "g_mlp")
            mlp_dve("mlp0")
            norm_dve(dve, "n_fin0", "g_final", split=False)
            norm_dve(dve, "n_hg", "hgrn_norm_2")

            dve.tensor_tensor(small[:, 80:88], col("hgrn_lb_logits_2", 0, 8), col("hgrn_lb_logits_2", 8, 8), ALU.subtract)\
                .then_inc(s_("lb_in"), 1)
            dve.wait_ge(s_("lb_done"), 1)
            dve.tensor_scalar(small[:, 112:120], small[:, 88:96], -1.0, 1.0, ALU.mult, ALU.add).then_inc(s_("lb_1m"), 1)
            dve.memset(HP[:], 0.0).then_inc(s_("h_p0"), 1)
            dve.wait_ge(s_("lb_1m"), 1)
            dve.wait_ge(s_("h_p0"), 1)
            dve.wait_ge(hconst_in, 32)
            dve.tensor_copy(masks[:].rearrange("p l t -> p (l t)"), HE[:, 0:2].rearrange("p l t -> p (l t)"))\
                .then_inc(s_("masks_done"), 1)
            dve.wait_ge(s_("masks_done"), 1)
            dve.sem_inc(s_("hq_done"), 2)
            dve.sem_inc(s_("hg_done"), 2)
            dve.sem_inc(s_("ho_done"), 2)
            dve.sem_inc(s_("h_g_free"), 2)
            c = FIRST["hg"]
            with dve.Fori(0, 4) as i:
                for n in range(2):
                    dve.wait_ge(s_("hq_sg"), 2 * i + n + 1)
                    dve.tensor_tensor(HQ[:, n], ps[:, n], HSG[:, n], ALU.mult).then_inc(s_("hq_done"), 1)
                hc = s_("h_f")
                for n in range(2):
                    h = 2 * i + n
                    dve.wait_ge(s_("hf_sg"), h + 1)
                    dve.tensor_scalar(HF[:, n], HF[:, n], small[:, bass.ds(h + 112, 1)], small[:, bass.ds(h + 88, 1)],
                                      ALU.mult, ALU.add).then_inc(hc, 1)
                    dve.wait_ge(hc, 2 * h + 1)
                    dve.tensor_scalar(HK[:, n], HF[:, n], -1.0, 1.0, ALU.mult, ALU.add).then_inc(hc, 1)
                    dve.wait_ge(hc, 2 * h + 2)
                    dve.tensor_scalar(HF[:, n], HF[:, n], 2.0 ** -64, None, ALU.max).then_inc(s_("hf_done"), 1)
                for n in range(2):
                    dve.wait_ge(s_("hg_sg"), 2 * i + n + 1)
                    dve.tensor_tensor(HGATE[:, n], ps[:, n], HSG[:, 2 + n], ALU.mult).then_inc(s_("hg_done"), 1)
                for n in range(2):
                    h = 2 * i + n
                    b = HF[:, n]
                    dve.wait_ge(s_("h_ln"), h + 1)
                    dve.tensor_tensor_scan(b, reset[:], b, 0.0, ALU.mult, ALU.add).then_inc(s_("h_scan"), 1)
                    dve.wait_ge(s_("h_scan"), h + 1)
                    b4 = b.rearrange("p (c t) -> p c t", t=P)
                    last = b4[:, :, P - 1:P].to_broadcast([P, TB, P])
                    dve.tensor_tensor(HKD[:].rearrange("p (c t) -> p c t", t=P), last, b4, ALU.subtract)\
                        .then_inc(s_("h_kd_arg"), 1)
                    for l, m in enumerate(LEVELS):
                        bv = b.rearrange("p (g u t) -> p g u t", u=2, t=m)
                        ev = HE[:, l].rearrange("p (g u t) -> p g u t", u=2, t=m)
                        ref = bv[:, :, 0, m - 1:m].to_broadcast([P, T // (2 * m), m])
                        dve.tensor_tensor(ev[:, :, 0], ref, bv[:, :, 0], ALU.subtract).then_inc(s_("h_arg"), 1)
                        dve.tensor_tensor(ev[:, :, 1], bv[:, :, 1], ref, ALU.subtract).then_inc(s_("h_arg"), 1)
                    dve.wait_ge(s_("h_eb"), h + 1)
                    dve.tensor_tensor(HQD[:], HQ[:, n], HEB[:], ALU.mult).then_inc(s_("h_qd"), 1)
                    dve.wait_ge(s_("h_kd_e"), h + 1)
                    dve.tensor_tensor(HKD[:], HKD[:], HK[:, n], ALU.mult).then_inc(s_("h_kd"), 1)
                    for l, m in enumerate(LEVELS):
                        ev = HE[:, l].rearrange("p (g u t) -> p g u t", u=2, t=m)
                        qv = HQ[:, n].rearrange("p (g u t) -> p g u t", u=2, t=m)
                        kv = HK[:, n].rearrange("p (g u t) -> p g u t", u=2, t=m)
                        dve.wait_ge(s_("h_e"), 7 * h + l + 1)
                        dve.tensor_tensor(ev[:, :, 0], ev[:, :, 0], kv[:, :, 0], ALU.mult).then_inc(s_("h_qk"), 1)
                        dve.tensor_tensor(ev[:, :, 1], ev[:, :, 1], qv[:, :, 1], ALU.mult).then_inc(s_("h_qk"), 1)
                    for l in range(len(LEVELS) + 1):
                        dve.wait_ge(s_("h_g"), 8 * h + l + 1)
                        if l:
                            dve.wait_ge(s_("h_g_free"), 8 * h + l + 2)
                        dve.sem_inc(s_("h_g_seen"), 1)
                        dve.copy_predicated(HP[:].rearrange("p (c t) -> p c t", t=P),
                                            masks[:, l:l + 1].to_broadcast([P, TB, P]),
                                            ps[:, 4 + l % 2].rearrange("p (c t) -> p c t", t=P)).then_inc(s_("h_g_free"), 1)
                    for b_ in range(3):
                        dve.wait_ge(s_("h_st"), 3 * h + b_ + 1)
                        dst = HS[:, b_]
                        if b_ == 0:
                            dve.tensor_copy(dst, ps[:, 7, 384:512]).then_inc(s_("h_s"), 1)
                        else:
                            dve.wait_ge(s_("h_s"), 3 * h + b_)
                            dve.scalar_tensor_tensor(dst, HS[:, b_ - 1], HEB[:, b_ * P + P - 1:b_ * P + P], ps[:, 7, 384:512],
                                                     ALU.mult, ALU.add).then_inc(s_("h_s"), 1)
                    dve.wait_ge(s_("h_std"), h + 1)
                    dve.reciprocal(rst[:, 1], rst[:, 0]).then_inc(s_("h_inv"), 1)
                    dve.wait_ge(s_("h_inv"), h + 1)
                    dve.scalar_tensor_tensor(tmp[:, 1], ps[:, 6], col("hgrn_g_norm_2"), rst[:, 1], ALU.mult, ALU.mult)\
                        .then_inc(s_("h_t1"), 1)
                    dve.wait_ge(s_("h_t1"), h + 1)
                    dve.tensor_tensor(tmp[:, 1], tmp[:, 1], HGATE[:, n], ALU.mult).then_inc(s_("h_t2"), 1)
                    dve.wait_ge(s_("oh_done"), h + 1)
                    dve.tensor_tensor(OL[:, bass.ds(h, 1)], tmp[:, 1:2], OH[:, bass.ds(h, 1)].bitcast(F32), ALU.subtract)\
                        .then_inc(s_("ho_done"), 1)

            residual("hwo", FIRST["hwo"], 2, (s_("ho_done"), 2 + HEADS_H))
            scaled("n_mlp1", "mlp_norm_2")
            mlp_dve("mlp1")
            scaled_dve(dve, "n_kv", "kv_in_norm_2")
            squares_dve(dve, "n_kv")
            scaled_dve(dve, "n_mla", "mla_norm_2", 0, XH2, XL2)

            def small_copy(n, ready):
                for k in range(2):
                    dve.wait_ge(halves, ready[k])
                    dve.tensor_tensor(CK[:, k], ps[:, k], rst[:, 1], ALU.mult).then_inc(sig(n, "c"), 1)

            def small_norm_dve(n, gain, hi, lo, inv):
                dve.wait_ge(*at(n, "std", 1))
                dve.reciprocal(inv, rst[:, 0]).then_inc(sig(n, "inv"), 1)
                dve.wait_ge(*at(n, "inv", 1))
                for k in range(2):
                    dve.scalar_tensor_tensor(CK[:, 2 + k], CK[:, k], col(gain, k), inv, ALU.mult, ALU.mult)\
                        .then_inc(sig(n, "t"), 1)
                for k in range(2):
                    dve.wait_ge(*at(n, "hi", k + 1))
                    dve.tensor_tensor(lo[:, k], CK[:, 2 + k], hi[:, k].bitcast(F32), ALU.subtract).then_inc(sig(n, "lo"), 1)

            c = FIRST["kvq"]
            small_copy("ckv", [half_at(c, 0), half_at(c, 1)])
            dve.wait_ge(halves, half_at(c + 1))
            dve.tensor_tensor(QR[:, 2], ps[:, 2], rst[:, 1], ALU.mult).then_inc(s_("kr_raw"), 1)
            small_norm_dve("ckv", "kv_norm_2", CKH, CKL, tmp[:, 0])
            dve.wait_ge(mconst_in, 64)
            dve.wait_ge(s_("kr_raw"), 1)
            dve.wait_ge(*at("ckv", "lo", 2))
            kc = Count(dve, "kr_chain")
            dve.wait_ge(s_("kr_swap"), 1)
            kc.put(dve.tensor_tensor(tmp[:, 2], ps[:, 3], sin_t[:], ALU.mult))
            kc.put(dve.tensor_tensor(KR[:], QR[:, 2], cos_t[:], ALU.mult))
            kc.wait()
            kc.put(dve.tensor_tensor(KR[:], KR[:], tmp[:, 2], ALU.add))
            kc.wait()
            small_copy("cq", [half_at(c + 2), half_at(c + 3)])
            dve.wait_ge(*at("cq", "c", 2))
            small_norm_dve("cq", "mla_q_norm_2", CQH, CQL, rst[:, 1])

            dve.wait_ge(*at("cq", "lo", 2))
            dve.sem_inc(s_("al_done"), 1)
            with dve.Fori(0, 4) as i:
                for h in range(2):
                    dve.wait_ge(s_("qr_raw"), 2 * i + h + 1)
                    dve.wait_ge(s_("qr_swap"), 2 * i + h + 1)
                    dve.tensor_tensor(rst[:, 0], ps[:, 6 + h], sin_t[:], ALU.mult).then_inc(s_("qr_a"), 1)
                    dve.tensor_tensor(QR[:, h], QR[:, 2 + h], cos_t[:], ALU.mult).then_inc(s_("qr_a"), 1)
                    dve.wait_ge(s_("qr_a"), 4 * i + 2 * h + 2)
                    dve.tensor_tensor(QR[:, h], QR[:, h], rst[:, 0], ALU.add).then_inc(s_("qr_done"), 1)
                    dve.wait_ge(s_("qr_done"), 2 * i + h + 1)

                def row_max(h):
                    for b in range(TB):
                        t = 16 * i + 4 * h + b
                        dg = ps[:, b, b * P:(b + 1) * P]
                        dve.wait_ge(s_("a_qk"), t + 1)
                        dve.tensor_tensor(dg, dg, neg_t[:], ALU.add).then_inc(s_("a_mask"), 1)
                        dve.wait_ge(s_("a_mask"), t + 1)
                        dve.tensor_reduce(small[:, 96 + b:97 + b], ps[:, b, 0:(b + 1) * P], AX, ALU.max)\
                            .then_inc(s_("a_max"), 1)
                        dve.wait_ge(s_("a_max"), t + 1)
                        dve.tensor_scalar(small[:, 100 + b:101 + b], small[:, 96 + b:97 + b], -SCALE, None, ALU.mult)\
                            .then_inc(s_("a_nmax"), 1)

                def scale_rows(h):
                    for b in range(TB):
                        t = 16 * i + 4 * h + b
                        dve.wait_ge(s_("a_exp"), t + 5)
                        dve.reciprocal(small[:, 108 + b:109 + b], small[:, 104 + b:105 + b]).then_inc(s_("a_rs"), 1)
                        dve.wait_ge(s_("a_rs"), t + 1)
                        dve.tensor_scalar(PM[:, b, 0:(b + 1) * P], PM[:, b, 0:(b + 1) * P], small[:, 108 + b:109 + b], None,
                                          ALU.mult).then_inc(s_("a_pm"), 1)

                row_max(0)
                for h in range(4):
                    scale_rows(h)
                    if h < 3:
                        row_max(h + 1)
                    dve.wait_ge(s_("ah_done"), 4 * i + h + 1)
                    dve.tensor_tensor(AL[:, bass.ds(4 * i + h, 1)], ps[:, 6:7], AH[:, bass.ds(4 * i + h, 1)].bitcast(F32),
                                      ALU.subtract).then_inc(s_("al_done"), 1)

            residual("mwo", FIRST["mwo"], 1, (s_("al_done"), 1 + HEADS_M))
            scaled("n_mlp2", "mlp_norm_2", 8, XH2, XL2)
            mlp_dve("mlp2")
            norm_dve(dve, "n_fin1", "final_norm_2", split=False)

        @block.tensor
        def _(pe):
            pe.sem_inc(halves, 4)
            pe.wait_ge(consts_in, 48)
            pe.wait_ge(x_in, 16)
            for k in range(KD):
                if k >= 4:
                    pe.wait_ge(s_("x_fm"), k - 3)
                for b in range(TB):
                    mm = pe.transpose(ps[:, k % 4, b * P:(b + 1) * P], x_tm[:, b, k * P:(k + 1) * P], ident[:])
                mm.then_inc(s_("x_turned"), 1)

            def product(dst, his, los, xh, xl, start=True, stop=True):
                n = len(his)
                for k in range(n):
                    pe.matmul(dst, his[k], xh[k], start=start and k == 0, stop=False)
                    pe.matmul(dst, his[k], xl[k], start=False, stop=False)
                    mm = pe.matmul(dst, los[k], xh[k], start=False, stop=stop and k == n - 1)
                return mm

            def product_x(dst, his, los, xh, xl, start=True, stop=True):
                n = len(his)
                for k in range(n):
                    pe.matmul(dst, xh[k], his[k], start=start and k == 0, stop=False)
                    pe.matmul(dst, xh[k], los[k], start=False, stop=False)
                    mm = pe.matmul(dst, xl[k], his[k], start=False, stop=stop and k == n - 1)
                return mm

            def tiles(t, n=KD, first=0):
                return [t[:, first + k] for k in range(n)]

            def chunk_in(c):
                pe.wait_ge(lo_done, c + 3)

            def half8(s, n, bank, xh, xl):
                product(ps[:, bank], w8(w_hi, s, n), w8(w_lo, s, n), tiles(xh), tiles(xl)).then_inc(halves, 1)

            def pair(s, bank, xh, xl, ready=None):
                h = [w8(w_hi, s, n) for n in range(2)]
                l = [w8(w_lo, s, n) for n in range(2)]
                for k in range(KD):
                    if ready is not None:
                        pe.wait_ge(*ready(k))
                    for n in range(2):
                        dst = ps[:, bank + n]
                        pe.matmul(dst, h[n][k], xh[:, k], start=k == 0, stop=False)
                        pe.matmul(dst, h[n][k], xl[:, k], start=False, stop=False)
                        mm = pe.matmul(dst, l[n][k], xh[:, k], start=False, stop=k == KD - 1)
                        if k == KD - 1:
                            mm.then_inc(halves, 1)

            norm_pe(pe, "n_mix")

            def plain(c, iters, ev, xh, xl, ready=None):
                with pe.Fori(0, iters) as i:
                    for j in range(2):
                        chunk_in(2 * i + c + j)
                        pe.wait_ge(*ev(4 * i + 2 * j + 2))
                        if j == 0 and ready is not None:
                            pair(0, 0, xh, xl, ready)
                        else:
                            half8(j, 0, 2 * j, xh, xl)
                            half8(j, 1, 2 * j + 1, xh, xl)

            def z_bank(first):
                return lambda v: (s_("z_evac"), v + first)

            plain(FIRST["xb"], 3, z_bank(0), XH, XL, lambda k: at("n_mix", "lo", k + 1))
            plain(FIRST["ug"], 4, z_bank(12), XH, XL)
            plain(FIRST["gb"], 3, z_bank(28), XH, XL)
            plain(FIRST["sb"], 2, z_bank(40), XH, XL)

            pe.wait_ge(s_("conv"), KD * (TAPS_A + 1))
            for k in range(KD):
                mm = pe.matmul(ps[:, 7], ones[:], CO[:, k], start=k == 0, stop=k == KD - 1)
            mm.then_inc(s_("mu_mm"), 1)
            c = FIRST["sa"]
            for i in range(2):
                for j in range(2):
                    chunk_in(2 * i + c + j)
                    pe.wait_ge(s_("z_evac"), 48 + 4 * i + 2 * j + 2)
                    half8(j, 0, 2 * j, XH, XL)
                    half8(j, 1, 2 * j + 1, XH, XL)
                if i == 0:
                    pe.wait_ge(s_("xc_add"), KD - 1)
                    pe.matmul(ps[:, 7], ones[:], rst[:, 0], start=True, stop=True).then_inc(s_("var_mm"), 1)

            c = FIRST["yaband"]
            pe.wait_ge(s_("ln_std"), 1)
            pe.wait_ge(s_("z_evac"), 4 + 56)
            pe.wait_ge(s_("gb_g"), RT)
            with pe.Fori(0, 4) as i:
                chunk_in(2 * i + c)
                pe.wait_ge(s_("ma_done"), 2 * i + 2)
                pair(0, 6, XH, XL, lambda k: (s_("ul_done"), k + 1))
                chunk_in(2 * i + c + 1)
                pe.wait_ge(s_("vl_done"), 3 * i + 3)
                pe.wait_ge(s_("lru_done"), 3 * i + 3)
                for gate in range(2):
                    for o in range(3):
                        ks = [n for n, (r, q) in enumerate(BAND) if q == o]
                        wt = [[t[:, 1, (7 * gate + n) * P:(7 * gate + n + 1) * P] for n in ks] for t in (w_hi, w_lo)]
                        mm = product(ps[:, 3 * gate + o], wt[0], wt[1],
                                     [VH[:, BAND[n][0]] for n in ks], [VL[:, BAND[n][0]] for n in ks])
                    mm.then_inc(halves, 1)

            def single(c, kt, ev, xh, xl, banks=(0, 1, 2, 3), ready=None):
                with pe.Fori(0, 2) as i:
                    for j in range(4):
                        chunk_in(4 * i + c + j)
                        pe.wait_ge(*ev(4 * i + j + 1))
                        h, l = w1(w_hi, j % 2, kt), w1(w_lo, j % 2, kt)
                        for k in range(kt):
                            if ready is not None and j == 0:
                                pe.wait_ge(*ready(k))
                            mm = product(ps[:, banks[j]], h[k:k + 1], l[k:k + 1], [xh[:, k]], [xl[:, k]],
                                         start=k == 0, stop=k == kt - 1)
                            if k in (kt // 2 - 1, kt - 1):
                                mm.then_inc(halves, 1)

            pe.wait_ge(s_("ma_done"), 2 + KD)
            single(FIRST["bo"], RT, lambda v: (s_("yb_evac"), v), VGH, VGL, BO_BANKS, lambda k: (s_("vg_lo"), k + 1))
            plain(FIRST["wo"], 2, lambda v: at("wo", "x", v), MH, ML, lambda k: (s_("ml_done"), k + 1))

            def mlp_pe(n, xh, xl):
                c = FIRST[n]

                def up(q, i, first=False):
                    for j in range(2):
                        chunk_in(8 * q + 2 * i + c + j)
                        pe.wait_ge(*at(n, "dn", 8 * q + 2 * j + 2))
                        pe.wait_ge(*at(n, "t", 8 * q + 4 * i + 2 * j + 2))
                        if first and j == 0:
                            pair(0, 0, xh, xl, lambda k: at("n_" + n, "lo", k + 1))
                            squares_pe(pe, "n_" + n)
                        else:
                            half8(j, 0, 2 * j, xh, xl)
                            half8(j, 1, 2 * j + 1, xh, xl)

                def down(q):
                    with pe.Fori(0, 2) as i:
                        for j in range(2):
                            chunk_in(8 * q + 2 * i + c + 4 + j)
                            if j:
                                pe.wait_ge(*at(n, "t", 8 * q + 12))
                            pe.wait_ge(*at(n, "dn", 8 * q + 4 * i + 2 * j + 2))
                            if j == 0:
                                pe.wait_ge(*at(n, "t", 8 * q + 10))
                                pair(0, 0, FH, FL, lambda k: at(n, "fl", 8 * q + 5 + k))
                            else:
                                half8(1, 0, 2, FH, FL)
                                half8(1, 1, 3, FH, FL)

                up(0, 0, first=True)
                up(0, 1)
                down(0)
                with pe.Fori(1, 4) as q:
                    with pe.Fori(0, 2) as i:
                        up(q, i)
                    down(q)

            mlp_pe("mlp0", XH, XL)
            norm_pe(pe, "n_fin0")
            norm_pe(pe, "n_hg")

            c = FIRST["hg"]
            with pe.Fori(0, 4) as i:
                for n in range(4):
                    chunk_in(4 * i + c + n)
                    for j in range(2):
                        if n == 0:
                            if j == 0:
                                pe.wait_ge(s_("hg_done"), 2 * i + 2)
                                pair(0, 0, XH, XL, lambda k: at("n_hg", "lo", k + 1))
                        elif n == 1:
                            pe.wait_ge(s_("hv_done"), 2 * i + j + 1)
                            half8(1, j, 2 + j, XH, XL)
                        elif n == 2:
                            pe.wait_ge(s_("hq_done"), 2 * i + j + 3)
                            half8(0, j, j, XH, XL)
                        else:
                            pe.wait_ge(s_("hf_sg"), 2 * i + j + 1)
                            hi = w_hi[:, 1].rearrange("p (k n) -> p k n", k=8)
                            lo = w_lo[:, 1].rearrange("p (k n) -> p k n", k=8)
                            for b in range(2):
                                t0 = (2 * j + b) * P
                                mm = product_x(ps[:, 2 + j, b * 256:(b + 1) * 256], tiles(hi), tiles(lo),
                                               [XH[:, k, t0:t0 + P] for k in range(KD)],
                                               [XL[:, k, t0:t0 + P] for k in range(KD)])
                            mm.then_inc(halves, 1)
                for n in range(2):
                    h = 2 * i + n
                    for l in range(len(LEVELS) + 1):
                        pe.wait_ge(s_("h_g_free"), 8 * h + l + 1)
                        if l < len(LEVELS):
                            pe.wait_ge(s_("h_qk"), 14 * h + 2 * l + 2)
                        for b in range(TB):
                            t = slice(b * P, (b + 1) * P)
                            st, mv = (HE[:, l, t], HE[:, l, t]) if l < len(LEVELS) else (HK[:, n, t], HQ[:, n, t])
                            mm = pe.matmul(ps[:, 4 + l % 2, t], st, mv, start=True, stop=True)
                        mm.then_inc(s_("h_g"), 1)
                    pe.wait_ge(s_("h_kd"), h + 1)
                    for b in range(3):
                        pe.transpose(ps[:, 7, b * P:(b + 1) * P], HKD[:, b * P:(b + 1) * P], ident[:]).then_inc(s_("h_kt"), 1)
                    pe.wait_ge(s_("h_kt_c"), h + 1)
                    pe.wait_ge(s_("hv_done"), 2 * i + 4)
                    hv = [HV[:, b, n * P:(n + 1) * P] for b in range(TB)]
                    for b in range(3):
                        if b:
                            pe.wait_ge(s_("h_s"), 3 * h + b)
                        pe.matmul(ps[:, 7, 384:512], HKT[:, b], hv[b], start=True, stop=True).then_inc(s_("h_st"), 1)
                    pe.wait_ge(s_("h_g_free"), 8 * h + 10)
                    pe.wait_ge(s_("h_s"), 3 * h + 3)
                    for b in range(TB):
                        t = slice(b * P, (b + 1) * P)
                        mm = pe.matmul(ps[:, 6, t], hv[b], HP[:, t], start=True, stop=b == 0)
                        if b:
                            mm = pe.matmul(ps[:, 6, t], HS[:, b - 1], HQD[:, t], start=False, stop=True)
                    mm.then_inc(s_("h_o"), 1)
                    pe.wait_ge(s_("h_sq"), h + 1)
                    pe.matmul(ps[:, 7], ones[:], tmp[:, 0], start=True, stop=True).then_inc(s_("h_mean"), 1)

            pe.wait_ge(s_("ho_done"), 2 + HEADS_H)
            plain(FIRST["hwo"], 2, lambda v: at("hwo", "x", v), OH, OL)
            mlp_pe("mlp1", XH, XL)

            c = FIRST["kvq"]
            chunk_in(c)
            pe.wait_ge(*at("mlp1", "dn", 34))
            pair(0, 0, XH, XL, lambda k: at("n_kv", "lo", k + 1))

            def one_tile(c, s, bank, XH=XH, XL=XL):
                chunk_in(c)
                h, l = w1(w_hi, s, 8), w1(w_lo, s, 8)
                product(ps[:, bank], h[:4], l[:4], tiles(XH, 4), tiles(XL, 4), stop=False).then_inc(halves, 1)
                product(ps[:, bank], h[4:], l[4:], tiles(XH, 4, 4), tiles(XL, 4, 4), start=False).then_inc(halves, 1)

            def small_norm_pe(n):
                for k in range(2):
                    pe.wait_ge(*at(n, "sq", k + 1))
                    mm = pe.matmul(ps[:, 7], ones[:], tmp[:, k], start=k == 0, stop=k == 1)
                mm.then_inc(sig(n, "mean"), 1)

            pe.wait_ge(*at("mlp1", "dn", 36))
            one_tile(c + 1, 1, 2)
            squares_pe(pe, "n_kv")
            small_norm_pe("ckv")
            pe.wait_ge(mconst_in, 64)
            pe.wait_ge(s_("kr_raw"), 1)
            pe.matmul(ps[:, 3], swap_t[:], QR[:, 2], start=True, stop=True).then_inc(s_("kr_swap"), 1)
            pe.wait_ge(*at("n_mla", "lo", KD))
            one_tile(c + 2, 0, 0, XH2, XL2)
            one_tile(c + 3, 1, 1, XH2, XL2)
            small_norm_pe("cq")

            c = FIRST["att"]
            pe.wait_ge(*at("cq", "lo", 2))
            pe.sem_inc(s_("a_pt"), 4)
            pe.sem_inc(s_("a_pv"), 1)
            with pe.Fori(0, 4) as i:
                def part(t, s, at, k, step, n):
                    return [t[:, s, at + q * step:at + q * step + n] for q in range(k)]

                chunk_in(2 * i + c)
                pe.wait_ge(s_("a_exp"), 16 * i + 4)
                for h in range(4):
                    mm = product(ps[:, h], part(w_hi, 0, h * P, 2, 512, P), part(w_lo, 0, h * P, 2, 512, P),
                                 tiles(CKH, 2), tiles(CKL, 2))
                mm.then_inc(halves, 1)
                pe.wait_ge(s_("al_done"), 4 * i + 1)
                for b in range(TB):
                    mm = product_x(ps[:, 4 + b], part(w_hi, 0, 1024, 2, 512, 512), part(w_lo, 0, 1024, 2, 512, 512),
                                   [CKH[:, k, b * P:(b + 1) * P] for k in range(2)],
                                   [CKL[:, k, b * P:(b + 1) * P] for k in range(2)])
                mm.then_inc(halves, 1)
                chunk_in(2 * i + c + 1)
                for h in range(4):
                    pe.wait_ge(s_("kn_done"), 4 * i + h + 1)
                    mm = product(ps[:, h], part(w_hi, 1, h * P, 2, 512, P), part(w_lo, 1, h * P, 2, 512, P),
                                 tiles(CQH, 2), tiles(CQL, 2))
                mm.then_inc(halves, 1)
                pe.wait_ge(s_("vt_done"), 4 * i + 4)
                for h in range(2):
                    mm = product(ps[:, 4 + h], part(w_hi, 1, 1024 + h * P, 2, 256, P),
                                 part(w_lo, 1, 1024 + h * P, 2, 256, P), tiles(CQH, 2), tiles(CQL, 2))
                mm.then_inc(halves, 1)
                for h in range(2):
                    pe.wait_ge(s_("qr_raw"), 2 * i + h + 1)
                    pe.matmul(ps[:, 6 + h], swap_t[:], QR[:, 2 + h], start=True, stop=True).then_inc(s_("qr_swap"), 1)

                def scores(h):
                    r = slice(ROPE * (h % 2), ROPE * (h % 2) + ROPE)
                    for b in range(TB):
                        n = (b + 1) * P
                        pe.wait_ge(s_("a_exp"), 16 * i + 4 * h + b + 1)
                        pe.matmul(ps[:, b, 0:n], QN[:, h, b * P:n], KN[:, h, 0:n], start=True, stop=False)
                        pe.matmul(ps[:, b, 0:n], QR[r, h // 2, b * P:n], KR[r, 0:n], start=False, stop=True)\
                            .then_inc(s_("a_qk"), 1)

                def turn(h):
                    for b in range(TB):
                        t = 16 * i + 4 * h + b
                        pe.wait_ge(s_("a_pm"), t + 1)
                        pe.wait_ge(s_("a_ptc"), t + 1)
                        for j in range(b + 1):
                            mm = pe.transpose(ps[:, 4 + b % 2, j * P:(j + 1) * P], PM[:, b, j * P:(j + 1) * P], ident[:])
                        mm.then_inc(s_("a_pt"), 1)

                def weigh(h):
                    pe.wait_ge(s_("a_ptc"), 16 * i + 4 * h + 6)
                    pe.wait_ge(s_("al_done"), 4 * i + h + 1)
                    for j in range(TB):
                        mm = pe.matmul(ps[:, 6, j * P:T], VT[:, j, h * P:(h + 1) * P], PT[:, j, j * P:T],
                                       start=j == 0, stop=j == TB - 1)
                    mm.then_inc(s_("a_pv"), 1)

                pe.wait_ge(s_("qn_done"), 4 * i + 4)
                pe.wait_ge(s_("qr_done"), 2 * i + 2)
                scores(0)
                for h in range(4):
                    if h < 3:
                        scores(h + 1)
                    turn(h)
                    weigh(h)

            pe.wait_ge(s_("al_done"), 1 + HEADS_M)
            single(FIRST["mwo"], 16, lambda v: at("mwo", "x", v), AH, AL)
            mlp_pe("mlp2", XH2, XL2)
            norm_pe(pe, "n_fin1")
            pe.wait_ge(*at("n_fin1", "t", KD))
            for g in range(TB * 2):
                b = g // 2
                if g >= 4:
                    pe.wait_ge(s_("y_out"), g - 3)
                for j in range(4):
                    mm = pe.transpose(ps[:, g % 4, j * P:(j + 1) * P], X[:, 4 * (g % 2) + j, b * P:(b + 1) * P], ident[:])
                mm.then_inc(s_("y_turned"), 1)


def level_masks():
    s, t = np.arange(P)[:, None], np.arange(P)[None, :]
    out = [(s // (2 * m) == t // (2 * m)) & (s % (2 * m) < m) & (t % (2 * m) >= m) for m in LEVELS]
    return np.ascontiguousarray(np.stack(out + [s == t], axis=1).astype(np.float32).reshape(P, 2, T))


def rotary():
    half = ROPE // 2
    inv_freq = np.float32(10000.0) ** (-np.arange(half, dtype=np.float32) / np.float32(half))
    ang = (np.arange(T, dtype=np.float32)[:, None] * inv_freq[None, :]).T
    cos, sin = np.cos(ang), np.sin(ang)
    swap = np.zeros((P, P), np.float32)
    swap[np.arange(P), np.arange(P) ^ half] = 1.0
    return np.concatenate([cos] * 4), np.concatenate([-sin, sin] * 2), swap


def constants():
    cos, sin, swap = rotary()
    r = np.ones((P, T), np.float32)
    r[:, ::P] = 0.0
    return {
        "ident": np.eye(P, dtype=np.float32), "ones": np.ones((P, P), np.float32),
        "level_masks": level_masks(), "reset": r, "cos": cos, "sin": sin, "swap": swap,
        "neg": np.triu(np.full((P, P), -1e30, np.float32), 1),
    }


def pack_vectors(inputs):
    cols = []
    for name, n in VECTOR_WIDTHS:
        if name == "eps":
            v = np.full((P, 1), EPS, np.float32)
        elif name in ("conv_a_w", "conv_b_w"):
            w = np.asarray(inputs[name])[0]
            v = w.reshape(w.shape[0], -1, P).transpose(2, 1, 0).reshape(P, n)
        else:
            v = np.asarray(inputs[name]).reshape(n, P).T
        cols.append(v)
    return np.ascontiguousarray(np.concatenate(cols, axis=1))


WEIGHTS = ["w_in", "w_a_out", "w_rg_a", "w_rg_x", "w_b_out", "w_o", "w_1", "w_2", "hgrn_w_q_2", "hgrn_w_f_2",
           "hgrn_w_i_2", "hgrn_w_g_2", "hgrn_w_o_2", "mla_w_dq_2", "mla_w_uq_2", "mla_w_o_2"]
PLAIN = ["x", "kv_w_dkv_2", "kv_w_uk_2", "kv_w_uv_2", "mlp_w_up_2", "mlp_w_down_2"]


def kernel(**inputs):
    import concourse.bacc as _bacc
    from concourse.bass_utils import run_bass_kernel_spmd as _run

    nc = _bacc.Bacc("TRN2", target_bir_lowering=False, num_devices=1)
    arrays = {n: np.ascontiguousarray(inputs[n]) for n in WEIGHTS + PLAIN}
    arrays["vectors"] = pack_vectors(inputs)
    arrays.update(constants())
    aps, sent = {}, {}
    for name, v in arrays.items():
        sent[f"in_{name}"] = v
        ap = nc.dram_tensor(f"in_{name}", v.shape, mybir.dt.from_np(v.dtype), kind="ExternalInput").ap()
        aps[name] = ap[0] if name in WEIGHTS else ap
    out = nc.dram_tensor("out_0", (1, T, D), F32, kind="ExternalOutput").ap()
    build_program(nc, aps, out)
    r = _run(nc, [sent], core_ids=[0])
    return r.results[0]["out_0"]
```

```python
from contextlib import ExitStack

import numpy as np

import concourse.bass as bass
from concourse import mybir

P = 128
T = 512
TB = T // P
D = 1024
KD = D // P
D_RNN = 1536
RT = D_RNN // P
TAPS_A = 31
TAPS_B = 4
HEADS_H = 8
HEADS_M = 16
NOPE, ROPE = 128, 64
LORA = 256
D_FF = 4096
Q_FF = D_FF // 4
SCALE = float(NOPE + ROPE) ** -0.5
LEVELS = (64, 32, 16, 8, 4, 2, 1)
Y_BANKS = (4, 5, 6, 0, 1, 2, 3, 4)
BO_BANKS = (6, 7, 0, 1)
EPS = 1e-6

F32 = mybir.dt.float32
F32R = mybir.dt.float32r
U8 = mybir.dt.uint8
ALU = mybir.AluOpType
ACT = mybir.ActivationFunctionType
AX = mybir.AxisListType.X

VECTOR_WIDTHS = [
    ("g_mix", 8), ("b_in", 56), ("conv_a_b", 8), ("ln_g", 8), ("ln_b", 8), ("conv_b_b", 12),
    ("b_rg_a", 12), ("b_rg_x", 12), ("lam", 12), ("g_mlp", 8), ("g_final", 8), ("hgrn_norm_2", 8),
    ("hgrn_g_norm_2", 1), ("hgrn_lb_logits_2", 16), ("mla_norm_2", 8), ("mla_q_norm_2", 2),
    ("kv_in_norm_2", 8), ("kv_norm_2", 2), ("mlp_norm_2", 16), ("final_norm_2", 8),
    ("conv_b_w", 48), ("conv_a_w", 248), ("eps", 1),
]
COLUMN = {}
_at = 0
for _name, _n in VECTOR_WIDTHS:
    COLUMN[_name] = _at
    _at += _n
N_COLUMNS = _at

CHUNKS = [("ug", 8), ("xb", 6), ("sb", 4), ("gb", 6), ("sa", 4), ("bandya", 8), ("bo", 8), ("wo", 4),
          ("mlp0", 32), ("hg", 16), ("hwo", 4), ("mlp1", 32), ("kvq", 4), ("att", 8), ("mwo", 8),
          ("mlp2", 32)]
FIRST = {}
_at = 0
for _name, _n in CHUNKS:
    FIRST[_name] = _at
    _at += _n
N_CHUNKS = _at
MASK_COLUMNS = len(LEVELS) * 64 + P

BAND = [(0, 0), (1, 0), (0, 1), (1, 1), (2, 1), (1, 2), (2, 2)]


def build_program(nc, a, out):
    ctx = ExitStack()
    with ctx:
        top = [nc.sbuf_base + (-nc.sbuf_base) % 32]

        def place(name, shape, dt, at=None):
            size = int(np.prod(shape[1:])) * (1 if dt == U8 else 4)
            where = top[0] if at is None else at
            if at is None:
                top[0] += size + (-size) % 32
            return nc.alloc_sbuf_tensor_at(name, list(shape), dt, offset=where), where

        def sem(name):
            return ctx.enter_context(nc.semaphore(name))

        raw, _ = place("raw", [P, 2, 2048], F32)
        w_hi, _ = place("w_hi", [P, 2, 2048], F32R)
        w_lo, _ = place("w_lo", [P, 2, 2048], F32R)
        vec, _ = place("vec", [P, N_COLUMNS], F32)
        ident, _ = place("ident", [P, P], F32)
        ones, _ = place("ones", [P, P], F32)
        small, _ = place("small", [P, 128], F32)
        tmp, a_tmp = place("tmp", [P, 4, T], F32)
        rst, a_rst = place("rst", [P, 2, T], F32)
        X, _ = place("X", [P, KD, T], F32)
        XH, a_xh = place("XH", [P, KD, T], F32R)
        XL, _ = place("XL", [P, KD, T], F32R)
        S = top[0]
        TILE = T * 4

        x_tm, _ = place("x_tm", [P, TB, D], F32, S)
        CO, _ = place("CO", [P, KD, T], F32, S)
        LR, _ = place("LR", [P, 6, T], F32, S)
        MH, _ = place("MH", [P, KD, T], F32R, S)
        V, _ = place("V", [P, RT, T], F32, S + 8 * TILE)
        VGH, _ = place("VGH", [P, RT, T], F32R, S + 8 * TILE)
        G, _ = place("G", [P, RT, T], F32, S + 20 * TILE)
        VGL, _ = place("VGL", [P, RT, T], F32R, S + 20 * TILE)
        XBR_MORE = RT * 4 * 4
        XBR, _ = place("XBR", [P, RT, 4 + T], F32, S + 20 * TILE)
        SBG, _ = place("SBG", [P, KD, T], F32, S + 32 * TILE + XBR_MORE)
        ML, _ = place("ML", [P, KD, T], F32R, S + 32 * TILE + XBR_MORE)
        GA, _ = place("GA", [P, KD, T], F32, S + 40 * TILE + XBR_MORE)
        M, _ = place("M", [P, KD, T], F32, S + 40 * TILE + XBR_MORE)
        PAD = TAPS_A - 1
        UP, _ = place("UP", [P, 2, PAD + T], F32, a_tmp + 2 * TILE)
        VH, _ = place("VH", [P, 3, T], F32R, a_tmp)
        VL, _ = place("VL", [P, 3, T], F32R, a_tmp + 3 * TILE)
        assert a_rst == a_tmp + 4 * TILE
        at_end = S + 48 * TILE + XBR_MORE
        FH, _ = place("FH", [P, KD, T], F32R, S)
        FL, _ = place("FL", [P, KD, T], F32R, S + KD * TILE)
        base = S
        OH, _ = place("OH", [P, KD, T], F32R, base)
        OL, _ = place("OL", [P, KD, T], F32R, base + 8 * TILE)
        tiles_of = [
            ("HR", [P, T], F32),
            ("HZ", [P, T], F32), ("HQ", [P, T], F32), ("HK", [P, T], F32), ("HF", [P, T], F32),
            ("HGATE", [P, 2, T], F32),
            ("HVF", [P, T], F32), ("HV", [P, 2, TB, P], F32),
            ("HE", [P, 7, T], F32), ("HP", [P, T], F32), ("HQD", [P, 2, T], F32), ("HKD", [P, 2, T], F32),
            ("HEB", [P, 2, T], F32), ("HSG", [P, 2, T], F32), ("reset", [P, T], F32),
            ("HKT", [P, 3, P], F32), ("HS", [P, 3, P], F32), ("masks", [P, 9 * 256], U8),
        ]
        at_h, made = base + 16 * TILE, []
        for name, shape, dt in tiles_of:
            made.append(place(name, shape, dt, at_h)[0])
            size = int(np.prod(shape[1:])) * (1 if dt == U8 else 4)
            at_h += size + (-size) % 32
        HR, HZ, HQ, HK, HF, HGATE, HVF, HV, HE, HP, HQD, HKD, HEB, HSG, reset, HKT, HS, masks = made
        AH, _ = place("AH", [P, HEADS_M, T], F32R, a_xh)
        AL, _ = place("AL", [P, HEADS_M, T], F32R, S)
        base = S + 16 * TILE
        KN, _ = place("KN", [P, 4, T], F32, base)
        QN, _ = place("QN", [P, 4, T], F32, base + 4 * TILE)
        VT, _ = place("VT", [P, TB, 512], F32, base + 8 * TILE)
        TRIANGLE = TB * (TB + 1) // 2 * P
        PM, _ = place("PM", [P, 2, TRIANGLE], F32, base + 12 * TILE)
        PT, _ = place("PT", [P, TRIANGLE], F32, base + 17 * TILE)
        QR, _ = place("QR", [P, 4, T], F32, base + 20 * TILE)
        KR, _ = place("KR", [P, T], F32, base + 24 * TILE)
        cos_t, _ = place("cos_t", [P, T], F32, base + 25 * TILE)
        sin_t, _ = place("sin_t", [P, T], F32, base + 26 * TILE)
        swap_t, _ = place("swap_t", [P, P], F32, base + 27 * TILE)
        neg_t, _ = place("neg_t", [P, P], F32, base + 27 * TILE + 512)
        CKH, _ = place("CKH", [P, 2, T], F32R, base + 28 * TILE)
        CKL, _ = place("CKL", [P, 2, T], F32R, base + 30 * TILE)
        CQH, _ = place("CQH", [P, 2, T], F32R, a_tmp)
        CQL, _ = place("CQL", [P, 2, T], F32R, a_tmp + 2 * TILE)
        CQ, _ = place("CQ", [P, 8, T], F32, S + 8 * TILE)
        CK, _ = place("CK", [P, 8, T], F32, S)
        XH2, _ = place("XH2", [P, KD, T], F32R, base)
        XL2, _ = place("XL2", [P, KD, T], F32R, base + 8 * TILE)
        y_tm, _ = place("y_tm", [P, TB, D], F32, S)
        assert max(at_end, at_h, base + 32 * TILE) <= nc.sbuf_usable_end, (
            max(at_end, at_h, base + 32 * TILE) - nc.sbuf_usable_end)

        ps = ctx.enter_context(nc.psum_tensor("ps", [P, 8, T], F32))

        raw_in = [sem("raw_in_0"), sem("raw_in_1")]
        hi_done = sem("hi_done")
        lo_done = sem("lo_done")
        halves = sem("halves")
        band_in = sem("band_in")
        band_zero = sem("band_zero")
        parts_in = sem("parts_in")
        consts_in = sem("consts_in")
        x_in = [sem("x_in_0"), sem("x_in_1")]
        ident_in = sem("ident_in")
        out_done = sem("out_done")

        S_ = {}

        def s_(name):
            if name not in S_:
                S_[name] = sem(name)
            return S_[name]

        taken_over = {
            "a_exp": ("lru_b", RT), "a_mask": ("lru_e", RT), "a_max": ("lru_iv", RT), "a_nmax": ("lru_m", RT),
            "a_pm": ("lru_m1", RT), "a_pt": ("lru_r", RT), "a_ptc": ("lru_s", RT), "a_pv": ("lru_t", RT),
            "a_qk": ("lru_x", RT), "a_rs": ("vg_hi", RT), "ah_done": ("vg_t", RT), "al_done": ("vh_done", RT),
            "kn_done": ("vl_done", RT), "qn_done": ("gb_zz", RT), "qr_a": ("gb_p", RT),
            "qr_done": ("gb_th", RT), "qr_raw": ("gb_g", RT), "qr_swap": ("u_done", KD),
            "vt_done": ("x_fm", KD),
        }

        def att(name, value):
            return s_(taken_over[name][0]), value + taken_over[name][1]

        kinds = {
            "norm": ["n_mix", "n_fin1"],
            "scaled": ["n_mlp0", "n_hg", "n_mlp1", "n_mla", "n_kv", "n_mlp2"],
            "small": ["cq", "ckv"],
            "mlp": ["mlp0", "mlp1", "mlp2"],
            "sum": ["wo", "hwo", "mwo"],
        }
        kind_of = {n: kind for kind, stages in kinds.items() for n in stages}

        def signals(n, what):
            if kind_of[n] == "norm":
                if what in ("hi", "lo"):
                    return 0 if n == "n_fin1" else KD
                return 1 if what in ("ln", "inv") else KD
            if kind_of[n] == "scaled":
                if what in ("hi", "lo"):
                    return KD
                return 0 if n in ("n_hg", "n_mla") else {"sq": KD, "add": KD - 1, "mean": 1, "ln": 1, "inv": 1}[what]
            if kind_of[n] == "small":
                return 1 if what in ("mean", "ln", "inv") else 2
            return {"mlp": {"t": 4 + 32, "sq": 32, "fh": 32, "fl": 4 + 32, "dn": 4 + 32}, "sum": {"x": 4 + KD}}[kind_of[n]][what]

        def sig(n, what):
            return s_(kind_of[n] + "_" + what)

        def at(n, what, value):
            stages = kinds[kind_of[n]]
            return sig(n, what), value + sum(signals(m, what) for m in stages[:stages.index(n)])

        def half_at(c, j=1):
            return 2 * c + (5 + j)

        def col(name, k=0, n=1):
            return vec[:, COLUMN[name] + k:COLUMN[name] + k + n]

        def dcol(name, k):
            return vec[:, bass.ds(k + COLUMN[name], 1)]

        def w8(t, s, n):
            v = t[:, s].rearrange("p (k n) -> p k n", k=8)
            return [v[:, k, n * P:(n + 1) * P] for k in range(8)]

        def w1(t, s, kt):
            v = t[:, s, 0:kt * P].rearrange("p (k n) -> p k n", k=kt)
            return [v[:, k] for k in range(kt)]

        def rows(b):
            return slice(b * (b + 1) // 2 * P, (b + 1) * (b + 2) // 2 * P)

        def y_half(n):
            return y_tm[:, n % TB, n // TB * 512:n // TB * 512 + 512]

        class Count:

            def __init__(self, eng, name):
                self.eng, self.sem, self.at = eng, s_(name), 0

            def put(self, instruction):
                instruction.then_inc(self.sem, 1)
                self.at = self.at + 1
                return self.at

            def wait(self, value=None):
                self.eng.wait_ge(self.sem, self.at if value is None else value)

        def inverse_act(act, n, width, dst=None):
            act.activation(rst[:, 0], ps[:, 7], ACT.Ln, bias=col("eps"), scale=1.0 / width).then_inc(sig(n, "ln"), 1)
            act.wait_ge(*at(n, "ln", 1))
            act.activation(rst[:, 1] if dst is None else dst, rst[:, 0], ACT.Exp, scale=-0.5)\
                .then_inc(sig(n, "inv"), 1)

        def norm_act(act, n, ready, split=True, first=None):
            for k in range(KD):
                act.wait_ge(*ready(k))
                if k >= 4:
                    act.wait_ge(*at(n, "mean", k - 3))
                act.activation(tmp[:, k % 4], X[:, k], ACT.Square).then_inc(sig(n, "sq"), 1)
            if first is not None:
                first()
            act.wait_ge(*at(n, "mean", KD))
            inverse_act(act, n, D)
            if split:
                for k in range(KD):
                    act.wait_ge(*at(n, "t", k + 1))
                    act.activation(XH[:, k], tmp[:, 2 + k % 2], ACT.Copy).then_inc(sig(n, "hi"), 1)

        def norm_pe(pe, n):
            for k in range(KD):
                pe.wait_ge(*at(n, "sq", k + 1))
                pe.matmul(ps[:, 7], ones[:], tmp[:, k % 4], start=k == 0, stop=k == KD - 1)\
                    .then_inc(sig(n, "mean"), 1)

        def norm_dve(dve, n, gain, off=0, split=True, invert=True):
            if invert:
                dve.wait_ge(*at(n, "inv", 1))
            for k in range(KD + 1):
                if k < KD:
                    if split and k >= 2:
                        dve.wait_ge(*at(n, "lo", k - 1))
                    dve.scalar_tensor_tensor(tmp[:, 2 + k % 2] if split else X[:, k], X[:, k],
                                             col(gain, off + k), rst[:, 1], ALU.mult, ALU.mult)\
                        .then_inc(sig(n, "t"), 1)
                if split and k >= 1:
                    dve.wait_ge(*at(n, "hi", k))
                    dve.tensor_tensor(XL[:, k - 1], tmp[:, 2 + (k - 1) % 2], XH[:, k - 1].bitcast(F32),
                                      ALU.subtract).then_inc(sig(n, "lo"), 1)

        def scaled_act(act, n, ready, gain, off=0, xh=XH, split=None):
            for k in range(KD):
                if k == KD - 2 and split is not None:
                    split()
                act.wait_ge(*ready(k))
                act.activation(xh[:, k], X[:, k], ACT.Copy, scale=col(gain, off + k)).then_inc(sig(n, "hi"), 1)

        def squares_act(act, n, inverse=True):
            for k in range(KD):
                if k >= 4:
                    act.wait_ge(*at(n, "add", k - 4 + (k == 4)))
                act.activation(tmp[:, k % 4], X[:, k], ACT.Square).then_inc(sig(n, "sq"), 1)
            if inverse:
                rest_act(act, n)

        def rest_act(act, n):
            act.wait_ge(*at(n, "mean", 1))
            inverse_act(act, n, D)

        def scaled_dve(dve, n, gain, off=0, xh=XH, xl=XL):
            for k in range(KD):
                dve.wait_ge(*at(n, "hi", k + 1))
                dve.scalar_tensor_tensor(xl[:, k], X[:, k], col(gain, off + k), xh[:, k].bitcast(F32), ALU.mult,
                                         ALU.subtract).then_inc(sig(n, "lo"), 1)

        def squares_dve(dve, n, inverse=True):
            for k in range(1, KD):
                dve.wait_ge(*at(n, "sq", k + 1))
                if k >= 2:
                    dve.wait_ge(*at(n, "add", k - 1))
                dve.tensor_tensor(rst[:, 0], rst[:, 0] if k >= 2 else tmp[:, 0], tmp[:, k % 4], ALU.add)\
                    .then_inc(sig(n, "add"), 1)
            if inverse:
                dve.wait_ge(*at(n, "inv", 1))

        def squares_pe(pe, n):
            pe.wait_ge(*at(n, "add", KD - 1))
            pe.matmul(ps[:, 7], ones[:], rst[:, 0], start=True, stop=True).then_inc(sig(n, "mean"), 1)

        block = ctx.enter_context(nc.Block())

        @block.sync
        def _(sp):
            sp.dma_start(ident[:], a["ident"]).then_inc(ident_in, 16)
            for h in range(2):
                cols = slice(h * 512, h * 512 + 512)
                sp.dma_start(x_tm[:, :, cols], a["x"][:, :, cols].rearrange("b (t p) d -> p (b t) d", p=P)).then_inc(x_in[h], 16)
            sp.dma_start(vec[:], a["vectors"]).then_inc(consts_in, 16)
            sp.dma_start(ones[:], a["ones"]).then_inc(consts_in, 16)

            def slot_free(c):
                sp.wait_ge(lo_done, c + 1)

            def load8(c, s, w, col0, row0=0, waited=False):
                if not waited:
                    slot_free(c)
                v = raw[:, s].rearrange("p (k n) -> p k n", k=8)
                for h in range(2):
                    sp.dma_start(v[:, 4 * h:4 * h + 4],
                                 w[bass.ds(row0 + 512 * h, 512), bass.ds(col0, 256)]
                                 .rearrange("(k p) n -> p k n", p=P)).then_inc(raw_in[s], 16)

            def load1(c, s, w, col0, kt):
                slot_free(c)
                v = raw[:, s, 0:kt * P].rearrange("p (k n) -> p k n", k=kt)
                for h in range(2):
                    sp.dma_start(v[:, h * kt // 2:(h + 1) * kt // 2],
                                 w[h * kt * P // 2:(h + 1) * kt * P // 2, bass.ds(col0, P)]
                                 .rearrange("(k p) n -> p k n", p=P)).then_inc(raw_in[s], 16)

            w_in = a["w_in"]

            def load_pairs(stage, iters, col0):
                c = FIRST[stage]
                with sp.Fori(0, iters) as i:
                    for s in range(2):
                        load8(2 * i + c + s, s, w_in, i * 512 + 256 * s + col0)

            c = FIRST["ug"]
            with sp.Fori(0, 4) as i:
                load8(2 * i + c, 0, w_in, i * 256)
                load8(2 * i + c + 1, 1, w_in, i * 256 + D)
            load_pairs("xb", 3, 2 * D)
            load_pairs("sb", 2, 3 * D + 2 * D_RNN)
            load_pairs("gb", 3, 2 * D + D_RNN)
            load_pairs("sa", 2, 2 * D + 2 * D_RNN)
            c = FIRST["bandya"]
            with sp.Fori(0, 4) as i:
                slot_free(2 * i + c)
                sp.wait_ge(band_zero, 1)
                n = 0
                for gate, w in enumerate((a["w_rg_a"], a["w_rg_x"])):
                    for j in range(4):
                        r = 96 * j
                        while r < 96 * j + 96:
                            r1 = min(96 * j + 96, (r // P + 1) * P)
                            q = 96 * j
                            while q < 96 * j + 96:
                                q1 = min(96 * j + 96, (q // P + 1) * P)
                                b = 7 * gate + BAND.index((r // P, q // P))
                                sp.dma_start(
                                    raw[r % P:r % P + r1 - r, 0, b * P + q % P:b * P + q % P + q1 - q],
                                    w[bass.ds(i * 4 + j, 1), r - 96 * j:r1 - 96 * j,
                                      q - 96 * j:q1 - 96 * j].rearrange("h r q -> (h r) q"))\
                                    .then_inc(band_in, 16)
                                n += 16
                                q = q1
                            r = r1
                sp.wait_ge(band_in, i * n + n)
                sp.sem_inc(raw_in[0], 32)
                slot_free(2 * i + c + 1)
                sp.sem_inc(s_("slot_seen"), 1)
                load8(2 * i + c + 1, 1, a["w_a_out"], i * 256, waited=True)
            c = FIRST["bo"]
            with sp.Fori(0, 4) as i:
                for s in range(2):
                    load1(2 * i + c + s, s, a["w_b_out"], i * 256 + P * s, RT)
            c = FIRST["wo"]
            with sp.Fori(0, 2) as i:
                for s in range(2):
                    load8(2 * i + c + s, s, a["w_o"], i * 512 + 256 * s)

            def load_mlp(c, up, down):
                with sp.Fori(0, 4) as q:
                    with sp.Fori(0, 2) as i:
                        for s in range(2):
                            load8(8 * q + 2 * i + c + s, s, up, q * Q_FF + i * 512 + 256 * s)
                    with sp.Fori(0, 2) as i:
                        for s in range(2):
                            load8(8 * q + 2 * i + c + 4 + s, s, down, i * 512 + 256 * s, q * Q_FF)

            load_mlp(FIRST["mlp0"], a["w_1"], a["w_2"])
            c = FIRST["hg"]
            with sp.Fori(0, HEADS_H) as h:
                for s, ws in enumerate((("hgrn_w_q_2", "hgrn_w_f_2"), ("hgrn_w_g_2", "hgrn_w_i_2"))):
                    slot_free(2 * h + c + s)
                    sp.sem_inc(s_("slot_seen"), 1)
                    v = raw[:, s].rearrange("p (k n) -> p k n", k=8)
                    for n, w in enumerate(ws):
                        sp.dma_start(v[:, :, n * P:(n + 1) * P],
                                     a[w][:, bass.ds(h * P, P)].rearrange("(k p) n -> p k n", p=P)).then_inc(raw_in[s], 16)
            c = FIRST["hwo"]
            with sp.Fori(0, 2) as i:
                for s in range(2):
                    load8(2 * i + c + s, s, a["hgrn_w_o_2"], i * 512 + 256 * s)
            load_mlp(FIRST["mlp1"], a["mlp_w_up_2"][0], a["mlp_w_down_2"][0])
            c = FIRST["kvq"]
            load1(c, 0, a["mla_w_dq_2"], 0, 8)
            load1(c + 1, 1, a["mla_w_dq_2"], P, 8)
            load8(c + 2, 0, a["kv_w_dkv_2"], 0)
            slot_free(c + 3)
            v = raw[:, 1, 0:8 * P].rearrange("p (k n) -> p k n", k=8)
            for h in range(2):
                sp.dma_start(v[:, :, h * ROPE:(h + 1) * ROPE],
                             a["kv_w_dkv_2"][:, LORA:LORA + ROPE].rearrange("(k p) n -> p k n", p=P))\
                    .then_inc(raw_in[1], 16)
            c = FIRST["att"]
            with sp.Fori(0, 4) as i:
                slot_free(2 * i + c)
                src = a["mla_w_uq_2"].rearrange("(k p) (h n) -> k p h n", p=P, n=NOPE + ROPE)
                for k in range(2):
                    sp.dma_start(raw[:, 0, k * 512:(k + 1) * 512].rearrange("p (h n) -> p h n", h=4),
                                 src[k][:, bass.ds(i * 4, 4), 0:NOPE]).then_inc(parts_in, 16)
                    sp.dma_start(raw[:, 0, 1024 + k * 256:1280 + k * 256].rearrange("p (h n) -> p h n", h=4),
                                 src[k][:, bass.ds(i * 4, 4), NOPE:NOPE + ROPE]).then_inc(parts_in, 16)
                sp.wait_ge(parts_in, i * 64 + 64)
                sp.sem_inc(raw_in[0], 32)
                slot_free(2 * i + c + 1)
                sp.sem_inc(s_("slot_seen"), 1)
                for h, w in enumerate(("kv_w_uk_2", "kv_w_uv_2")):
                    sp.dma_start(raw[:, 1, h * 1024:(h + 1) * 1024].rearrange("p (k n) -> p k n", k=2),
                                 a[w][:, bass.ds(i * 512, 512)].rearrange("(k p) n -> p k n", p=P))\
                        .then_inc(raw_in[1], 16)
            c = FIRST["mwo"]
            with sp.Fori(0, 4) as i:
                for s in range(2):
                    load1(2 * i + c + s, s, a["mla_w_o_2"], i * 256 + P * s, 16)
            load_mlp(FIRST["mlp2"], a["mlp_w_up_2"][1], a["mlp_w_down_2"][1])
            for s in range(2):
                load8(N_CHUNKS + s, s, a["mlp_w_down_2"][1], 512 + 256 * s, 3 * Q_FF)
            for b, (ready, n) in enumerate((("y_act", 3), ("y_dve", 3), ("y_act", 4), ("y_dve", 4))):
                sp.wait_ge(s_(ready), n)
                sp.dma_start(out[0, b * P:(b + 1) * P], y_tm[:, b]).then_inc(out_done, 16)
            sp.wait_ge(out_done, 16 * TB)

        @block.gpsimd
        def _(pool):
            pool.sem_inc(lo_done, 2)

            def split_lo(c, s):
                pool.wait_ge(hi_done, c + 1)
                pool.tensor_tensor(w_lo[:, s], raw[:, s], w_hi[:, s].bitcast(F32), ALU.subtract)\
                    .then_inc(lo_done, 1)

            with pool.Fori(0, FIRST["bandya"] // 2 - 1) as i:
                for s in range(2):
                    split_lo(2 * i + s, s)
            split_lo(FIRST["bandya"] - 2, 0)
            pool.wait_ge(lo_done, 2 + FIRST["bandya"] - 1)
            pool.memset(raw[:, 0], 0.0).then_inc(band_zero, 1)
            split_lo(FIRST["bandya"] - 1, 1)
            with pool.Fori(FIRST["bandya"] // 2, N_CHUNKS // 2) as i:
                for s in range(2):
                    split_lo(2 * i + s, s)

        @block.scalar
        def _(act):
            def split_hi(c, s):
                act.wait_ge(raw_in[s], 16 * (c - s) + 32)
                act.wait_ge(halves, 2 * c + 2)
                act.activation(w_hi[:, s], raw[:, s], ACT.Copy).then_inc(hi_done, 1)

            for k in range(KD):
                act.wait_ge(s_("x_turned"), k + 1)
                act.activation(X[:, k], ps[:, k % 4], ACT.Copy).then_inc(s_("x_fm"), 1)
            act.wait_ge(consts_in, 32)
            act.sem_inc(s_("z_evac"), 4)
            norm_act(act, "n_mix", lambda k: (s_("x_fm"), k + 1), first=lambda: (split_hi(0, 0), split_hi(1, 1)))

            act.wait_ge(s_("lam_abs"), 2)
            act.activation(small[:, 24:36], small[:, 12:24], ACT.Exp, scale=-1.0).then_inc(s_("lam_e"), 1)

            ev = s_("z_evac")

            def four_columns(stage, i, dst, func, bias, off=0):
                c = FIRST[stage]
                for j in range(4):
                    act.wait_ge(halves, half_at(2 * i + c + j // 2, j % 2))
                    act.activation(dst[:, bass.ds(4 * i + j, 1), off:off + T], ps[:, j:j + 1], func,
                                   bias=dcol("b_in", 4 * i + bias + j)).then_inc(ev, 1)
                    if j % 2:
                        split_hi(2 * i + c + j // 2 + 2, j // 2)

            def columns(stage, iters, dst, func, bias, off=0):
                with act.Fori(0, iters) as i:
                    four_columns(stage, i, dst, func, bias, off)

            c = FIRST["ug"]
            with act.Fori(0, 4) as i:
                for j in range(4):
                    act.wait_ge(halves, half_at(2 * i + c + j // 2, j % 2))
                    act.activation((CO, GA)[j // 2][:, bass.ds(2 * i + j % 2, 1)], ps[:, j:j + 1],
                                   (ACT.Identity, ACT.Sigmoid)[j // 2],
                                   bias=dcol("b_in", 2 * i + KD * (j // 2) + j % 2)).then_inc(ev, 1)
                    if j % 2:
                        split_hi(2 * i + c + j // 2 + 2, j // 2)
            columns("xb", 3, XBR, ACT.Identity, 2 * KD, 4)
            columns("sb", 2, SBG, ACT.Sigmoid, 48)
            act.wait_ge(s_("v_done"), RT)
            def gelu_act(g):
                for j in range(3):
                    if g:
                        act.wait_ge(s_("gb_g"), 3 * g - 2 + j)
                    act.wait_ge(ev, 4 + 36 + 3 * g + j + 1)
                    act.activation(ps[:, 4 + j], G[:, 3 * g + j], ACT.Square).then_inc(s_("gb_zz"), 1)
                for j in range(3):
                    act.wait_ge(s_("gb_p"), 3 * g + j + 1)
                    act.activation(ps[:, 4 + j], ps[:, 4 + j], ACT.Tanh, scale=0.7978845608028654)\
                        .then_inc(s_("gb_th"), 1)

            columns("gb", 2, G, ACT.Identity, 28)
            gelu_act(0)
            gelu_act(1)
            four_columns("gb", 2, G, ACT.Identity, 28)
            gelu_act(2)

            act.wait_ge(s_("mu_mm"), 1)
            act.activation(rst[:, 1], ps[:, 7], ACT.Copy, scale=1.0 / D).then_inc(s_("mu_done"), 1)
            for k in range(KD):
                act.wait_ge(s_("xc_done"), k + 1)
                if k >= 4:
                    act.wait_ge(s_("xc_add"), max(k - 4, 1))
                act.activation(tmp[:, k % 4], CO[:, k], ACT.Square).then_inc(s_("xc_sq"), 1)

            c = FIRST["sa"]
            act.wait_ge(s_("u_done"), KD)
            for i in range(2):
                for j in range(4):
                    act.wait_ge(halves, half_at(2 * i + c + j // 2, j % 2))
                    act.activation(M[:, 4 * i + j], ps[:, j], ACT.Sigmoid, bias=col("b_in", 40 + 4 * i + j))\
                        .then_inc(ev, 1)
                    if j % 2:
                        split_hi(2 * i + c + j // 2 + 2, j // 2)
                        if (i, j) == (0, 1):
                            gelu_act(3)
                if i == 0:
                    act.wait_ge(s_("var_mm"), 1)
                    act.activation(rst[:, 0], ps[:, 7], ACT.Ln, bias=col("eps"), scale=1.0 / D)\
                        .then_inc(s_("ln_inv"), 1)
                    act.wait_ge(s_("ln_inv"), 1)
                    act.activation(rst[:, 1], rst[:, 0], ACT.Exp, scale=-0.5).then_inc(s_("ln_inv"), 1)
                    for k in range(KD):
                        act.wait_ge(s_("ln_y"), k + 1)
                        if k >= 4:
                            act.wait_ge(s_("ln_u"), k - 3)
                        act.activation(tmp[:, k % 4], CO[:, k], ACT.Sigmoid, bias=col("ln_b", k)).then_inc(s_("ln_sg"), 1)

            act.wait_ge(halves, half_at(c + 3))
            for k in range(KD):
                act.wait_ge(s_("ln_u"), k + 1)
                act.activation(XH[:, k], CO[:, k], ACT.Copy).then_inc(s_("uh_done"), 1)

            c = FIRST["bandya"]
            act.wait_ge(s_("ch_done"), 2)
            act.wait_ge(s_("ul_done"), KD)
            with act.Fori(0, 4) as i:
                act.wait_ge(halves, half_at(2 * i + c))
                act.wait_ge(s_("lru_done"), 3 * i + 3)
                for j in range(3):
                    act.activation(LR[:, 3 + j], ps[:, 3 + j], ACT.Sigmoid, bias=dcol("b_rg_x", 3 * i + j))\
                        .then_inc(s_("lru_x"), 1)
                for j in range(3):
                    act.activation(LR[:, j], ps[:, j], ACT.Sigmoid, bias=dcol("b_rg_a", 3 * i + j))\
                        .then_inc(s_("lru_r"), 1)
                split_hi(2 * i + c + 2, 0)
                for j in range(3):
                    act.wait_ge(s_("lru_r"), 3 * i + j + 1)
                    act.wait_ge(s_("lru_iv"), 3 * i + j + 1)
                    act.activation(LR[:, 3 + j], LR[:, j], ACT.Tanh, scale=small[:, bass.ds(3 * i + 60 + j, 1)])\
                        .then_inc(s_("lru_t"), 1)
                for j in range(3):
                    act.wait_ge(s_("lru_t"), 3 * i + j + 1)
                    act.activation(LR[:, j], LR[:, j], ACT.Exp, scale=small[:, bass.ds(3 * i + 24 + j, 1)])\
                        .then_inc(s_("lru_e"), 1)
                for j in range(3):
                    act.activation(LR[:, 3 + j], LR[:, 3 + j], ACT.Sqrt, scale=-1.0).then_inc(s_("lru_s"), 1)
                split_hi(2 * i + c + 3, 1)

            c = FIRST["bo"]
            with act.Fori(0, 2) as i:
                for j in range(4):
                    act.wait_ge(s_("m_done"), 4 * i + j + 5)
                    act.activation(MH[:, bass.ds(4 * i + j, 1)], M[:, bass.ds(4 * i + j, 1)], ACT.Copy)\
                        .then_inc(s_("mh_done"), 1)
                    split_hi(4 * i + c + j + 2, j % 2)

            def ahead(c, n):
                with act.Fori(0, n - 1) as i:
                    for s in range(2):
                        split_hi(2 * i + c + s + 2, s)
                split_hi(c + 2 * n, 0)

            ahead(FIRST["wo"], 2)

            def mlp_act(n):
                c = FIRST[n]
                with act.Fori(0, 4) as q:
                    with act.Fori(0, 2) as i:
                        for j in range(4):
                            act.wait_ge(*at(n, "t", 8 * q + 4 * i + j + 5))
                            act.activation(FH[:, bass.ds(4 * i + j, 1)], tmp[:, j % 2:j % 2 + 1], ACT.Square)\
                                .then_inc(sig(n, "fh"), 1)
                            if j % 2:
                                split_hi(8 * q + 2 * i + c + j // 2 + 2, j // 2)
                    with act.Fori(0, 2) as i:
                        for s in range(2):
                            split_hi(8 * q + 2 * i + c + 6 + s, s)

            scaled_act(act, "n_mlp0", lambda k: at("wo", "x", k + 5), "g_mlp",
                       split=lambda: split_hi(FIRST["wo"] + 5, 1))
            squares_act(act, "n_mlp0")
            act.dma_start(HE[:, 0:2].rearrange("p l t -> p (l t)")[:, 0:MASK_COLUMNS], a["level_masks"])\
                .then_inc(consts_in, 16)
            act.dma_start(reset[:], a["reset"]).then_inc(consts_in, 16)
            mlp_act("mlp0")
            act.wait_ge(s_("f_gain"), 1)
            for k in range(KD):
                act.wait_ge(*at("mlp0", "dn", 28 + k + 1))
                act.activation(XH[:, k], X[:, k], ACT.Copy, scale=small[:, 48 + k:49 + k]).then_inc(sig("n_hg", "hi"), 1)
            for k in range(KD):
                if k >= 2:
                    act.wait_ge(s_("f_add"), max(2 * k - 4, 2))
                act.activation(tmp[:, k % 2], X[:, k], ACT.Square).then_inc(s_("f_sq"), 1)
                act.activation(tmp[:, 2 + k % 2], X[:, k], ACT.Square, scale=col("g_final", k)).then_inc(s_("f_sq"), 1)
            act.wait_ge(s_("f_gain"), 2)
            act.activation(small[:, 88:96], small[:, 80:88], ACT.Sigmoid).then_inc(s_("lb_done"), 1)
            for n in range(2):
                act.wait_ge(s_("f_sums"), n + 1)
                act.activation(rst[:, n], ps[:, 7] if n == 0 else rst[:, 1], ACT.Ln, bias=col("eps"), scale=1.0 / D)\
                    .then_inc(s_("f_ln"), 1)
                act.wait_ge(s_("f_ln"), n + 1)
                act.activation(rst[:, n], rst[:, n], ACT.Exp, scale=-0.5).then_inc(s_("f_r"), 1)

            c = FIRST["hg"]

            def gates_act(h, before=True):
                act.wait_ge(s_("h_q0"), h + 1)
                act.activation(HSG[:, 0], HZ[:], ACT.Sigmoid).then_inc(s_("hq_sg"), 1)
                act.wait_ge(s_("h_f0"), h + 1)
                act.activation(HF[:], HF[:], ACT.Sigmoid).then_inc(s_("hf_sg"), 1)
                split_hi(2 * h + c + 2, 0)

            def out_gate_act(h, n):
                act.wait_ge(s_("h_g0"), h + 1)
                act.activation(HSG[:, 1], HGATE[:, n], ACT.Sigmoid).then_inc(s_("hg_sg"), 1)

            def decays_act(h, n):
                act.wait_ge(s_("hf_done"), h + 1)
                act.activation(HF[:], HF[:], ACT.Ln).then_inc(s_("h_ln"), 1)
                act.wait_ge(s_("h_scan"), h + 1)
                act.activation(HEB[:, n], HF[:], ACT.Exp).then_inc(s_("h_eb"), 1)
                act.wait_ge(s_("h_kd_arg"), h + 1)
                act.activation(HKD[:, n], HKD[:, n], ACT.Exp).then_inc(s_("h_kd_e"), 1)
                for l in range(len(LEVELS)):
                    act.wait_ge(s_("h_arg"), 14 * h + 2 * l + 2)
                    act.activation(HE[:, l], HE[:, l], ACT.Exp).then_inc(s_("h_e"), 1)
                split_hi(2 * h + c + 3, 1)

            def values_act(h, n):
                act.wait_ge(s_("h_vt"), h + 1)
                act.activation(HV[:, n].rearrange("p b v -> p (b v)"), ps[:, 3], ACT.Copy).then_inc(s_("h_v"), 1)

            def head_act(h, n, more=True):
                if more:
                    gates_act(h + 1)
                out_gate_act(h, n)
                act.wait_ge(s_("h_kt"), h + 1)
                act.activation(HKT[:].rearrange("p b d -> p (b d)"), ps[:, 7, 0:384], ACT.Copy).then_inc(s_("h_kt_c"), 1)
                if more:
                    decays_act(h + 1, 1 - n)
                act.wait_ge(s_("h_o"), h + 1)
                act.activation(tmp[:, 0], ps[:, 6], ACT.Square).then_inc(s_("h_sq"), 1)
                if more:
                    values_act(h + 1, 1 - n)
                act.wait_ge(s_("h_mean"), h + 1)
                act.activation(rst[:, 0], ps[:, 7], ACT.Ln, bias=col("eps"), scale=1.0 / P).then_inc(s_("h_ms"), 1)
                act.wait_ge(s_("h_ms"), h + 2)
                act.activation(rst[:, 1], rst[:, 0], ACT.Exp, scale=-0.5).then_inc(s_("h_inv"), 1)
                act.wait_ge(s_("h_t2"), h + 1)
                act.activation(OH[:, bass.ds(h, 1)], tmp[:, 1:2], ACT.Copy).then_inc(s_("oh_done"), 1)

            act.sem_inc(s_("h_ms"), 1)
            gates_act(0)
            decays_act(0, 0)
            values_act(0, 0)
            with act.Fori(0, HEADS_H // 2 - 1) as i:
                for n in range(2):
                    head_act(2 * i + n, n)
            head_act(6, 0)
            head_act(7, 1, more=False)

            ahead(FIRST["hwo"], 2)
            scaled_act(act, "n_mlp1", lambda k: at("hwo", "x", k + 5), "mlp_norm_2",
                       split=lambda: split_hi(FIRST["hwo"] + 5, 1))
            squares_act(act, "n_mlp1")
            act.dma_start(cos_t[:], a["cos"]).then_inc(consts_in, 16)
            act.dma_start(sin_t[:], a["sin"]).then_inc(consts_in, 16)
            act.dma_start(swap_t[:], a["swap"]).then_inc(consts_in, 16)
            act.dma_start(neg_t[:], a["neg"]).then_inc(consts_in, 16)
            mlp_act("mlp1")
            c = FIRST["kvq"]
            scaled_act(act, "n_mla", lambda k: at("mlp1", "dn", 28 + k + 1), "mla_norm_2")
            squares_act(act, "n_kv", inverse=False)
            split_hi(c + 2, 0)
            scaled_act(act, "n_kv", lambda k: at("mlp1", "dn", 28 + k + 1), "kv_in_norm_2", 0, XH2)
            split_hi(c + 3, 1)
            rest_act(act, "n_kv")

            def small_squares(n, W):
                for k in range(2):
                    act.wait_ge(*at(n, "c", k + 1))
                    act.activation(W[:, 4 + k], W[:, k], ACT.Square).then_inc(sig(n, "sq"), 1)

            def small_rest(n, W, hi):
                act.wait_ge(*at(n, "mean", 1))
                inverse_act(act, n, LORA, W[:, 6])
                for k in range(2):
                    act.wait_ge(*at(n, "t", k + 1))
                    act.activation(hi[:, k], W[:, 2 + k], ACT.Copy).then_inc(sig(n, "hi"), 1)

            small_squares("cq", CQ)
            split_hi(c + 4, 0)
            small_rest("cq", CQ, CQH)
            small_squares("ckv", CK)
            split_hi(c + 5, 1)
            small_rest("ckv", CK, CKH)

            c = FIRST["att"]
            act.sem_inc(att("a_exp", 0)[0], 4)
            act.sem_inc(att("a_ptc", 0)[0], 2)
            with act.Fori(0, 4) as i:
                for h in range(4):
                    act.wait_ge(halves, half_at(2 * i + c, 0))
                    act.activation(QN[:, h], ps[:, h], ACT.Copy).then_inc(att("qn_done", 0)[0], 1)
                for h in range(2):
                    act.wait_ge(halves, half_at(2 * i + c, 1))
                    act.activation(QR[:, 2 + h], ps[:, 4 + h], ACT.Copy).then_inc(att("qr_raw", 0)[0], 1)
                split_hi(2 * i + c + 2, 0)
                for h in range(4):
                    act.wait_ge(halves, half_at(2 * i + c + 1, 0))
                    act.activation(KN[:, h], ps[:, h], ACT.Copy).then_inc(att("kn_done", 0)[0], 1)
                for b in range(TB):
                    act.wait_ge(halves, half_at(2 * i + c + 1, 1))
                    act.activation(VT[:, b], ps[:, 4 + b], ACT.Copy).then_inc(att("vt_done", 0)[0], 1)
                split_hi(2 * i + c + 3, 1)

                def exps(h):
                    for b in range(TB):
                        act.wait_ge(*att("a_nmax", 16 * i + 4 * h + b + 1))
                        act.wait_ge(*att("a_pt", 16 * i + 4 * h + b + 1))
                        act.activation(PM[:, h % 2, rows(b)], ps[:, b, 0:(b + 1) * P], ACT.Exp,
                                       bias=small[:, 100 + b:101 + b], scale=SCALE,
                                       accum_out=small[:, 104 + b:105 + b]).then_inc(att("a_exp", 0)[0], 1)

                def turned(h):
                    for b in range(TB):
                        act.wait_ge(*att("a_pt", 16 * i + 4 * h + b + 9))
                        act.wait_ge(*att("a_pv", 4 * i + h + 1))
                        act.activation(PT[:, rows(b)], ps[:, 4 + b % 2, 0:(b + 1) * P], ACT.Copy).then_inc(att("a_ptc", 0)[0], 1)

                def out_hi(h):
                    act.wait_ge(*att("a_pv", 4 * i + h + 2))
                    act.activation(AH[:, bass.ds(4 * i + h, 1)], ps[:, 6:7], ACT.Copy).then_inc(att("ah_done", 0)[0], 1)

                exps(0)
                for h in range(4):
                    if h < 3:
                        exps(h + 1)
                    turned(h)
                    out_hi(h)

            ahead(FIRST["mwo"], 4)
            scaled_act(act, "n_mlp2", lambda k: at("mwo", "x", k + 5), "mlp_norm_2", 8, XH2,
                       split=lambda: split_hi(FIRST["mwo"] + 9, 1))
            squares_act(act, "n_mlp2")
            mlp_act("mlp2")
            for k in range(KD):
                act.wait_ge(*at("mlp2", "dn", 28 + k + 1))
                if k >= 4:
                    act.wait_ge(s_("y_add"), max(k - 4, 1))
                act.activation(tmp[:, k % 4], X[:, k], ACT.Square).then_inc(s_("y_sq"), 1)
                act.activation(X[:, k], X[:, k], ACT.Copy, scale=col("final_norm_2", k)).then_inc(s_("y_gain"), 1)
            act.wait_ge(s_("y_mean"), 1)
            act.activation(small[:, 96:100], ps[:, 7, 0:TB], ACT.Ln, bias=col("eps"), scale=1.0 / D)\
                .then_inc(s_("y_inv"), 1)
            act.wait_ge(s_("y_inv"), 1)
            act.activation(small[:, 100:104], small[:, 96:100], ACT.Exp, scale=-0.5).then_inc(s_("y_inv"), 1)
            act.wait_ge(s_("y_inv"), 2)
            for n in range(0, 2 * TB, 2):
                act.wait_ge(s_("y_turned"), n + 1)
                act.activation(y_half(n), ps[:, Y_BANKS[n]], ACT.Copy, scale=small[:, 100 + n % TB:101 + n % TB])\
                    .then_inc(s_("y_act"), 1)

        @block.vector
        def _(dve):
            dve.memset(XBR[:, :, 0:4], 0.0).then_inc(s_("pads"), 1)
            dve.wait_ge(consts_in, 32)
            lam = Count(dve, "lam_abs")
            chain = Count(dve, "chain")
            nl, ab, e, sm = small[:, 0:12], small[:, 12:24], small[:, 24:36], small[:, 36:48]
            zz, rr, ch = small[:, 48:60], small[:, 72:84], small[:, 60:72]
            lam.put(dve.tensor_scalar(nl, col("lam", 0, 12), -1.0, None, ALU.mult))
            lam.wait()
            lam.put(dve.tensor_tensor(ab, nl, col("lam", 0, 12), ALU.max))
            norm_dve(dve, "n_mix", "g_mix")

            lc = chain
            dve.wait_ge(s_("lam_e"), 1)
            lc.put(dve.tensor_scalar(sm, e, 2.0, None, ALU.add))
            lc.wait()
            lc.put(dve.reciprocal(rr, sm))
            lc.wait()
            lc.put(dve.tensor_tensor(zz, e, rr, ALU.mult))
            lc.wait()
            lc.put(dve.tensor_tensor(sm, zz, zz, ALU.mult))
            lc.wait()
            lc.put(dve.tensor_scalar(rr, sm, 1.0 / 17, None, ALU.mult))
            for n in range(15, 1, -2):
                lc.wait()
                lc.put(dve.scalar_tensor_tensor(rr, rr, 1.0 / n, sm, ALU.add, ALU.mult))
            lc.wait()
            lc.put(dve.scalar_tensor_tensor(rr, rr, 1.0, zz, ALU.add, ALU.mult))
            lc.put(dve.tensor_scalar(nl, nl, 0.0, -4.0, ALU.max, ALU.mult))
            lc.wait()
            dve.scalar_tensor_tensor(ch, rr, -8.0, nl, ALU.mult, ALU.add).then_inc(s_("ch_done"), 1)
            dve.wait_ge(s_("ch_done"), 1)
            dve.tensor_scalar(e, ch, 2.0, None, ALU.mult).then_inc(s_("ch_done"), 1)

            dve.wait_ge(*at("n_mix", "lo", KD))
            dve.memset(UP[:, :, 0:PAD], 0.0).then_inc(s_("pads"), 1)
            dve.wait_ge(s_("pads"), 2)
            cs = s_("conv")
            ev = s_("z_evac")

            def conv_a(i):
                for n in range(2):
                    t = bass.ds(2 * i + n, 1)
                    dve.wait_ge(ev, 4 * i + 7 + n)
                    dve.tensor_tensor(UP[:, n:n + 1, PAD:PAD + T], CO[:, t], GA[:, t], ALU.mult).then_inc(s_("u_done"), 1)
                base = i * (2 * TAPS_A + 2)
                for tap in range(TAPS_A):
                    for n in range(2):
                        acc = CO[:, bass.ds(2 * i + n, 1)] if tap % 2 == 0 else tmp[:, n:n + 1]
                        src = UP[:, n:n + 1, tap:tap + T]
                        w = dcol("conv_a_w", (2 * i + n) * TAPS_A + tap)
                        if tap == 0:
                            dve.wait_ge(s_("u_done"), 2 * i + n + 1)
                            dve.tensor_scalar(acc, src, w, dcol("conv_a_b", 2 * i + n), ALU.mult, ALU.add).then_inc(cs, 1)
                        elif tap == 1:
                            dve.tensor_scalar(acc, src, w, None, ALU.mult).then_inc(cs, 1)
                        else:
                            dve.wait_ge(cs, base + 2 * (tap - 2) + n + 1)
                            dve.scalar_tensor_tensor(acc, src, w, acc, ALU.mult, ALU.add).then_inc(cs, 1)
                for n in range(2):
                    t = bass.ds(2 * i + n, 1)
                    dve.wait_ge(cs, base + 2 * (TAPS_A - 1) + n + 1)
                    dve.tensor_tensor(CO[:, t], CO[:, t], tmp[:, n:n + 1], ALU.add).then_inc(cs, 1)
                dve.wait_ge(cs, base + 2 * TAPS_A + 2)

            with dve.Fori(0, 3) as i:
                conv_a(i)

            with dve.Fori(0, 3) as i:
                for k in range(TAPS_B):
                    for j in range(4):
                        t = 4 * i + j
                        src = XBR[:, bass.ds(t, 1), 1 + k:1 + k + T]
                        w = dcol("conv_b_w", t * 4 + k)
                        acc = V[:, bass.ds(t, 1)]
                        part = s_("v_part")
                        if k == 0:
                            dve.wait_ge(ev, t + 16 + 5)
                            dve.tensor_scalar(acc, src, w, dcol("conv_b_b", t), ALU.mult, ALU.add).then_inc(part, 1)
                        else:
                            dve.wait_ge(part, 12 * i + 4 * (k - 1) + j + 1)
                            dve.scalar_tensor_tensor(acc, src, w, acc, ALU.mult, ALU.add)\
                                .then_inc(part if k < TAPS_B - 1 else s_("v_done"), 1)

            conv_a(3)

            def gelu_dve(g):
                for j in range(3):
                    w = ps[:, 4 + j]
                    dve.wait_ge(s_("gb_zz"), 3 * g + j + 1)
                    dve.tensor_scalar(w, w, 0.044715, 1.0, ALU.mult, ALU.add).then_inc(s_("gb_q"), 1)
                for j in range(3):
                    w = ps[:, 4 + j]
                    dve.wait_ge(s_("gb_q"), 3 * g + j + 1)
                    dve.tensor_tensor(w, w, G[:, 3 * g + j], ALU.mult).then_inc(s_("gb_p"), 1)
                for j in range(3):
                    dve.wait_ge(s_("gb_th"), 3 * g + j + 1)
                    dve.scalar_tensor_tensor(G[:, 3 * g + j], ps[:, 4 + j], 1.0, G[:, 3 * g + j], ALU.add, ALU.mult)\
                        .then_inc(s_("gb_g"), 1)

            for g in range(3):
                gelu_dve(g)
            dve.wait_ge(s_("mu_done"), 1)
            for k in range(KD):
                dve.tensor_tensor(CO[:, k], CO[:, k], rst[:, 1], ALU.subtract).then_inc(s_("xc_done"), 1)
            for k in range(1, KD):
                dve.wait_ge(s_("xc_sq"), k + 1)
                if k >= 2:
                    dve.wait_ge(s_("xc_add"), k - 1)
                dve.tensor_tensor(rst[:, 0], rst[:, 0] if k >= 2 else tmp[:, 0], tmp[:, k % 4], ALU.add)\
                    .then_inc(s_("xc_add"), 1)

            gelu_dve(3)
            dve.wait_ge(s_("ln_inv"), 2)
            for k in range(KD):
                dve.scalar_tensor_tensor(CO[:, k], CO[:, k], col("ln_g", k), rst[:, 1], ALU.mult, ALU.mult)\
                    .then_inc(s_("ln_y"), 1)
            for k in range(KD):
                dve.wait_ge(s_("ln_sg"), k + 1)
                dve.scalar_tensor_tensor(CO[:, k], CO[:, k], col("ln_b", k), tmp[:, k % 4], ALU.add, ALU.mult)\
                    .then_inc(s_("ln_u"), 1)

            c = FIRST["bandya"]
            def gate_input(i):
                for j in range(3):
                    dve.tensor_scalar(VH[:, j:j + 1], V[:, bass.ds(3 * i + j, 1)], 1.0, None, ALU.mult).then_inc(s_("vh_done"), 1)
                for j in range(3):
                    dve.wait_ge(s_("vh_done"), 3 * i + j + 1)
                    dve.tensor_tensor(VL[:, j:j + 1], V[:, bass.ds(3 * i + j, 1)], VH[:, j:j + 1].bitcast(F32),
                                      ALU.subtract).then_inc(s_("vl_done"), 1)

            dve.sem_inc(s_("lru_done"), 3)
            dve.sem_inc(s_("ma_done"), 2)
            dve.wait_ge(s_("ln_u"), KD)
            gate_input(0)
            for k in range(KD):
                dve.wait_ge(s_("uh_done"), k + 1)
                dve.tensor_tensor(XL[:, k], CO[:, k], XH[:, k].bitcast(F32), ALU.subtract).then_inc(s_("ul_done"), 1)

            def group(i, last=False):
                tiles = [(j, bass.ds(3 * i + j, 1), 3 * i + j + 1) for j in range(3)]
                dve.wait_ge(halves, half_at(2 * i + c))
                if not last:
                    gate_input(i + 1)
                for j, t, n in tiles:
                    dve.wait_ge(s_("lru_x"), n)
                    dve.wait_ge(s_("vl_done"), n)
                    dve.tensor_tensor(V[:, t], LR[:, 3 + j:4 + j], V[:, t], ALU.mult).then_inc(s_("lru_iv"), 1)
                for j in range(2):
                    dve.wait_ge(halves, half_at(2 * i + c + 1, j))
                    m = M[:, bass.ds(2 * i + j, 1)]
                    dve.tensor_tensor(m, m, ps[:, 6 + j:7 + j], ALU.mult).then_inc(s_("ma_done"), 1)
                for j, t, n in tiles:
                    dve.wait_ge(s_("lru_e"), n)
                    dve.wait_ge(s_("lru_s"), n)
                    dve.scalar_tensor_tensor(LR[:, 3 + j], LR[:, j], 1.0, LR[:, 3 + j], ALU.add, ALU.mult)\
                        .then_inc(s_("lru_m"), 1)
                for j, t, n in tiles:
                    dve.wait_ge(s_("lru_m"), n)
                    dve.memset(LR[:, 3 + j, 0:1], 1.0).then_inc(s_("lru_m1"), 1)
                for j, t, n in tiles:
                    dve.wait_ge(s_("lru_m1"), n)
                    dve.wait_ge(s_("lru_iv"), n)
                    dve.tensor_tensor(V[:, t], V[:, t], LR[:, 3 + j:4 + j], ALU.mult).then_inc(s_("lru_b"), 1)
                for j, t, n in tiles:
                    dve.wait_ge(s_("lru_b"), n)
                    v = V[:, t].rearrange("p a t -> p (a t)")
                    dve.tensor_tensor_scan(v, LR[:, j], v, 0.0, ALU.mult, ALU.add).then_inc(s_("lru_done"), 1)
                for j, t, n in tiles:
                    dve.wait_ge(s_("lru_done"), 3 * i + j + 4)
                    dve.scalar_tensor_tensor(G[:, t], G[:, t], 0.5, V[:, t], ALU.mult, ALU.mult).then_inc(s_("vg_t"), 1)
                for j, t, n in tiles:
                    dve.wait_ge(s_("vg_t"), n)
                    dve.tensor_scalar(VGH[:, t], G[:, t], 1.0, None, ALU.mult).then_inc(s_("vg_hi"), 1)
                for j, t, n in tiles:
                    dve.wait_ge(s_("vg_hi"), n)
                    dve.tensor_tensor(VGL[:, t], G[:, t], VGH[:, t].bitcast(F32), ALU.subtract).then_inc(s_("vg_lo"), 1)

            with dve.Fori(0, 3) as i:
                group(i)
            group(3, last=True)

            dve.wait_ge(s_("vg_lo"), RT)
            dve.sem_inc(s_("m_done"), 4)
            dve.sem_inc(s_("yb_evac"), 4)
            c = FIRST["bo"]
            with dve.Fori(0, 2) as i:
                for j in range(4):
                    t = bass.ds(4 * i + j, 1)
                    dve.wait_ge(halves, half_at(4 * i + c + j))
                    dve.tensor_tensor(SBG[:, t], ps[:, BO_BANKS[j]:BO_BANKS[j] + 1], SBG[:, t], ALU.mult)\
                        .then_inc(s_("yb_evac"), 1)
                    dve.wait_ge(s_("yb_evac"), 4 * i + j + 5)
                    dve.tensor_tensor(M[:, t], M[:, t], SBG[:, t], ALU.add).then_inc(s_("m_done"), 1)
                    dve.wait_ge(s_("mh_done"), 4 * i + j + 1)
                    dve.tensor_tensor(ML[:, t], M[:, t], MH[:, t].bitcast(F32), ALU.subtract).then_inc(s_("ml_done"), 1)

            def residual(n, c, per, banks_free):
                xs = sig(n, "x")
                dve.wait_ge(*banks_free)
                dve.sem_inc(xs, 4)
                with dve.Fori(0, 2) as i:
                    for j in range(4):
                        dve.wait_ge(halves, half_at(2 * i + c + j // 2, j % 2) if per == 2 else half_at(4 * i + c + j))
                        dve.tensor_tensor(X[:, bass.ds(4 * i + j, 1)], X[:, bass.ds(4 * i + j, 1)], ps[:, j:j + 1], ALU.add)\
                            .then_inc(xs, 1)

            def mlp_dve(n):
                c = FIRST[n]
                with dve.Fori(0, 4) as q:
                    with dve.Fori(0, 2) as i:
                        for j in range(4):
                            f = 8 * q + 4 * i + j
                            t, t2 = tmp[:, j % 2:j % 2 + 1], tmp[:, 2 + j % 2:3 + j % 2]
                            dve.wait_ge(halves, half_at(8 * q + 2 * i + c + j // 2, j % 2))
                            dve.wait_ge(*at(n, "fl", f + 3))
                            dve.scalar_tensor_tensor(t, ps[:, j:j + 1], 0.0, rst[:, 1:2], ALU.max, ALU.mult)\
                                .then_inc(sig(n, "t"), 1)
                            dve.wait_ge(*at(n, "t", f + 5))
                            dve.tensor_tensor(t2, t, t, ALU.mult).then_inc(sig(n, "sq"), 1)
                            dve.wait_ge(*at(n, "sq", f + 1))
                            dve.wait_ge(*at(n, "fh", f + 1))
                            dve.tensor_tensor(FL[:, bass.ds(4 * i + j, 1)], t2, FH[:, bass.ds(4 * i + j, 1)].bitcast(F32),
                                              ALU.subtract).then_inc(sig(n, "fl"), 1)
                    with dve.Fori(0, 2) as i:
                        for j in range(4):
                            dve.wait_ge(halves, half_at(8 * q + 2 * i + c + 4 + j // 2, j % 2))
                            dve.tensor_tensor(X[:, bass.ds(4 * i + j, 1)], X[:, bass.ds(4 * i + j, 1)], ps[:, j:j + 1],
                                              ALU.add).then_inc(sig(n, "dn"), 1)

            def scaled(n, gain, off=0, xh=XH, xl=XL):
                m = n[2:]
                dve.sem_inc(sig(m, "fl"), 4)
                dve.sem_inc(sig(m, "dn"), 4)
                dve.sem_inc(sig(m, "t"), 4)
                scaled_dve(dve, n, gain, off, xh, xl)
                squares_dve(dve, n)

            residual("wo", FIRST["wo"], 2, (s_("yb_evac"), 4 + KD))
            scaled("n_mlp0", "g_mlp")
            mlp_dve("mlp0")

            dve.tensor_tensor(small[:, 48:56], col("g_final", 0, 8), col("hgrn_norm_2", 0, 8), ALU.mult)\
                .then_inc(s_("f_gain"), 1)
            dve.tensor_tensor(small[:, 80:88], col("hgrn_lb_logits_2", 0, 8), col("hgrn_lb_logits_2", 8, 8), ALU.subtract)\
                .then_inc(s_("f_gain"), 1)
            dve.memset(HP[:], 0.0).then_inc(s_("h_ready"), 1)
            dve.wait_ge(s_("f_gain"), 1)
            for k in range(KD):
                dve.wait_ge(*at("n_hg", "hi", k + 1))
                dve.scalar_tensor_tensor(XL[:, k], X[:, k], small[:, 48 + k:49 + k], XH[:, k].bitcast(F32), ALU.mult,
                                         ALU.subtract).then_inc(sig("n_hg", "lo"), 1)
            for k in range(1, KD):
                for n, acc in enumerate((HZ, HF)):
                    dve.wait_ge(s_("f_sq"), 2 * k + n + 1)
                    if k >= 2:
                        dve.wait_ge(s_("f_add"), 2 * (k - 2) + n + 1)
                    dve.tensor_tensor(acc[:], acc[:] if k >= 2 else tmp[:, 2 * n], tmp[:, 2 * n + k % 2], ALU.add)\
                        .then_inc(s_("f_add"), 1)
            dve.wait_ge(consts_in, 32 + 32)
            mk = HE[:, 0:2].rearrange("p l t -> p (l t)")
            dve.tensor_copy(masks[:, 0:7 * 256].rearrange("p (l c t) -> p l c t", l=7, c=TB),
                            mk[:, 0:7 * 64].rearrange("p (l c t) -> p l c t", l=7, c=1).to_broadcast([P, 7, TB, 64]))\
                .then_inc(s_("h_ready"), 1)
            dve.tensor_copy(masks[:, 7 * 256:9 * 256].rearrange("p (c t) -> p c t", c=TB),
                            mk[:, 7 * 64:MASK_COLUMNS].rearrange("p (c t) -> p c t", c=1).to_broadcast([P, TB, P]))\
                .then_inc(s_("h_ready"), 1)
            dve.wait_ge(s_("lb_done"), 1)
            dve.tensor_scalar(small[:, 112:120], small[:, 88:96], -1.0, 1.0, ALU.mult, ALU.add).then_inc(s_("h_ready"), 1)
            fr = chain
            dve.wait_ge(s_("f_r"), 1)
            dve.wait_ge(s_("f_mm"), 2)
            fr.put(dve.tensor_tensor(rst[:, 1], ps[:, 6], rst[:, 0], ALU.mult))
            fr.wait()
            dve.tensor_tensor(rst[:, 1], rst[:, 1], rst[:, 0], ALU.mult).then_inc(s_("f_sums"), 1)
            dve.wait_ge(s_("f_r"), 2)
            fr.put(dve.tensor_tensor(HR[:], rst[:, 0], rst[:, 1], ALU.mult))
            fr.wait()
            dve.wait_ge(s_("h_ready"), 4)
            c = FIRST["hg"]

            def gates_dve(h):
                dve.wait_ge(halves, half_at(2 * h + c, 1))
                dve.tensor_tensor(HZ[:], ps[:, 0], HR[:], ALU.mult).then_inc(s_("h_q0"), 1)
                dve.tensor_tensor(HF[:], ps[:, 1], HR[:], ALU.mult).then_inc(s_("h_f0"), 1)

            def levels_dve(h):
                for l in range(len(LEVELS) + 1):
                    dve.wait_ge(s_("h_g"), 8 * h + l + 1)
                    if l:
                        dve.wait_ge(s_("h_g_free"), 8 * h + l)
                    dve.sem_inc(s_("h_g_seen"), 1)
                    if l == 0:
                        dve.copy_predicated(HP[:], masks[:, 7 * 256:9 * 256], ps[:, 6]).then_inc(s_("h_g_free"), 1)
                    else:
                        m = LEVELS[l - 1]
                        dve.copy_predicated(
                            HP[:].rearrange("p (g u t) -> p g u t", u=2, t=m)[:, :, 1],
                            masks[:, (l - 1) * 256:l * 256].rearrange("p (g t) -> p g t", t=m),
                            ps[:, 4 + (l - 1) % 2, 0:256].rearrange("p (g t) -> p g t", t=m)).then_inc(s_("h_g_free"), 1)

            def decays_dve(h, n):
                dve.wait_ge(s_("hq_sg"), h + 1)
                dve.tensor_tensor(HQ[:], HZ[:], HSG[:, 0], ALU.mult).then_inc(s_("hq_done"), 1)
                hc = s_("h_f")
                dve.wait_ge(s_("hf_sg"), h + 1)
                dve.tensor_scalar(HF[:], HF[:], small[:, bass.ds(h + 112, 1)], small[:, bass.ds(h + 88, 1)],
                                  ALU.mult, ALU.add).then_inc(hc, 1)
                dve.wait_ge(hc, 2 * h + 1)
                dve.tensor_scalar(HK[:], HF[:], -1.0, 1.0, ALU.mult, ALU.add).then_inc(hc, 1)
                dve.wait_ge(hc, 2 * h + 2)
                dve.tensor_scalar(HF[:], HF[:], 2.0 ** -64, None, ALU.max).then_inc(s_("hf_done"), 1)
                dve.wait_ge(s_("h_ln"), h + 1)
                b = HF[:]
                dve.tensor_tensor_scan(b, reset[:], b, 0.0, ALU.mult, ALU.add).then_inc(s_("h_scan"), 1)
                dve.wait_ge(s_("h_scan"), h + 1)
                b4 = b.rearrange("p (c t) -> p c t", t=P)
                last = b4[:, :, P - 1:P].to_broadcast([P, TB, P])
                dve.tensor_tensor(HKD[:, n].rearrange("p (c t) -> p c t", t=P), last, b4, ALU.subtract)\
                    .then_inc(s_("h_kd_arg"), 1)
                for l, m in enumerate(LEVELS):
                    bv = b.rearrange("p (g u t) -> p g u t", u=2, t=m)
                    ev = HE[:, l].rearrange("p (g u t) -> p g u t", u=2, t=m)
                    ref = bv[:, :, 0, m - 1:m].to_broadcast([P, T // (2 * m), m])
                    dve.tensor_tensor(ev[:, :, 0], ref, bv[:, :, 0], ALU.subtract).then_inc(s_("h_arg"), 1)
                    dve.tensor_tensor(ev[:, :, 1], bv[:, :, 1], ref, ALU.subtract).then_inc(s_("h_arg"), 1)

            def rest_dve(h, n):
                dve.wait_ge(halves, half_at(2 * h + c + 1, 1))
                dve.tensor_tensor(HVF[:], ps[:, 3], HR[:], ALU.mult).then_inc(s_("h_vf"), 1)
                dve.tensor_tensor(HGATE[:, n], ps[:, 2], HR[:], ALU.mult).then_inc(s_("h_g0"), 1)

            def decayed_dve(h, n):
                dve.wait_ge(s_("hq_done"), h + 1)
                dve.wait_ge(s_("h_eb"), h + 1)
                dve.tensor_tensor(HQD[:, n], HQ[:], HEB[:, n], ALU.mult).then_inc(s_("h_qd"), 1)
                dve.wait_ge(s_("h_kd_e"), h + 1)
                dve.tensor_tensor(HKD[:, n], HKD[:, n], HK[:], ALU.mult).then_inc(s_("h_kd"), 1)
                for l, m in enumerate(LEVELS):
                    ev = HE[:, l].rearrange("p (g u t) -> p g u t", u=2, t=m)
                    qv = HQ[:].rearrange("p (g u t) -> p g u t", u=2, t=m)
                    kv = HK[:].rearrange("p (g u t) -> p g u t", u=2, t=m)
                    dve.wait_ge(s_("h_e"), 7 * h + l + 1)
                    dve.tensor_tensor(ev[:, :, 0], ev[:, :, 0], kv[:, :, 0], ALU.mult).then_inc(s_("h_qk"), 1)
                    dve.tensor_tensor(ev[:, :, 1], ev[:, :, 1], qv[:, :, 1], ALU.mult).then_inc(s_("h_qk"), 1)

            def head_dve(h, n, more=True):
                if more:
                    gates_dve(h + 1)
                levels_dve(h)
                dve.wait_ge(s_("hg_sg"), h + 1)
                dve.tensor_tensor(HGATE[:, n], HGATE[:, n], HSG[:, 1], ALU.mult).then_inc(s_("hg_done"), 1)
                if more:
                    decays_dve(h + 1, 1 - n)
                    rest_dve(h + 1, 1 - n)
                dve.wait_ge(s_("h_st"), h + 1)
                for b_ in range(3):
                    st = ps[:, 7, b_ * P:(b_ + 1) * P]
                    if b_ == 0:
                        dve.tensor_copy(HS[:, 0], st).then_inc(s_("h_s"), 1)
                    else:
                        dve.wait_ge(s_("h_s"), 3 * h + b_)
                        dve.scalar_tensor_tensor(HS[:, b_], HS[:, b_ - 1], HEB[:, n, b_ * P + P - 1:b_ * P + P], st,
                                                 ALU.mult, ALU.add).then_inc(s_("h_s"), 1)
                if more:
                    decayed_dve(h + 1, 1 - n)
                dve.wait_ge(s_("h_inv"), h + 1)
                dve.scalar_tensor_tensor(tmp[:, 1], ps[:, 6], col("hgrn_g_norm_2"), rst[:, 1], ALU.mult, ALU.mult)\
                    .then_inc(s_("h_t1"), 1)
                dve.wait_ge(s_("h_t1"), h + 2)
                dve.tensor_tensor(tmp[:, 1], tmp[:, 1], HGATE[:, n], ALU.mult).then_inc(s_("h_t2"), 1)
                dve.wait_ge(s_("oh_done"), h + 1)
                dve.tensor_tensor(OL[:, bass.ds(h, 1)], tmp[:, 1:2], OH[:, bass.ds(h, 1)].bitcast(F32), ALU.subtract)\
                    .then_inc(s_("ho_done"), 1)

            dve.sem_inc(s_("h_t1"), 1)
            gates_dve(0)
            decays_dve(0, 0)
            rest_dve(0, 0)
            decayed_dve(0, 0)
            chain.at += KD
            for k in range(KD):
                dve.scalar_tensor_tensor(X[:, k], X[:, k], col("g_final", k), rst[:, 0], ALU.mult, ALU.mult)\
                    .then_inc(chain.sem, 1)
            with dve.Fori(0, HEADS_H // 2 - 1) as i:
                for n in range(2):
                    head_dve(2 * i + n, n)
            head_dve(6, 0)
            head_dve(7, 1, more=False)

            residual("hwo", FIRST["hwo"], 2, (s_("ho_done"), HEADS_H))
            scaled("n_mlp1", "mlp_norm_2")
            mlp_dve("mlp1")
            scaled_dve(dve, "n_mla", "mla_norm_2")
            squares_dve(dve, "n_kv", inverse=False)
            scaled_dve(dve, "n_kv", "kv_in_norm_2", 0, XH2, XL2)
            dve.wait_ge(*at("n_kv", "inv", 1))
            c = FIRST["kvq"]

            def small_copy(n, W, bank, ready):
                for k in range(2):
                    dve.wait_ge(halves, ready[k])
                    dve.tensor_tensor(W[:, k], ps[:, bank + k], rst[:, 1], ALU.mult).then_inc(sig(n, "c"), 1)

            def small_norm_dve(n, W, gain, hi, lo):
                dve.wait_ge(*at(n, "inv", 1))
                for k in range(2):
                    dve.scalar_tensor_tensor(W[:, 2 + k], W[:, k], col(gain, k), W[:, 6], ALU.mult, ALU.mult)\
                        .then_inc(sig(n, "t"), 1)
                for k in range(2):
                    dve.wait_ge(*at(n, "hi", k + 1))
                    dve.tensor_tensor(lo[:, k], W[:, 2 + k], hi[:, k].bitcast(F32), ALU.subtract).then_inc(sig(n, "lo"), 1)

            small_copy("cq", CQ, 4, [half_at(c), half_at(c + 1)])
            small_copy("ckv", CK, 0, [half_at(c + 2, 0), half_at(c + 2, 1)])
            small_norm_dve("cq", CQ, "mla_q_norm_2", CQH, CQL)
            dve.wait_ge(halves, half_at(c + 3))
            dve.tensor_tensor(QR[:, 2], ps[:, 2], rst[:, 1], ALU.mult).then_inc(s_("kr_raw"), 1)
            dve.wait_ge(consts_in, 32 + 32 + 64)
            dve.wait_ge(s_("kr_raw"), 1)
            kc = chain
            kc.put(dve.tensor_tensor(KR[:], QR[:, 2], cos_t[:], ALU.mult))
            dve.wait_ge(s_("kr_swap"), 1)
            kc.put(dve.tensor_tensor(CK[:, 7], ps[:, 3], sin_t[:], ALU.mult))
            kc.wait()
            kc.put(dve.tensor_tensor(KR[:], KR[:], CK[:, 7], ALU.add))
            kc.wait()
            small_norm_dve("ckv", CK, "kv_norm_2", CKH, CKL)

            dve.wait_ge(*at("ckv", "lo", 2))
            dve.wait_ge(*at("cq", "lo", 2))
            dve.sem_inc(att("al_done", 0)[0], 1)
            with dve.Fori(0, 4) as i:
                for h in range(2):
                    dve.wait_ge(*att("qr_raw", 2 * i + h + 1))
                    dve.wait_ge(*att("qr_swap", 2 * i + h + 1))
                    dve.tensor_tensor(rst[:, 0], ps[:, 6 + h], sin_t[:], ALU.mult).then_inc(att("qr_a", 0)[0], 1)
                    dve.tensor_tensor(QR[:, h], QR[:, 2 + h], cos_t[:], ALU.mult).then_inc(att("qr_a", 0)[0], 1)
                    dve.wait_ge(*att("qr_a", 4 * i + 2 * h + 2))
                    dve.tensor_tensor(QR[:, h], QR[:, h], rst[:, 0], ALU.add).then_inc(att("qr_done", 0)[0], 1)
                    dve.wait_ge(*att("qr_done", 2 * i + h + 1))

                def row_max(h):
                    for b in range(TB):
                        t = 16 * i + 4 * h + b
                        dg = ps[:, b, b * P:(b + 1) * P]
                        dve.wait_ge(*att("a_qk", t + 1))
                        dve.tensor_tensor(dg, dg, neg_t[:], ALU.add).then_inc(att("a_mask", 0)[0], 1)
                        dve.wait_ge(*att("a_mask", t + 1))
                        dve.tensor_reduce(small[:, 96 + b:97 + b], ps[:, b, 0:(b + 1) * P], AX, ALU.max)\
                            .then_inc(att("a_max", 0)[0], 1)
                        dve.wait_ge(*att("a_max", t + 1))
                        dve.tensor_scalar(small[:, 100 + b:101 + b], small[:, 96 + b:97 + b], -SCALE, None, ALU.mult)\
                            .then_inc(att("a_nmax", 0)[0], 1)

                def scale_rows(h):
                    for b in range(TB):
                        t = 16 * i + 4 * h + b
                        dve.wait_ge(*att("a_exp", t + 5))
                        dve.reciprocal(small[:, 108 + b:109 + b], small[:, 104 + b:105 + b]).then_inc(att("a_rs", 0)[0], 1)
                        dve.wait_ge(*att("a_rs", t + 1))
                        dve.tensor_scalar(PM[:, h % 2, rows(b)], PM[:, h % 2, rows(b)], small[:, 108 + b:109 + b], None,
                                          ALU.mult).then_inc(att("a_pm", 0)[0], 1)

                row_max(0)
                scale_rows(0)
                for h in range(4):
                    if h < 3:
                        row_max(h + 1)
                        scale_rows(h + 1)
                    dve.wait_ge(*att("ah_done", 4 * i + h + 1))
                    dve.tensor_tensor(AL[:, bass.ds(4 * i + h, 1)], ps[:, 6:7], AH[:, bass.ds(4 * i + h, 1)].bitcast(F32),
                                      ALU.subtract).then_inc(att("al_done", 0)[0], 1)

            residual("mwo", FIRST["mwo"], 1, att("al_done", 1 + HEADS_M))
            scaled("n_mlp2", "mlp_norm_2", 8, XH2, XL2)
            mlp_dve("mlp2")
            for k in range(1, KD):
                dve.wait_ge(s_("y_sq"), k + 1)
                if k >= 2:
                    dve.wait_ge(s_("y_add"), k - 1)
                dve.tensor_tensor(rst[:, 0], rst[:, 0] if k >= 2 else tmp[:, 0], tmp[:, k % 4], ALU.add)\
                    .then_inc(s_("y_add"), 1)
            dve.wait_ge(s_("y_inv"), 2)
            for n in range(1, 2 * TB, 2):
                dve.wait_ge(s_("y_turned"), n + 1)
                dve.tensor_scalar(y_half(n), ps[:, Y_BANKS[n]], small[:, 100 + n % TB:101 + n % TB], None, ALU.mult)\
                    .then_inc(s_("y_dve"), 1)

        @block.tensor
        def _(pe):
            pe.sem_inc(halves, 4)
            pe.wait_ge(ident_in, 16)
            for k in range(KD):
                pe.wait_ge(x_in[k // 4], 16)
                if k >= 4:
                    pe.wait_ge(s_("x_fm"), k - 3)
                for b in range(TB):
                    mm = pe.transpose(ps[:, k % 4, b * P:(b + 1) * P], x_tm[:, b, k * P:(k + 1) * P], ident[:])
                mm.then_inc(s_("x_turned"), 1)

            def product(dst, his, los, xh, xl, start=True, stop=True):
                n = len(his)
                for k in range(n):
                    pe.matmul(dst, his[k], xh[k], start=start and k == 0, stop=False)
                    pe.matmul(dst, his[k], xl[k], start=False, stop=False)
                    mm = pe.matmul(dst, los[k], xh[k], start=False, stop=stop and k == n - 1)
                return mm

            def product_x(dst, his, los, xh, xl, start=True, stop=True):
                n = len(his)
                for k in range(n):
                    pe.matmul(dst, xh[k], his[k], start=start and k == 0, stop=False)
                    pe.matmul(dst, xh[k], los[k], start=False, stop=False)
                    mm = pe.matmul(dst, xl[k], his[k], start=False, stop=stop and k == n - 1)
                return mm

            def tiles(t, n=KD, first=0):
                return [t[:, first + k] for k in range(n)]

            def chunk_in(c):
                pe.wait_ge(lo_done, c + 3)

            def half8(s, n, bank, xh, xl):
                product(ps[:, bank], w8(w_hi, s, n), w8(w_lo, s, n), tiles(xh), tiles(xl)).then_inc(halves, 1)

            def pair(s, bank, xh, xl, ready=None):
                h = [w8(w_hi, s, n) for n in range(2)]
                l = [w8(w_lo, s, n) for n in range(2)]
                for k in range(KD):
                    if ready is not None:
                        pe.wait_ge(*ready(k))
                    for n in range(2):
                        dst = ps[:, bank + n]
                        pe.matmul(dst, h[n][k], xh[:, k], start=k == 0, stop=False)
                        pe.matmul(dst, h[n][k], xl[:, k], start=False, stop=False)
                        mm = pe.matmul(dst, l[n][k], xh[:, k], start=False, stop=k == KD - 1)
                        if k == KD - 1:
                            mm.then_inc(halves, 1)

            pe.wait_ge(consts_in, 32)
            norm_pe(pe, "n_mix")

            def plain(c, iters, ev, xh, xl, ready=None):
                with pe.Fori(0, iters) as i:
                    for j in range(2):
                        chunk_in(2 * i + c + j)
                        pe.wait_ge(*ev(4 * i + 2 * j + 2))
                        if j == 0 and ready is not None:
                            pair(0, 0, xh, xl, ready)
                        else:
                            half8(j, 0, 2 * j, xh, xl)
                            half8(j, 1, 2 * j + 1, xh, xl)

            def z_bank(first):
                return lambda v: (s_("z_evac"), v + first)

            plain(FIRST["ug"], 4, z_bank(0), XH, XL, lambda k: at("n_mix", "lo", k + 1))
            plain(FIRST["xb"], 3, z_bank(16), XH, XL)
            plain(FIRST["sb"], 2, z_bank(28), XH, XL)
            plain(FIRST["gb"], 3, z_bank(36), XH, XL)

            pe.wait_ge(s_("conv"), KD * (TAPS_A + 1))
            for k in range(KD):
                mm = pe.matmul(ps[:, 7], ones[:], CO[:, k], start=k == 0, stop=k == KD - 1)
            mm.then_inc(s_("mu_mm"), 1)
            c = FIRST["sa"]
            for i in range(2):
                for j in range(2):
                    chunk_in(2 * i + c + j)
                    pe.wait_ge(s_("z_evac"), 48 + 4 * i + 2 * j + 2)
                    half8(j, 0, 2 * j, XH, XL)
                    half8(j, 1, 2 * j + 1, XH, XL)
                if i == 0:
                    pe.wait_ge(s_("xc_add"), KD - 1)
                    pe.matmul(ps[:, 7], ones[:], rst[:, 0], start=True, stop=True).then_inc(s_("var_mm"), 1)

            c = FIRST["bandya"]
            pe.wait_ge(s_("ln_inv"), 1)
            pe.wait_ge(s_("z_evac"), 4 + 56)
            pe.wait_ge(s_("gb_g"), RT)

            def band_ya(i, banks_free=None):
                chunk_in(2 * i + c)
                pe.wait_ge(s_("vl_done"), 3 * i + 3)
                if banks_free is not None:
                    pe.wait_ge(*banks_free)
                for gate in range(2):
                    for o in range(3):
                        ks = [n for n, (r, q) in enumerate(BAND) if q == o]
                        wt = [[t[:, 0, (7 * gate + n) * P:(7 * gate + n + 1) * P] for n in ks] for t in (w_hi, w_lo)]
                        mm = product(ps[:, 3 * gate + o], wt[0], wt[1],
                                     [VH[:, BAND[n][0]] for n in ks], [VL[:, BAND[n][0]] for n in ks])
                    mm.then_inc(halves, 1)
                chunk_in(2 * i + c + 1)
                pe.wait_ge(s_("ma_done"), 2 * i + 2)
                pair(1, 6, XH, XL, lambda k: (s_("ul_done"), k + 1))

            band_ya(0)
            with pe.Fori(1, 4) as i:
                band_ya(i, (s_("lru_r"), 3 * i))

            def single(c, kt, ev, xh, xl, banks=(0, 1, 2, 3), ready=None):
                with pe.Fori(0, 2) as i:
                    for j in range(4):
                        chunk_in(4 * i + c + j)
                        pe.wait_ge(*ev(4 * i + j + 1))
                        h, l = w1(w_hi, j % 2, kt), w1(w_lo, j % 2, kt)
                        for k in range(kt):
                            if ready is not None and j == 0:
                                pe.wait_ge(*ready(k))
                            mm = product(ps[:, banks[j]], [h[k]], [l[k]], [xh[:, k]], [xl[:, k]],
                                         start=k == 0, stop=k == kt - 1)
                            if k in (kt // 2 - 1, kt - 1):
                                mm.then_inc(halves, 1)

            pe.wait_ge(s_("ma_done"), 2 + KD)
            single(FIRST["bo"], RT, lambda v: (s_("yb_evac"), v), VGH, VGL, BO_BANKS, lambda k: (s_("vg_lo"), k + 1))
            plain(FIRST["wo"], 2, lambda v: at("wo", "x", v), MH, ML, lambda k: (s_("ml_done"), k + 1))

            def mlp_pe(n, xh, xl):
                c = FIRST[n]

                def up(q, i, first=False):
                    for j in range(2):
                        chunk_in(8 * q + 2 * i + c + j)
                        pe.wait_ge(*at(n, "dn", 8 * q + 2 * j + 2))
                        pe.wait_ge(*at(n, "t", 8 * q + 4 * i + 2 * j + 2))
                        if first and j == 0:
                            pair(0, 0, xh, xl, lambda k: at("n_" + n, "lo", k + 1))
                            squares_pe(pe, "n_" + n)
                        else:
                            half8(j, 0, 2 * j, xh, xl)
                            half8(j, 1, 2 * j + 1, xh, xl)

                def down(q):
                    with pe.Fori(0, 2) as i:
                        for j in range(2):
                            chunk_in(8 * q + 2 * i + c + 4 + j)
                            if j:
                                pe.wait_ge(*at(n, "t", 8 * q + 12))
                            pe.wait_ge(*at(n, "dn", 8 * q + 4 * i + 2 * j + 2))
                            if j == 0:
                                pe.wait_ge(*at(n, "t", 8 * q + 10))
                                pair(0, 0, FH, FL, lambda k: at(n, "fl", 8 * q + 5 + k))
                            else:
                                half8(1, 0, 2, FH, FL)
                                half8(1, 1, 3, FH, FL)

                up(0, 0, first=True)
                up(0, 1)
                down(0)
                with pe.Fori(1, 4) as q:
                    with pe.Fori(0, 2) as i:
                        up(q, i)
                    down(q)

            mlp_pe("mlp0", XH, XL)
            c = FIRST["hg"]

            def gates_pe(h):
                chunk_in(2 * h + c)
                pair(0, 0, XH, XL, lambda k: at("n_hg", "lo", k + 1))

            def rest_pe(h):
                chunk_in(2 * h + c + 1)
                pair(1, 2, XH, XL)

            def turn_values(h):
                pe.wait_ge(s_("h_vf"), h + 1)
                for b in range(TB):
                    mm = pe.transpose(ps[:, 3, b * P:(b + 1) * P], HVF[:, b * P:(b + 1) * P], ident[:])
                mm.then_inc(s_("h_vt"), 1)

            def head_pe(h, n, more=True):
                if more:
                    pe.wait_ge(s_("h_q0"), h + 1)
                    pe.wait_ge(s_("h_f0"), h + 1)
                    gates_pe(h + 1)
                pe.wait_ge(s_("h_t1"), h + 1)
                pe.wait_ge(s_("h_qk"), 14 * h + 14)
                for b in range(TB):
                    t = slice(b * P, (b + 1) * P)
                    mm = pe.matmul(ps[:, 6, t], HK[:, t], HQ[:, t], start=True, stop=True)
                mm.then_inc(s_("h_g"), 1)
                for l, m in enumerate(LEVELS):
                    if l >= 2:
                        pe.wait_ge(s_("h_g_free"), 8 * h + l)
                    for b in range(TB):
                        e = HE[:, l, b * P:(b + 1) * P]
                        mm = pe.matmul(ps[:, 4 + l % 2, b * 64:b * 64 + 64].rearrange("p (g t) -> p g t", t=m), e,
                                       e.rearrange("p (g u t) -> p g u t", u=2, t=m)[:, :, 1], start=True, stop=True)
                    mm.then_inc(s_("h_g"), 1)
                pe.wait_ge(s_("h_kd"), h + 1)
                pe.wait_ge(s_("h_ms"), h + 1)
                for b in range(3):
                    mm = pe.transpose(ps[:, 7, b * P:(b + 1) * P], HKD[:, n, b * P:(b + 1) * P], ident[:])
                mm.then_inc(s_("h_kt"), 1)
                if more:
                    pe.wait_ge(s_("h_g0"), h + 1)
                    pe.wait_ge(s_("h_v"), h + 1)
                    rest_pe(h + 1)
                pe.wait_ge(s_("h_kt_c"), h + 1)
                pe.wait_ge(s_("h_v"), h + 1)
                for b in range(3):
                    mm = pe.matmul(ps[:, 7, b * P:(b + 1) * P], HKT[:, b], HV[:, n, b], start=True, stop=True)
                mm.then_inc(s_("h_st"), 1)
                pe.wait_ge(s_("h_g_free"), 8 * h + 8)
                pe.wait_ge(s_("h_s"), 3 * h + 3)
                pe.wait_ge(s_("h_qd"), h + 1)
                for b in range(TB):
                    t = slice(b * P, (b + 1) * P)
                    mm = pe.matmul(ps[:, 6, t], HV[:, n, b], HP[:, t], start=True, stop=b == 0)
                    if b:
                        mm = pe.matmul(ps[:, 6, t], HS[:, b - 1], HQD[:, n, t], start=False, stop=True)
                mm.then_inc(s_("h_o"), 1)
                if more:
                    turn_values(h + 1)
                pe.wait_ge(s_("h_sq"), h + 1)
                pe.matmul(ps[:, 7], ones[:], tmp[:, 0], start=True, stop=True).then_inc(s_("h_mean"), 1)

            pe.wait_ge(*at("mlp0", "dn", 34))
            gates_pe(0)
            pe.wait_ge(s_("f_add"), 2 * (KD - 1))
            pe.matmul(ps[:, 7], ones[:], HZ[:], start=True, stop=True).then_inc(s_("f_sums"), 1)
            pe.matmul(ps[:, 6], ones[:], HF[:], start=True, stop=True).then_inc(s_("f_mm"), 2)
            pe.wait_ge(*at("mlp0", "dn", 36))
            rest_pe(0)
            turn_values(0)
            with pe.Fori(0, HEADS_H // 2 - 1) as i:
                for n in range(2):
                    head_pe(2 * i + n, n)
            head_pe(6, 0)
            head_pe(7, 1, more=False)

            plain(FIRST["hwo"], 2, lambda v: at("hwo", "x", v), OH, OL, lambda k: (s_("ho_done"), k + 1))
            mlp_pe("mlp1", XH, XL)

            c = FIRST["kvq"]

            def one_tile(c, s, bank, xh, xl, ready=None):
                chunk_in(c)
                h, l = w1(w_hi, s, 8), w1(w_lo, s, 8)
                for k in range(KD):
                    if ready is not None:
                        pe.wait_ge(*ready(k))
                    mm = product(ps[:, bank], [h[k]], [l[k]], [xh[:, k]], [xl[:, k]], start=k == 0, stop=k == KD - 1)
                    if k in (KD // 2 - 1, KD - 1):
                        mm.then_inc(halves, 1)

            def small_norm_pe(n, W):
                for k in range(2):
                    pe.wait_ge(*at(n, "sq", k + 1))
                    mm = pe.matmul(ps[:, 7], ones[:], W[:, 4 + k], start=k == 0, stop=k == 1)
                mm.then_inc(sig(n, "mean"), 1)

            one_tile(c, 0, 4, XH, XL, lambda k: at("n_mla", "lo", k + 1))
            one_tile(c + 1, 1, 5, XH, XL)
            squares_pe(pe, "n_kv")
            chunk_in(c + 2)
            pe.wait_ge(*at("mlp1", "dn", 36))
            pair(0, 0, XH2, XL2, lambda k: at("n_kv", "lo", k + 1))
            small_norm_pe("cq", CQ)
            one_tile(c + 3, 1, 2, XH2, XL2)
            pe.wait_ge(*at("cq", "ln", 1))
            small_norm_pe("ckv", CK)
            pe.wait_ge(consts_in, 32 + 32 + 64)
            pe.wait_ge(s_("kr_raw"), 1)
            pe.matmul(ps[:, 3], swap_t[:], QR[:, 2], start=True, stop=True).then_inc(s_("kr_swap"), 1)

            c = FIRST["att"]
            pe.wait_ge(*at("cq", "lo", 2))
            pe.sem_inc(att("a_pt", 0)[0], 8)
            pe.sem_inc(att("a_pv", 0)[0], 1)
            with pe.Fori(0, 4) as i:
                def part(t, s, at, k, step, n):
                    return [t[:, s, at + q * step:at + q * step + n] for q in range(k)]

                chunk_in(2 * i + c)
                pe.wait_ge(*att("a_exp", 16 * i + 4))
                for h in range(4):
                    mm = product(ps[:, h], part(w_hi, 0, h * P, 2, 512, P), part(w_lo, 0, h * P, 2, 512, P),
                                 tiles(CQH, 2), tiles(CQL, 2))
                mm.then_inc(halves, 1)
                for h in range(2):
                    mm = product(ps[:, 4 + h], part(w_hi, 0, 1024 + h * P, 2, 256, P),
                                 part(w_lo, 0, 1024 + h * P, 2, 256, P), tiles(CQH, 2), tiles(CQL, 2))
                mm.then_inc(halves, 1)
                chunk_in(2 * i + c + 1)
                for h in range(4):
                    if h == 0:
                        pe.wait_ge(*at("ckv", "lo", 2))
                    pe.wait_ge(*att("qn_done", 4 * i + h + 1))
                    mm = product(ps[:, h], part(w_hi, 1, h * P, 2, 512, P), part(w_lo, 1, h * P, 2, 512, P),
                                 tiles(CKH, 2), tiles(CKL, 2))
                    if h == 0:
                        pe.wait_ge(*att("al_done", 4 * i + 1))
                        for pair_ in range(2):
                            pe.wait_ge(*att("qr_raw", 2 * i + pair_ + 1))
                            pe.matmul(ps[:, 6 + pair_], swap_t[:], QR[:, 2 + pair_], start=True, stop=True)\
                                .then_inc(att("qr_swap", 0)[0], 1)
                mm.then_inc(halves, 1)
                for b in range(TB):
                    if b == 2:
                        pe.wait_ge(*att("qr_done", 2 * i + 2))
                    mm = product_x(ps[:, 4 + b], part(w_hi, 1, 1024, 2, 512, 512), part(w_lo, 1, 1024, 2, 512, 512),
                                   [CKH[:, k, b * P:(b + 1) * P] for k in range(2)],
                                   [CKL[:, k, b * P:(b + 1) * P] for k in range(2)])
                mm.then_inc(halves, 1)

                def scores(h):
                    r = slice(ROPE * (h % 2), ROPE * (h % 2) + ROPE)
                    for b in range(TB):
                        n = (b + 1) * P
                        pe.wait_ge(*att("a_exp", 16 * i + 4 * h + b + 1))
                        pe.matmul(ps[:, b, 0:n], QN[:, h, b * P:n], KN[:, h, 0:n], start=True, stop=False)
                        pe.matmul(ps[:, b, 0:n], QR[r, h // 2, b * P:n], KR[r, 0:n], start=False, stop=True)\
                            .then_inc(att("a_qk", 0)[0], 1)

                def turn(h):
                    for b in range(TB):
                        t = 16 * i + 4 * h + b
                        pe.wait_ge(*att("a_pm", t + 1))
                        pe.wait_ge(*att("a_ptc", t + 1))
                        for j in range(b + 1):
                            mm = pe.transpose(ps[:, 4 + b % 2, j * P:(j + 1) * P],
                                              PM[:, h % 2, rows(b)][:, j * P:(j + 1) * P], ident[:])
                        mm.then_inc(att("a_pt", 0)[0], 1)

                def weigh(h):
                    pe.wait_ge(*att("al_done", 4 * i + h + 1))
                    for b in range(TB):
                        pe.wait_ge(*att("a_ptc", 16 * i + 4 * h + b + 3))
                        for j in range(b + 1):
                            mm = pe.matmul(ps[:, 6, b * P:(b + 1) * P], VT[:, j, h * P:(h + 1) * P],
                                           PT[:, rows(b)][:, j * P:(j + 1) * P], start=j == 0, stop=j == b)
                    mm.then_inc(att("a_pv", 0)[0], 1)

                pe.wait_ge(*att("kn_done", 4 * i + 4))
                scores(0)
                pe.wait_ge(*att("vt_done", 4 * i + 4))
                for h in range(4):
                    if h < 3:
                        scores(h + 1)
                    turn(h)
                    weigh(h)

            pe.wait_ge(*att("al_done", 1 + HEADS_M))
            single(FIRST["mwo"], 16, lambda v: at("mwo", "x", v), AH, AL)
            mlp_pe("mlp2", XH2, XL2)
            def turn_back(n):
                if Y_BANKS[n] < 4:
                    pe.wait_ge(*at("mlp2", "dn", 33 + Y_BANKS[n]))
                for j in range(4):
                    k = 4 * (n // TB) + j
                    pe.wait_ge(s_("y_gain"), k + 1)
                    mm = pe.transpose(ps[:, Y_BANKS[n], j * P:(j + 1) * P], X[:, k, n % TB * P:(n % TB + 1) * P], ident[:])
                mm.then_inc(s_("y_turned"), 1)

            for n in range(TB):
                turn_back(n)
            pe.wait_ge(s_("y_add"), KD - 1)
            for b in range(TB):
                mm = pe.matmul(ps[:, 7, b:b + 1], rst[:, 0, b * P:(b + 1) * P], ones[:, 0:1], start=True, stop=True)
            mm.then_inc(s_("y_mean"), 1)
            for n in range(TB, 2 * TB):
                if n == 2 * TB - 1:
                    pe.wait_ge(s_("y_act"), 1)
                turn_back(n)


def level_masks():
    s, t = np.arange(P)[:, None], np.arange(P)[None, :]
    out = [((s // (2 * m) == t // (2 * m)) & (s % (2 * m) < m))[:, np.arange(P) % (2 * m) >= m] for m in LEVELS]
    return np.ascontiguousarray(np.concatenate(out + [s == t], axis=1).astype(np.float32))


def rotary():
    half = ROPE // 2
    inv_freq = np.float32(10000.0) ** (-np.arange(half, dtype=np.float32) / np.float32(half))
    ang = (np.arange(T, dtype=np.float32)[:, None] * inv_freq[None, :]).T
    cos, sin = np.cos(ang), np.sin(ang)
    swap = np.zeros((P, P), np.float32)
    swap[np.arange(P), np.arange(P) ^ half] = 1.0
    return np.concatenate([cos] * 4), np.concatenate([-sin, sin] * 2), swap


def constants():
    cos, sin, swap = rotary()
    r = np.ones((P, T), np.float32)
    r[:, ::P] = 0.0
    return {
        "ident": np.eye(P, dtype=np.float32), "ones": np.ones((P, P), np.float32),
        "level_masks": level_masks(), "reset": r, "cos": cos, "sin": sin, "swap": swap,
        "neg": np.triu(np.full((P, P), -1e30, np.float32), 1),
    }


def pack_vectors(inputs):
    cols = []
    for name, n in VECTOR_WIDTHS:
        if name == "eps":
            v = np.full((P, 1), EPS, np.float32)
        elif name in ("conv_a_w", "conv_b_w"):
            w = np.asarray(inputs[name])[0]
            v = w.reshape(w.shape[0], -1, P).transpose(2, 1, 0).reshape(P, n)
        else:
            v = np.asarray(inputs[name]).reshape(n, P).T
        cols.append(v)
    return np.ascontiguousarray(np.concatenate(cols, axis=1))


WEIGHTS = ["w_in", "w_a_out", "w_rg_a", "w_rg_x", "w_b_out", "w_o", "w_1", "w_2", "hgrn_w_q_2", "hgrn_w_f_2",
           "hgrn_w_i_2", "hgrn_w_g_2", "hgrn_w_o_2", "mla_w_dq_2", "mla_w_uq_2", "mla_w_o_2"]
PLAIN = ["x", "kv_w_dkv_2", "kv_w_uk_2", "kv_w_uv_2", "mlp_w_up_2", "mlp_w_down_2"]


def kernel(**inputs):
    import concourse.bacc as _bacc
    from concourse.bass_utils import run_bass_kernel_spmd as _run

    nc = _bacc.Bacc("TRN2", target_bir_lowering=False, num_devices=1)
    arrays = {n: np.ascontiguousarray(inputs[n]) for n in WEIGHTS + PLAIN}
    arrays["vectors"] = pack_vectors(inputs)
    arrays.update(constants())
    aps, sent = {}, {}
    for name, v in arrays.items():
        sent[f"in_{name}"] = v
        ap = nc.dram_tensor(f"in_{name}", v.shape, mybir.dt.from_np(v.dtype), kind="ExternalInput").ap()
        aps[name] = ap[0] if name in WEIGHTS else ap
    out = nc.dram_tensor("out_0", (1, T, D), F32, kind="ExternalOutput").ap()
    build_program(nc, aps, out)
    r = _run(nc, [sent], core_ids=[0])
    return r.results[0]["out_0"]
```
